# Optimizing a Trainium2 kernel written in Bass

```python
import jax, jax.numpy as jnp
from jax import lax
import numpy as np

D_MODEL = 1024
BATCH = 1
SEQ = 2048
DEPTH = 1

CHUNK = 64
Q_BLOCK = 128
PLE_DIM = 256
GDN_HEADS = 4
GDN_DK = 128
GDN_DV = 128
CONV_WIDTH = 4
MLA_HEADS = 4
MLA_NOPE = 128
MLA_ROPE = 64
MLA_V = 128
Q_LORA = 384
KV_LORA = 256
ROPE_THETA = 10000.0
D_FF = -(-(8 * D_MODEL) // (3 * 256)) * 256

GDN_QK = GDN_HEADS * GDN_DK
GDN_VW = GDN_HEADS * GDN_DV
MIX_WIDTH = GDN_VW + MLA_HEADS * MLA_V
IN_SIZES = (GDN_QK, GDN_QK, GDN_VW, GDN_VW, GDN_HEADS, GDN_HEADS, Q_LORA, KV_LORA, MLA_ROPE)
IN_SPLITS = tuple(int(v) for v in np.cumsum(IN_SIZES)[:-1])
IN_WIDTH = int(sum(IN_SIZES))
ALPHA = (2.0 * DEPTH) ** 0.25
BETA = (8.0 * DEPTH) ** -0.25
LN_EPS = 1e-5
RMS_EPS = 1e-6

kernel_name = 'hymba_gdn_mla_deepnorm_ple_trunk'

def layer_norm(x, g, b):
    xf = x.astype(jnp.float32)
    mu = jnp.mean(xf, -1, keepdims=True)
    var = jnp.mean(jnp.square(xf - mu), -1, keepdims=True)
    return ((xf - mu) * lax.rsqrt(var + LN_EPS) * g + b).astype(x.dtype)

def rms_norm(x, g):
    xf = x.astype(jnp.float32)
    return (xf * lax.rsqrt(jnp.mean(xf * xf, -1, keepdims=True) + RMS_EPS) * g).astype(x.dtype)

def l2_norm(x):
    xf = x.astype(jnp.float32)
    return xf * lax.rsqrt(jnp.sum(xf * xf, -1, keepdims=True) + RMS_EPS)

def rope_tables(positions):
    inv_freq = ROPE_THETA ** (-jnp.arange(0, MLA_ROPE, 2, dtype=jnp.float32) / MLA_ROPE)
    ang = positions.astype(jnp.float32)[..., None] * inv_freq
    return jnp.cos(ang), jnp.sin(ang)

def apply_rope(x, cos, sin):
    x1, x2 = jnp.split(x.astype(jnp.float32), 2, axis=-1)
    return jnp.concatenate([x1 * cos - x2 * sin, x2 * cos + x1 * sin], -1).astype(x.dtype)

def causal_dwconv(x, w):
    return lax.conv_general_dilated(
        x, w[:, None, :].astype(x.dtype), window_strides=(1,),
        padding=[(CONV_WIDTH - 1, 0)], dimension_numbers=('NWC', 'WIO', 'NWC'),
        feature_group_count=x.shape[-1])

def gated_delta_rule(q, k, v, g, beta):
    B, S, H, DK = q.shape
    DV = v.shape[-1]
    N = S // CHUNK
    f32 = jnp.float32

    def chunks(t):
        t = t.astype(f32).reshape((B, N, CHUNK, H) + t.shape[3:])
        return jnp.moveaxis(t, (1, 3), (0, 2))

    q = chunks(q) * DK ** -0.5
    k = chunks(k)
    v = chunks(v)
    beta = chunks(beta)
    g = jnp.cumsum(chunks(g), axis=-1)
    tri_incl = jnp.tril(jnp.ones((CHUNK, CHUNK), bool))
    tri_strict = jnp.tril(jnp.ones((CHUNK, CHUNK), bool), -1)
    decay = jnp.exp(jnp.where(tri_incl, g[..., :, None] - g[..., None, :], -jnp.inf))
    k_beta = k * beta[..., None]
    lower = jnp.where(tri_strict, jnp.einsum('nbhid,nbhjd->nbhij', k_beta, k) * decay, 0.0)
    rhs = jnp.concatenate([v * beta[..., None], k_beta * jnp.exp(g)[..., None]], -1)
    sol = lax.linalg.triangular_solve(lower + jnp.eye(CHUNK, dtype=f32), rhs,
                                      left_side=True, lower=True, unit_diagonal=True)
    u, w = sol[..., :DV], sol[..., DV:]
    attn = jnp.where(tri_incl, jnp.einsum('nbhid,nbhjd->nbhij', q, k) * decay, 0.0)
    g_last = g[..., -1]
    q_dec = q * jnp.exp(g)[..., None]
    k_dec = k * jnp.exp(g_last[..., None] - g)[..., None]

    def step(state, xs):
        q_c, k_c, u_c, w_c, attn_c, gl = xs
        v_new = u_c - jnp.einsum('bhck,bhkv->bhcv', w_c, state)
        o = jnp.einsum('bhck,bhkv->bhcv', q_c, state) + jnp.einsum('bhij,bhjv->bhiv', attn_c, v_new)
        state = state * jnp.exp(gl)[..., None, None] + jnp.einsum('bhck,bhcv->bhkv', k_c, v_new)
        return state, o

    s0 = jnp.zeros((B, H, DK, DV), f32)
    _, o = lax.scan(step, s0, (q_dec, k_dec, u, w, attn, g_last))
    return jnp.moveaxis(o, (0, 2), (1, 3)).reshape(B, S, H, DV)

def mla_attention(q_nope, q_rope, k_nope, k_rope, v):
    S = q_nope.shape[1]
    scale = (MLA_NOPE + MLA_ROPE) ** -0.5
    frame_chunk = jnp.arange(S) // CHUNK
    outs = []
    for blk in range(S // Q_BLOCK):
        q0, q1 = blk * Q_BLOCK, (blk + 1) * Q_BLOCK
        s = (jnp.einsum('bqhd,bkhd->bhqk', q_nope[:, q0:q1], k_nope[:, :q1])
             + jnp.einsum('bqhd,bkd->bhqk', q_rope[:, q0:q1], k_rope[:, :q1])).astype(jnp.float32) * scale
        mask = frame_chunk[None, :q1] <= frame_chunk[q0:q1, None]
        prob = jax.nn.softmax(jnp.where(mask, s, -jnp.inf), axis=-1).astype(v.dtype)
        outs.append(jnp.einsum('bhqk,bkhd->bqhd', prob, v[:, :q1]))
    return jnp.concatenate(outs, axis=1)

def hybrid_layer(x, p_i, cos, sin, w_in, conv_w, a_log, dt_bias, gdn_norm_g, q_norm_g,
                 w_uq, kv_norm_g, w_ukv, w_out, ln1_g, ln1_b, w_gate_up, w_down,
                 ln2_g, ln2_b, w_ple, w_ple_gate):
    B, S, _ = x.shape
    h = x @ w_in
    q, k, v, z, b, a, c_q, c_kv, k_r = jnp.split(h, IN_SPLITS, axis=-1)

    qkv = jax.nn.silu(causal_dwconv(jnp.concatenate([q, k, v], -1), conv_w))
    q, k, v = jnp.split(qkv, [GDN_QK, 2 * GDN_QK], axis=-1)
    q = l2_norm(q.reshape(B, S, GDN_HEADS, GDN_DK))
    k = l2_norm(k.reshape(B, S, GDN_HEADS, GDN_DK))
    v = v.reshape(B, S, GDN_HEADS, GDN_DV)
    beta = jax.nn.sigmoid(b.astype(jnp.float32))
    g = -jnp.exp(a_log.astype(jnp.float32)) * jax.nn.softplus(a.astype(jnp.float32) + dt_bias)
    o_gdn = gated_delta_rule(q, k, v, g, beta)
    o_gdn = rms_norm(o_gdn, gdn_norm_g) * jax.nn.silu(z.reshape(B, S, GDN_HEADS, GDN_DV).astype(jnp.float32))

    qm = (rms_norm(c_q, q_norm_g) @ w_uq).reshape(B, S, MLA_HEADS, MLA_NOPE + MLA_ROPE)
    q_nope, q_rope = jnp.split(qm, [MLA_NOPE], axis=-1)
    q_rope = apply_rope(q_rope, cos[:, :, None, :], sin[:, :, None, :])
    kv = (rms_norm(c_kv, kv_norm_g) @ w_ukv).reshape(B, S, MLA_HEADS, MLA_NOPE + MLA_V)
    k_nope, v_m = jnp.split(kv, [MLA_NOPE], axis=-1)
    k_rope = apply_rope(k_r, cos, sin)
    o_mla = mla_attention(q_nope, q_rope, k_nope, k_rope, v_m)

    mix = jnp.concatenate([o_gdn.reshape(B, S, GDN_VW).astype(x.dtype),
                           o_mla.reshape(B, S, MLA_HEADS * MLA_V)], axis=-1) @ w_out
    x = layer_norm(ALPHA * x + mix, ln1_g, ln1_b)

    gate, up = jnp.split(x @ w_gate_up, 2, axis=-1)
    x = layer_norm(ALPHA * x + (jax.nn.silu(gate) * up) @ w_down, ln2_g, ln2_b)

    return x + jax.nn.sigmoid(x @ w_ple_gate) * (p_i @ w_ple)

def setup_inputs(seed: int = 0) -> dict:
    key = jax.random.key(seed)
    ks = jax.random.split(key, 24)
    f32 = jnp.float32
    nrm = lambda k, shape, scale: jax.random.normal(k, shape, f32) * scale
    x = jax.random.normal(ks[0], (BATCH, SEQ, D_MODEL), f32)
    p = jax.random.normal(ks[1], (DEPTH, BATCH, SEQ, PLE_DIM), f32)
    offset = jax.random.randint(ks[2], (BATCH, 1), 0, 64) * CHUNK
    positions = (offset + jnp.arange(SEQ, dtype=jnp.int32)[None, :]).astype(jnp.int32)
    dt = jnp.exp(jax.random.uniform(ks[3], (DEPTH, GDN_HEADS), f32) * (np.log(0.1) - np.log(1e-3)) + np.log(1e-3))
    return {
        'x': x,
        'p': p,
        'positions': positions,
        'w_in': nrm(ks[4], (DEPTH, D_MODEL, IN_WIDTH), D_MODEL ** -0.5),
        'conv_w': nrm(ks[5], (DEPTH, CONV_WIDTH, 2 * GDN_QK + GDN_VW), CONV_WIDTH ** -0.5),
        'a_log': jnp.log(jax.random.uniform(ks[6], (DEPTH, GDN_HEADS), f32, 1.0, 16.0)),
        'dt_bias': dt + jnp.log(-jnp.expm1(-dt)),
        'gdn_norm_g': 1.0 + nrm(ks[7], (DEPTH, GDN_DV), 0.1),
        'q_norm_g': 1.0 + nrm(ks[8], (DEPTH, Q_LORA), 0.1),
        'w_uq': nrm(ks[9], (DEPTH, Q_LORA, MLA_HEADS * (MLA_NOPE + MLA_ROPE)), Q_LORA ** -0.5),
        'kv_norm_g': 1.0 + nrm(ks[10], (DEPTH, KV_LORA), 0.1),
        'w_ukv': nrm(ks[11], (DEPTH, KV_LORA, MLA_HEADS * (MLA_NOPE + MLA_V)), KV_LORA ** -0.5),
        'w_out': nrm(ks[12], (DEPTH, MIX_WIDTH, D_MODEL), MIX_WIDTH ** -0.5 * BETA),
        'ln1_g': 1.0 + nrm(ks[13], (DEPTH, D_MODEL), 0.1),
        'ln1_b': nrm(ks[14], (DEPTH, D_MODEL), 0.02),
        'w_gate_up': nrm(ks[15], (DEPTH, D_MODEL, 2 * D_FF), D_MODEL ** -0.5),
        'w_down': nrm(ks[16], (DEPTH, D_FF, D_MODEL), D_FF ** -0.5 * BETA),
        'ln2_g': 1.0 + nrm(ks[17], (DEPTH, D_MODEL), 0.1),
        'ln2_b': nrm(ks[18], (DEPTH, D_MODEL), 0.02),
        'w_ple': nrm(ks[19], (DEPTH, PLE_DIM, D_MODEL), PLE_DIM ** -0.5),
        'w_ple_gate': nrm(ks[20], (DEPTH, D_MODEL, D_MODEL), D_MODEL ** -0.5),
    }

def reference(x, p, positions, w_in, conv_w, a_log, dt_bias, gdn_norm_g, q_norm_g, w_uq,
              kv_norm_g, w_ukv, w_out, ln1_g, ln1_b, w_gate_up, w_down, ln2_g, ln2_b,
              w_ple, w_ple_gate):
    cos, sin = rope_tables(positions)
    for i in range(DEPTH):
        x = hybrid_layer(x, p[i], cos, sin, w_in[i], conv_w[i], a_log[i], dt_bias[i],
                         gdn_norm_g[i], q_norm_g[i], w_uq[i], kv_norm_g[i], w_ukv[i],
                         w_out[i], ln1_g[i], ln1_b[i], w_gate_up[i], w_down[i],
                         ln2_g[i], ln2_b[i], w_ple[i], w_ple_gate[i])
    return x


_drawn_inputs = setup_inputs


def setup_inputs(seed=0):
    import zlib

    import numpy as np

    out = dict(_drawn_inputs(seed))
    spreads = {}
    factors = {'gdn_norm_g': 8.158, 'q_norm_g': 8.0, 'kv_norm_g': 8.0, 'ln1_b': 3.067, 'ln2_b': 3.242}
    for name, (base, spread) in spreads.items():
        noise = np.random.default_rng([zlib.crc32(name.encode()), seed]).standard_normal(out[name].shape)
        drawn = base * np.exp(spread * noise) if base else spread * noise
        out[name] = __import__('jax').numpy.asarray(drawn.astype(out[name].dtype))
    for name, factor in factors.items():
        out[name] = (out[name] * factor).astype(out[name].dtype)
    return out
```

```python
from contextlib import ExitStack

import numpy as np

import concourse.bass as bass
from concourse import mybir

F32 = mybir.dt.float32
F32R = mybir.dt.float32r
I32 = mybir.dt.int32
ACT = mybir.ActivationFunctionType
ALU = mybir.AluOpType
AX = mybir.AxisListType

P = 128
D_MODEL = 1024
SEQ = 2048
CHUNK = 64
PLE_DIM = 256
HEADS = 4
ROPE = 64
Q_LORA = 384
KV_LORA = 256
D_FF = 2816
CONV_WIDTH = 4
ROPE_THETA = 10000.0
ALPHA = 2.0 ** 0.25
LN_EPS = 1e-5
RMS_EPS = 1e-6
NTOK = 512
BLOCKS = SEQ // NTOK
TILES = SEQ // P
KD = D_MODEL // P
KQ = Q_LORA // P
KC = KV_LORA // P
FT = D_FF // P
T_Q, T_K, T_V, T_Z = 0, HEADS, 2 * HEADS, 3 * HEADS
T_CQ = 4 * HEADS
T_CKV = T_CQ + KQ
T_KR = T_CKV + KC
N_IN = T_KR + 1


class Scope:

    def __init__(self, nc, ctx, stage):
        self.nc, self.ctx, self.stage, self.sems = nc, ctx, stage, []
        ctx.callback(self.clear)

    def sb(self, name, shape, dt=F32):
        return self.ctx.enter_context(self.nc.sbuf_tensor(f"{self.stage}_{name}", shape, dt))

    def ps(self, name, shape):
        return self.ctx.enter_context(self.nc.psum_tensor(f"{self.stage}_{name}", shape, F32))

    def sem(self, name):
        self.sems.append(self.nc.alloc_semaphore(f"{self.stage}_{name}"))
        return self.sems[-1]

    def clear(self):
        self.nc.clear_and_free_semaphores(self.sems)
        self.nc.all_engine_barrier()


def project_in(nc, xT, w_in, conv_w, hT):
    with ExitStack() as ctx:
        s = Scope(nc, ctx, "in")
        x_raw = s.sb("x_raw", [P, 2, SEQ])
        x_hi = s.sb("x_hi", [P, KD, SEQ], F32R)
        x_lo = s.sb("x_lo", [P, KD, SEQ], F32R)
        w_raw = s.sb("w_raw", [P, 2, KD * P])
        w_hi = s.sb("w_hi", [P, 2, KD * P], F32R)
        w_lo = s.sb("w_lo", [P, 2, KD * P], F32R)
        taps = s.sb("taps", [P, T_Z * CONV_WIDTH])
        h_pad = s.sb("h_pad", [P, SEQ + CONV_WIDTH - 1])
        zero = s.sb("zero", [P, 1])
        conv = s.sb("conv", [P, SEQ])
        out = s.sb("out", [P, SEQ])
        h_ps = s.ps("h_ps", [P, 2, BLOCKS, NTOK])

        x_loaded = [s.sem(f"x_loaded{b}") for b in range(2)]
        x_hi_done = s.sem("x_hi_done")
        x_lo_done = s.sem("x_lo_done")
        w_loaded = [s.sem(f"w_loaded{b}") for b in range(2)]
        w_hi_done = s.sem("w_hi_done")
        w_lo_done = s.sem("w_lo_done")
        taps_loaded = s.sem("taps_loaded")
        h_made = s.sem("h_made")
        h_ps_free = s.sem("h_ps_free")
        zeroed = s.sem("zeroed")
        h_copied = s.sem("h_copied")
        conv_step = s.sem("conv_step")
        conv_free = s.sem("conv_free")
        out_made = s.sem("out_made")
        out_free = s.sem("out_free")
        stored = s.sem("stored")
        block = ctx.enter_context(nc.Block())

        @block.sync
        def _(sp):
            sp.dma_start(taps[:, :], conv_w).then_inc(taps_loaded, 16)
            for k in range(KD):
                if k >= 2:
                    sp.wait_ge(x_lo_done, k - 1)
                sp.dma_start(x_raw[:, k % 2, :], xT[:, k, :]).then_inc(x_loaded[k % 2], 16)
            sp.sem_inc(out_free, 1)
            with sp.Fori(0, N_IN) as m:
                sp.wait_ge(out_made, m + 1)
                sp.dma_start(hT[bass.ds(m, 1)].rearrange("a p t -> p (a t)"), out[:, :]).then_inc(stored, 16)
                sp.wait_ge(stored, 16 * m + 16)
                sp.sem_inc(out_free, 1)

        @block.gpsimd
        def _(pool):
            def load(m, b):
                pool.dma_start(w_raw[:, b, :], w_in[bass.ds(m, 1)].rearrange("a p f -> p (a f)")).then_inc(w_loaded[b], 16)

            def split(i, b):
                m = 2 * i + b
                pool.wait_ge(w_loaded[b], 16 * i + 16)
                pool.wait_ge(h_ps_free, m + 1)
                pool.tensor_tensor(w_hi[:, b, :], w_raw[:, b, :], zero[:, 0:1].broadcast_to([P, KD * P]),
                                   ALU.add).then_inc(w_hi_done, 1)
                pool.wait_ge(w_hi_done, m + 1)
                pool.tensor_tensor(w_lo[:, b, :], w_raw[:, b, :], w_hi[:, b, :].bitcast(F32),
                                   ALU.subtract).then_inc(w_lo_done, 1)

            pool.memset(zero[:, :], 0.0).then_inc(zeroed, 1)
            pool.wait_ge(zeroed, 1)
            load(0, 0)
            load(1, 1)
            with pool.Fori(0, N_IN // 2 - 1) as i:
                for b in range(2):
                    split(i, b)
                    pool.wait_ge(w_lo_done, 2 * i + b + 1)
                    load(2 * i + b + 2, b)
            for b in range(2):
                split(N_IN // 2 - 1, b)

        @block.tensor
        def _(pe):
            with pe.Fori(0, N_IN // 2) as i:
                for b in range(2):
                    m = 2 * i + b
                    pe.wait_ge(w_lo_done, m + 1)
                    pe.wait_ge(h_ps_free, m + 1)
                    for k in range(KD):
                        pe.wait_ge(x_lo_done, k + 1)
                        ws = slice(k * P, (k + 1) * P)
                        for t in range(BLOCKS):
                            ts = slice(t * NTOK, (t + 1) * NTOK)
                            acc = h_ps[:, b, t, :]
                            pe.matmul(acc, w_lo[:, b, ws], x_hi[:, k, ts], start=(k == 0), stop=False)
                            pe.matmul(acc, w_hi[:, b, ws], x_lo[:, k, ts], start=False, stop=False)
                            last = pe.matmul(acc, w_hi[:, b, ws], x_hi[:, k, ts], start=False, stop=(k == KD - 1))
                    last.then_inc(h_made, 1)

        @block.scalar
        def _(act):
            act.sem_inc(h_ps_free, 2)
            act.sem_inc(conv_free, 1)
            for k in range(KD):
                act.wait_ge(x_loaded[k % 2], 16 * (k // 2 + 1))
                act.activation(x_hi[:, k, :], x_raw[:, k % 2, :], ACT.Copy).then_inc(x_hi_done, 1)

            def conv_tile(i, b):
                m = 2 * i + b
                act.wait_ge(h_made, m + 1)
                act.wait_ge(conv_step, CONV_WIDTH * m + 1)
                act.activation(h_pad[:, CONV_WIDTH - 1:], h_ps[:, b].rearrange("p a t -> p (a t)"),
                               ACT.Copy).then_inc(h_copied, 1)
                act.wait_ge(h_copied, m + 1)
                act.sem_inc(h_ps_free, 1)
                act.wait_ge(conv_step, CONV_WIDTH * (m + 1) + 1)
                act.wait_ge(out_free, m + 1)
                act.activation(out[:, :], conv[:, :], ACT.Silu).then_inc(out_made, 1)
                act.wait_ge(out_made, m + 1)
                act.sem_inc(conv_free, 1)

            def plain_tile(i, b, func):
                m = 2 * i + b
                act.wait_ge(h_made, m + 1)
                act.wait_ge(out_free, m + 1)
                act.activation(out[:, :], h_ps[:, b].rearrange("p a t -> p (a t)"), func).then_inc(out_made, 1)
                act.wait_ge(out_made, m + 1)
                act.sem_inc(h_ps_free, 1)

            act.preload_act_table(ACT.Silu)
            for first, last, tile in ((0, T_Z, conv_tile),
                                      (T_Z, T_CQ, lambda i, b: plain_tile(i, b, ACT.Silu)),
                                      (T_CQ, N_IN, lambda i, b: plain_tile(i, b, ACT.Copy))):
                with act.Fori(first // 2, last // 2) as i:
                    for b in range(2):
                        tile(i, b)

        @block.vector
        def _(dve):
            for k in range(KD):
                dve.wait_ge(x_hi_done, k + 1)
                dve.tensor_tensor(x_lo[:, k, :], x_raw[:, k % 2, :], x_hi[:, k, :].bitcast(F32),
                                  ALU.subtract).then_inc(x_lo_done, 1)
            dve.wait_ge(taps_loaded, 16)
            dve.memset(h_pad[:, 0:CONV_WIDTH - 1], 0.0).then_inc(conv_step, 1)
            with dve.Fori(0, T_Z // 2) as i:
                for b in range(2):
                    m = 2 * i + b
                    dve.wait_ge(h_copied, m + 1)
                    for j in range(CONV_WIDTH):
                        if j == 0:
                            dve.wait_ge(conv_free, m + 1)
                            op = dve.tensor_scalar(conv[:, :], h_pad[:, 0:SEQ], taps[:, bass.ds(CONV_WIDTH * m, 1)], None, ALU.mult)
                        else:
                            dve.wait_ge(conv_step, CONV_WIDTH * m + j + 1)
                            op = dve.scalar_tensor_tensor(conv[:, :], h_pad[:, j:j + SEQ], taps[:, bass.ds(CONV_WIDTH * m + j, 1)],
                                                          conv[:, :], ALU.mult, ALU.add)
                        op.then_inc(conv_step, 1)


def split_resident(s, act, dve, name, raw, hi, lo, loaded):
    hi_done, lo_done = s.sem(f"{name}_hi_done"), s.sem(f"{name}_lo_done")

    def on_scalar():
        act.wait_ge(loaded, 16)
        act.activation(hi, raw, ACT.Copy).then_inc(hi_done, 1)

    def on_vector():
        dve.wait_ge(hi_done, 1)
        dve.tensor_tensor(lo, raw, hi.bitcast(F32), ALU.subtract).then_inc(lo_done, 1)

    return on_scalar, on_vector, lo_done


def latents(nc, hT, positions, inv_freq, w_uq, w_ukv, gains, made):
    NG = 14
    SCALE = float(P + ROPE) ** -0.5
    parts = [{n: made[n + half].bitcast(F32) for n in ("qnT", "qrT", "knT", "krT", "v")} for half in ("_hi", "_lo")]
    G_QN, G_KN, G_V = 2, 6, 10
    RING = 5
    MAGIC = 1.5 * 2.0 ** 23
    TWO_PI_1 = 6.28125
    TWO_PI_2 = float(np.float32(0.00193500518798828125))
    TWO_PI_3 = float(np.float32(2 * np.pi - TWO_PI_1 - TWO_PI_2))
    PI_IN = 3.1415925
    with ExitStack() as ctx:
        s = Scope(nc, ctx, "lat")
        NQ = 2 * P + HEADS * P
        NKV = 2 * HEADS * P
        uq_hi = s.sb("uq_hi", [P, KQ, NQ], F32R)
        uq_lo = s.sb("uq_lo", [P, KQ, NQ], F32R)
        ukv_hi = s.sb("ukv_hi", [P, KC, NKV], F32R)
        ukv_lo = s.sb("ukv_lo", [P, KC, NKV], F32R)
        gain = s.sb("gain", [P, KQ + KC])
        freq = s.sb("freq", [P, 1])
        ones = s.sb("ones", [P, P])
        half_pi = s.sb("half_pi", [P, 1])
        eps = s.sb("eps", [P, 1])
        turn = s.sb("turn", [P, P])
        turns_hi = s.sb("turns_hi", [P, SEQ])
        pos, cos = turns_hi[:, :].bitcast(I32), turns_hi
        sin = s.sb("sin", [P, SEQ])
        lat = s.sb("lat", [P, 2, KQ + KC, NTOK])
        kr = s.sb("kr", [ROPE, 2, NTOK])
        sq = s.sb("sq", [P, KQ + KC, NTOK])
        rstd = s.sb("rstd", [P, 2, NTOK])
        nrm_hi = s.sb("nrm_hi", [P, 2, KQ + KC, NTOK], F32R)
        nrm_lo = s.sb("nrm_lo", [P, 2, KQ + KC, NTOK], F32R)
        raw_r = s.sb("raw_r", [P, 2, NTOK])
        out_hi = s.sb("out_hi", [P, NG - 2, NTOK], F32R)
        out_lo = s.sb("out_lo", [P, NG - 2, NTOK], F32R)
        flat_hi = out_hi[:].rearrange("p a t -> p (a t)").bitcast(F32)
        flat_lo = out_lo[:].rearrange("p a t -> p (a t)").bitcast(F32)
        ang, turns = flat_hi[:, 0:SEQ], flat_hi[:, SEQ:2 * SEQ]
        uq_raw = flat_lo[:, 0:KQ * NQ].rearrange("p (k n) -> p k n", k=KQ)
        ukv_raw = flat_lo[:, KQ * NQ:KQ * NQ + KC * NKV].rearrange("p (k n) -> p k n", k=KC)
        rot_hi = s.sb("rot_hi", [P, 3, NTOK], F32R)
        rot_lo = s.sb("rot_lo", [P, 3, NTOK], F32R)
        rot = s.sb("rot", [P, NTOK])
        swapped = s.sb("swapped", [P, NTOK])
        ssq_ps = s.ps("ssq_ps", [P, 2, NTOK])
        ring = s.ps("ring", [P, RING, NTOK])
        turn_ps = s.ps("turn_ps", [P, NTOK])

        uq_loaded, ukv_loaded = s.sem("uq_loaded"), s.sem("ukv_loaded")
        small_loaded, pos_loaded = s.sem("small_loaded"), s.sem("pos_loaded")
        consts = s.sem("consts")
        table = s.sem("table")
        reduced = s.sem("reduced")
        table_done = s.sem("table_done")
        lat_loaded = [s.sem(f"lat_loaded{b}") for b in range(2)]
        sq_done = s.sem("sq_done")
        ssq_done = s.sem("ssq_done")
        rms_done = s.sem("rms_done")
        rstd_done = s.sem("rstd_done")
        nrm_done = s.sem("nrm_done")
        nrm_hi_done = s.sem("nrm_hi_done")
        nrm_lo_done = s.sem("nrm_lo_done")
        group_done = s.sem("group_done")
        out_copied = s.sem("out_copied")
        out_lo_done = s.sem("out_lo_done")
        turned = s.sem("turned")
        cos_part = s.sem("cos_part")
        sin_part = s.sem("sin_part")
        rot_done = s.sem("rot_done")
        rot_hi_done, rot_lo_done = s.sem("rot_hi_done"), s.sem("rot_lo_done")
        stored = s.sem("stored")
        block = ctx.enter_context(nc.Block())
        tok = [slice(t * NTOK, (t + 1) * NTOK) for t in range(BLOCKS)]
        STORES = 12
        BANKS = NG - 2

        uq_act, uq_dve, uq_ready = split_resident(s, nc.scalar, nc.vector, "uq", uq_raw, uq_hi[:], uq_lo[:], uq_loaded)
        ukv_act, ukv_dve, ukv_ready = split_resident(s, nc.scalar, nc.vector, "ukv", ukv_raw, ukv_hi[:], ukv_lo[:], ukv_loaded)

        @block.sync
        def _(sp):
            def load(t):
                b = t % 2
                if t >= 2:
                    sp.wait_ge(nrm_lo_done, t - 1)
                    sp.wait_ge(rot_done, 3 * (t - 1))
                sp.dma_start(lat[:, b], hT[T_CQ:T_KR, :, tok[t]].rearrange("a p t -> p a t")).then_inc(lat_loaded[b], 16)
                sp.dma_start(kr[:, b], hT[T_KR, 0:ROPE, tok[t]]).then_inc(lat_loaded[b], 16)

            sp.dma_start(gain[:], gains).then_inc(small_loaded, 16)
            sp.dma_start(freq[:], inv_freq).then_inc(small_loaded, 16)
            sp.dma_start(pos, positions.partition_broadcast(P)).then_inc(pos_loaded, 16)
            load(0)
            sp.dma_start(uq_raw, w_uq).then_inc(uq_loaded, 16)
            sp.dma_start(ukv_raw, w_ukv).then_inc(ukv_loaded, 16)
            load(1)
            for t in range(BLOCKS):
                sp.wait_ge(out_copied, NG * (t + 1))
                sp.wait_ge(out_lo_done, BANKS * (t + 1))
                for part, src in zip(parts, (out_hi[:].bitcast(F32), out_lo[:].bitcast(F32))):
                    sp.dma_start(part["qnT"][:, :, tok[t]].rearrange("h p t -> p h t"), src[:, 0:4]).then_inc(stored, 16)
                    sp.dma_start(part["knT"][:, :, tok[t]].rearrange("h p t -> p h t"), src[:, 4:8]).then_inc(stored, 16)
                    sp.dma_start(part["v"][4 * t:4 * t + 4].rearrange("a p n -> p a n"), src[:, 8:12]).then_inc(stored, 16)
                sp.wait_ge(rot_lo_done, 3 * (t + 1))
                for part, src in zip(parts, (rot_hi[:].bitcast(F32), rot_lo[:].bitcast(F32))):
                    for g in range(2):
                        sp.dma_start(part["qrT"][2 * g:2 * g + 2, :, tok[t]].rearrange("h p t -> (h p) t"), src[:, g]).then_inc(stored, 16)
                    sp.dma_start(part["krT"][:, tok[t]], src[0:ROPE, 2]).then_inc(stored, 16)
                if t + 2 < BLOCKS:
                    load(t + 2)
            sp.wait_ge(stored, 16 * STORES * BLOCKS)

        @block.gpsimd
        def _(pool):
            pool.memset(ones[:], 1.0).then_inc(consts, 1)
            pool.memset(half_pi[:], float(np.pi / 2)).then_inc(consts, 1)
            pool.memset(eps[:], RMS_EPS).then_inc(consts, 1)
            pool.memset(turn[:], 0.0).then_inc(consts, 1)
            pool.wait_ge(consts, 4)
            for n, half in enumerate(range(0, P, ROPE)):
                view = turn[:, half:half + ROPE // 2]
                pool.affine_select(out=view, in_=view, compare_op=ALU.not_equal, fill=-1.0, base=-half - ROPE // 2,
                                   pattern=[[-1, ROPE // 2]], channel_multiplier=1).then_inc(consts, 1)
                view = turn[:, half + ROPE // 2:half + ROPE]
                pool.affine_select(out=view, in_=view, compare_op=ALU.not_equal, fill=1.0, base=-half,
                                   pattern=[[-1, ROPE // 2]], channel_multiplier=1).then_inc(consts, 1)

        @block.tensor
        def _(pe):
            def sums(t):
                pe.wait_ge(sq_done, t + 1)
                pe.wait_ge(consts, 8)
                if t:
                    pe.wait_ge(rms_done, 2 * t)
                for c, (k0, k1) in enumerate(((0, KQ), (KQ, KQ + KC))):
                    for k in range(k0, k1):
                        last = pe.matmul(ssq_ps[:, c], ones[:], sq[:, k], start=(k == k0), stop=(k == k1 - 1))
                last.then_inc(ssq_done, 1)

            def group(t, g):
                b, n = t % 2, NG * t + g
                if n >= RING:
                    pe.wait_ge(out_copied, n - RING + 1)
                    lows = BANKS * ((n - RING) // NG) + max((n - RING) % NG - 1, 0)
                    if lows:
                        pe.wait_ge(out_lo_done, lows)
                acc = ring[:, n % RING]
                if g < G_KN:
                    cols, ks, k0 = slice(g * P, (g + 1) * P), range(KQ), 0
                    whi, wlo = uq_hi, uq_lo
                else:
                    cols, ks, k0 = slice((g - G_KN) * P, (g - G_KN + 1) * P), range(KC), KQ
                    whi, wlo = ukv_hi, ukv_lo
                for k in ks:
                    if g < G_V:
                        ops = [(wlo[:, k, cols], nrm_hi[:, b, k0 + k]), (whi[:, k, cols], nrm_lo[:, b, k0 + k]),
                               (whi[:, k, cols], nrm_hi[:, b, k0 + k])]
                    else:
                        ts, vs = slice((g - G_V) * P, (g - G_V + 1) * P), slice(HEADS * P, NKV)
                        ops = [(nrm_lo[:, b, k0 + k, ts], whi[:, k, vs]), (nrm_hi[:, b, k0 + k, ts], wlo[:, k, vs]),
                               (nrm_hi[:, b, k0 + k, ts], whi[:, k, vs])]
                    for n, (stay, move) in enumerate(ops):
                        last = pe.matmul(acc, stay, move, start=(k == 0 and n == 0), stop=(k == ks[-1] and n == 2))
                last.then_inc(group_done, 1)

            def swap(t, g):
                if 3 * t + g:
                    pe.wait_ge(sin_part, 3 * t + g)
                rows = P if g < 2 else ROPE
                if g < 2:
                    pe.wait_ge(out_copied, NG * t + g + 1)
                src = raw_r[:, g] if g < 2 else kr[:, t % 2]
                pe.matmul(turn_ps[0:rows], turn[0:rows, 0:rows], src, start=True, stop=True).then_inc(turned, 1)

            sums(0)
            pe.wait_ge(uq_ready, 1)
            pe.wait_ge(ukv_ready, 1)
            for t in range(BLOCKS):
                if t + 1 < BLOCKS:
                    sums(t + 1)
                pe.wait_ge(nrm_lo_done, t + 1)
                for g in range(NG):
                    group(t, g)
                    if g in (4, 7, 10):
                        swap(t, (g - 4) // 3)

        @block.scalar
        def _(act):
            def squares(t):
                act.wait_ge(lat_loaded[t % 2], 32 * (t // 2 + 1))
                if t:
                    act.wait_ge(ssq_done, t)
                act.activation(sq[:], lat[:, t % 2], ACT.Square).then_inc(sq_done, 1)

            def roots(t):
                act.wait_ge(ssq_done, t + 1)
                if t:
                    act.wait_ge(nrm_done, (KQ + KC) * t)
                for c, width in enumerate((Q_LORA, KV_LORA)):
                    act.activation(rstd[:, c], ssq_ps[:, c], ACT.Sqrt, scale=1.0 / width, bias=eps[:, 0:1]).then_inc(rms_done, 1)

            def high(t):
                act.wait_ge(nrm_done, (KQ + KC) * (t + 1))
                if t >= 2:
                    act.wait_ge(group_done, NG * (t - 1))
                act.activation(nrm_hi[:, t % 2], lat[:, t % 2], ACT.Copy).then_inc(nrm_hi_done, 1)

            uq_act()
            ukv_act()
            act.wait_ge(consts, 8)
            squares(0)
            roots(0)
            act.wait_ge(table, 12)
            act.activation(sin[:], ang, ACT.Sin).then_inc(table_done, 1)
            act.activation(turns, ang, ACT.Abs).then_inc(table, 1)
            act.wait_ge(table, 13)
            act.activation(cos[:], turns, ACT.Sin, scale=-1.0, bias=half_pi[:, 0:1]).then_inc(table_done, 1)
            high(0)
            for t in range(BLOCKS):
                if t + 1 < BLOCKS:
                    squares(t + 1)
                    roots(t + 1)
                for g in range(NG):
                    n = NG * t + g
                    act.wait_ge(group_done, n + 1)
                    if t and g == 0:
                        act.wait_ge(stored, 16 * STORES * t)
                        act.wait_ge(rot_done, 3 * t)
                    to = raw_r[:, g] if g < G_QN else out_hi[:, g - G_QN]
                    act.activation(to, ring[:, n % RING], ACT.Copy, scale=SCALE if g < G_KN else 1.0).then_inc(out_copied, 1)
                    if g in (7, 10, 13):
                        r = (g - 7) // 3
                        rows = P if r < 2 else ROPE
                        act.wait_ge(rot_done, 3 * t + r + 1)
                        act.activation(rot_hi[0:rows, r], rot[0:rows], ACT.Copy).then_inc(rot_hi_done, 1)
                if t + 1 < BLOCKS:
                    high(t + 1)

        @block.vector
        def _(dve):
            def norm(t):
                b = t % 2
                dve.wait_ge(rms_done, 2 * (t + 1))
                dve.reciprocal(rstd[:], rstd[:]).then_inc(rstd_done, 1)
                dve.wait_ge(rstd_done, t + 1)
                for k in range(KQ + KC):
                    dve.scalar_tensor_tensor(lat[:, b, k], lat[:, b, k], gain[:, k:k + 1], rstd[:, int(k >= KQ)],
                                             ALU.mult, ALU.mult).then_inc(nrm_done, 1)

            def low(t):
                dve.wait_ge(nrm_hi_done, t + 1)
                dve.tensor_tensor(nrm_lo[:, t % 2], lat[:, t % 2], nrm_hi[:, t % 2].bitcast(F32), ALU.subtract).then_inc(nrm_lo_done, 1)

            def rotate(t, g):
                rows = P if g < 2 else ROPE
                src = raw_r[:, g] if g < 2 else kr[:, t % 2]
                n = 3 * t + g
                if g < 2:
                    dve.wait_ge(out_copied, NG * t + g + 1)
                if n:
                    dve.wait_ge(rot_lo_done, n)
                dve.tensor_tensor(rot[0:rows], src, cos[0:rows, tok[t]], ALU.mult).then_inc(cos_part, 1)
                dve.wait_ge(turned, n + 1)
                dve.tensor_tensor(swapped[0:rows], turn_ps[0:rows], sin[0:rows, tok[t]], ALU.mult).then_inc(sin_part, 1)
                dve.wait_ge(cos_part, n + 1)
                dve.wait_ge(sin_part, n + 1)
                dve.tensor_tensor(rot[0:rows], rot[0:rows], swapped[0:rows], ALU.add).then_inc(rot_done, 1)

            def rotate_low(t, g):
                rows = P if g < 2 else ROPE
                dve.wait_ge(rot_hi_done, 3 * t + g + 1)
                if t:
                    dve.wait_ge(stored, 16 * STORES * t)
                dve.tensor_tensor(rot_lo[0:rows, g], rot[0:rows], rot_hi[0:rows, g].bitcast(F32), ALU.subtract).then_inc(rot_lo_done, 1)

            def low_out(t, g):
                n = NG * t + g
                dve.wait_ge(out_copied, n + 1)
                if t and g == G_QN:
                    dve.wait_ge(stored, 16 * STORES * t)
                dve.scalar_tensor_tensor(out_lo[:, g - G_QN], ring[:, n % RING], SCALE if g < G_KN else 1.0,
                                         out_hi[:, g - G_QN].bitcast(F32), ALU.mult, ALU.subtract).then_inc(out_lo_done, 1)

            uq_dve()
            ukv_dve()
            dve.wait_ge(small_loaded, 32)
            dve.wait_ge(pos_loaded, 16)
            norm(0)
            steps = [
                lambda: dve.tensor_copy(ang, pos),
                lambda: dve.tensor_scalar(ang, ang, freq[:, 0:1], None, ALU.mult),
                lambda: dve.tensor_scalar(turns, ang, float(1 / (2 * np.pi)), MAGIC, ALU.mult, ALU.add),
                lambda: dve.tensor_scalar(turns, turns, -MAGIC, None, ALU.add),
                lambda: dve.tensor_scalar(turns_hi[:], turns, 2048 * MAGIC, -2048 * MAGIC, ALU.add, ALU.add),
                lambda: dve.tensor_tensor(turns, turns, turns_hi[:], ALU.subtract),
            ]
            for part in (TWO_PI_1, TWO_PI_2, TWO_PI_3):
                steps.append(lambda part=part: dve.scalar_tensor_tensor(ang, turns_hi[:], -part, ang, ALU.mult, ALU.add))
                steps.append(lambda part=part: dve.scalar_tensor_tensor(ang, turns, -part, ang, ALU.mult, ALU.add))
            for n, step in enumerate(steps[:-1]):
                if n:
                    dve.wait_ge(table, n)
                step().then_inc(table, 1)
            dve.wait_ge(table, 11)
            steps[-1]().then_inc(reduced, 1)
            dve.wait_ge(reduced, 1)
            dve.tensor_scalar(ang, ang, PI_IN, -PI_IN, ALU.min, ALU.max).then_inc(table, 1)
            low(0)
            dve.wait_ge(table_done, 2)
            for t in range(BLOCKS):
                for g in range(G_QN, NG):
                    low_out(t, g)
                    if g in (5, 8, 11):
                        rotate(t, (g - 5) // 3)
                    if g in (7, 10, 13):
                        rotate_low(t, (g - 7) // 3)
                    if g == 7 and t + 1 < BLOCKS:
                        norm(t + 1)
                if t + 1 < BLOCKS:
                    low(t + 1)


def delta_rule(nc, hT, a_log, dt_bias, norm_g, mixT):
    LEVELS = (2, 4, 8, 16, 32)
    BETA, GCUM, BETA_G, K_DEC, GATE = range(5)
    with ExitStack() as ctx:
        s = Scope(nc, ctx, "dr")
        qkv = s.sb("qkv", [P, 2, 3 * HEADS, P])
        zT = s.sb("zT", [P, 2, HEADS, P])
        ba_raw = s.sb("ba_raw", [2 * HEADS, SEQ])
        ba = s.sb("ba", [P, TILES, 2 * HEADS])
        bias = s.sb("bias", [P, HEADS])
        rate = s.sb("rate", [P, HEADS])
        gnorm = s.sb("gnorm", [P, 1])
        soft = s.sb("soft", [P, 3, TILES, HEADS])
        scal = s.sb("scal", [P, TILES, 5 * HEADS])
        cur = s.sb("cur", [P, 2, 5, HEADS])
        ident = s.sb("ident", [P, P])
        ones = s.sb("ones", [P, P])
        upto = s.sb("upto", [P, P])
        below = s.sb("below", [P, P])
        chunk = s.sb("chunk", [P, P])
        corner = s.sb("corner", [P, 1 + len(LEVELS), P])
        eps_l2 = s.sb("eps_l2", [P, 1])
        cums = s.sb("cums", [P, HEADS, P])
        eg = s.sb("eg", [P, 2, HEADS, P])
        sq = s.sb("sq", [P, 2 * HEADS, P])
        ssq = s.sb("ssq", [P, 2 * HEADS])
        rn = s.sb("rn", [P, 4, 2 * HEADS])
        qk_n = s.sb("qk_n", [P, 2 * HEADS, P])
        vb = s.sb("vb", [P, HEADS, P])
        kbg = s.sb("kbg", [P, HEADS, P])
        kdec = s.sb("kdec", [P, 2, HEADS, P])
        qk_nT = s.sb("qk_nT", [P, 2 * HEADS, P])
        dif = s.sb("dif", [P, HEADS, P])
        dec = s.sb("dec", [P, 2, HEADS, P])
        L = s.sb("L", [P, HEADS, P])
        Z = s.sb("Z", [P, HEADS, P])
        U = s.sb("U", [P, HEADS, P])
        T = s.sb("T", [P, HEADS, P])
        attnT = s.sb("attnT", [P, 2, HEADS, P])
        wT = s.sb("wT", [P, 2, HEADS, P])
        u = s.sb("u", [P, 2, HEADS, P])
        qdT = s.sb("qdT", [P, 2, HEADS, P])
        S = s.sb("S", [P, HEADS, P])
        Sd = s.sb("Sd", [P, HEADS, P])
        vnew = s.sb("vnew", [P, HEADS, P])
        osq = s.sb("osq", [P, HEADS, P])
        ossq = s.sb("ossq", [P, HEADS])
        orn = s.sb("orn", [P, 4, HEADS])
        on = s.sb("on", [P, HEADS, P])
        mix = s.sb("mix", [P, HEADS, P])
        b0, b1, b2, b3, vs_ps, o_ps, kv_ps, oT_ps = [s.ps(f"b{n}", [P, HEADS, P]) for n in range(8)]

        const_sem, mask_sem = s.sem("consts"), s.sem("masks")
        small_loaded, ba_loaded = s.sem("small_loaded"), s.sem("ba_loaded")
        pre = s.sem("pre")
        loaded = [s.sem(f"loaded{b}") for b in range(2)]
        cur_done = s.sem("cur_done")
        banks_free = s.sem("banks_free")
        cums_done = s.sem("cums_done")
        turned_done = s.sem("turned_done")
        sq_done, eg_done = s.sem("sq_done"), s.sem("eg_done")
        ssq_done, log_done, root_done = s.sem("ssq_done"), s.sem("log_done"), s.sem("root_done")
        newton = s.sem("newton")
        scaled = s.sem("scaled")
        dif_done, clamp_done, dec_done = s.sem("dif_done"), s.sem("clamp_done"), s.sem("dec_done")
        kbg_done, kdec_done = s.sem("kbg_done"), s.sem("kdec_done")
        masked = s.sem("masked")
        back_done, back_copied = s.sem("back_done"), s.sem("back_copied")
        gram_done = s.sem("gram_done")
        L_done, attn_done = s.sem("L_done"), s.sem("attn_done")
        LT_done, tt_done, t_copied = s.sem("LT_done"), s.sem("tt_done"), s.sem("t_copied")
        zp_done, z_done, yp_done, u_step = s.sem("zp_done"), s.sem("z_done"), s.sem("yp_done"), s.sem("u_step")
        wu_done, wu_copied = s.sem("wu_done"), s.sem("wu_copied")
        qd_done = s.sem("qd_done")
        s_zero = s.sem("s_zero")
        ws_done, v_done, sd_done, kv_done, s_done = (s.sem(n) for n in ("ws_done", "v_done", "sd_done", "kv_done", "s_done"))
        o_done = s.sem("o_done")
        osq_done, ossq_done, olog_done, oroot_done, onewton = (s.sem(n) for n in ("osq_done", "ossq_done", "olog_done", "oroot_done", "onewton"))
        on_done, oT_done, mix_done, mix_free, stored = (s.sem(n) for n in ("on_done", "oT_done", "mix_done", "mix_free", "stored"))
        rec_done = s.sem("rec_done")
        block = ctx.enter_context(nc.Block())
        NL = len(LEVELS)
        N_MASKS = 5 + 2 * (1 + NL) + 1
        PRE_GATE = 13

        def column(c):
            return scal[:].rearrange("p t (c h) -> p t c h", c=5)[:, :, c, :]

        def heads(ap):
            return ap.unsqueeze(2).broadcast_to([P, ap.shape[1], P])

        def each(ap):
            return ap.unsqueeze(1).broadcast_to([P, HEADS, P])

        def pipeline(prepare, advance, both):
            def run(loop):
                prepare(0, 0)
                with loop(0, TILES // 2 - 1) as i:
                    both(2 * i, 0)
                    both(2 * i + 1, 1)
                both(TILES - 2, 0)
                advance(TILES - 1, 1)
            return run

        @block.sync
        def _(sp):
            def load(t, b):
                tok = bass.ds(P * t, P)
                sp.dma_start(qkv[:, b], hT[T_Q:T_Z, :, tok].rearrange("a p t -> p a t")).then_inc(loaded[b], 16)
                sp.dma_start(zT[:, b], hT[T_Z:T_CQ, :, tok].rearrange("a p t -> p a t")).then_inc(loaded[b], 16)

            def store(t):
                sp.wait_ge(mix_done, t + 1)
                sp.dma_start(mixT[0:HEADS, :, bass.ds(P * t, P)].rearrange("a p t -> p a t"), mix[:]).then_inc(stored, 16)
                sp.wait_ge(stored, 16 * t + 16)
                sp.sem_inc(mix_free, 1)

            sp.dma_start(ba_raw[:], hT[T_KR, ROPE:ROPE + 2 * HEADS, :]).then_inc(ba_loaded, 16)
            sp.dma_start(bias[:], dt_bias.partition_broadcast(P)).then_inc(small_loaded, 16)
            sp.dma_start(rate[:], a_log.partition_broadcast(P)).then_inc(small_loaded, 16)
            sp.dma_start(gnorm[:], norm_g).then_inc(small_loaded, 16)
            sp.sem_inc(mix_free, 1)
            load(0, 0)
            load(1, 1)
            with sp.Fori(0, TILES // 2 - 1) as i:
                for b in range(2):
                    store(2 * i + b)
                    load(2 * i + b + 2, b)
            store(TILES - 2)
            store(TILES - 1)

        @block.gpsimd
        def _(pool):
            n = [0]

            def put(out, in_, op, fill, base, pattern, mult):
                if n[0]:
                    pool.wait_ge(mask_sem, n[0])
                pool.affine_select(out=out, in_=in_, compare_op=op, fill=fill, base=base, pattern=pattern,
                                   channel_multiplier=mult).then_inc(mask_sem, 1)
                n[0] += 1

            pool.memset(ident[:], 0.0).then_inc(const_sem, 1)
            pool.memset(ones[:], 1.0).then_inc(const_sem, 1)
            pool.memset(eps_l2[:], RMS_EPS).then_inc(const_sem, 1)
            pool.memset(corner[:], 0.0).then_inc(const_sem, 1)
            pool.wait_ge(const_sem, 4)
            put(ident[:], ident[:], ALU.not_equal, 1.0, 0, [[-1, P]], 1)
            halves = lambda ap: ap.rearrange("p (c f) -> p c f", c=2)
            put(halves(chunk[:]), halves(ones[:]), ALU.is_ge, 0.0, 0, [[-CHUNK, 2], [0, CHUNK]], 1)
            put(halves(chunk[:]), halves(chunk[:]), ALU.is_ge, 0.0, CHUNK - 1, [[CHUNK, 2], [0, CHUNK]], -1)
            put(upto[:], chunk[:], ALU.is_ge, 0.0, 0, [[1, P]], -1)
            put(below[:], chunk[:], ALU.is_gt, 0.0, 0, [[-1, P]], 1)
            for l, size in enumerate((1,) + LEVELS):
                blocks = P // (2 * size)
                right = lambda ap: ap.rearrange("p (n h r) -> p n h r", h=2, r=size)[:, :, 1, :]
                put(right(corner[:, l]), right(ones[:]), ALU.is_ge, 0.0, 0, [[-2 * size, blocks], [0, size]], 1)
                put(right(corner[:, l]), right(corner[:, l]), ALU.is_ge, 0.0, size - 1, [[2 * size, blocks], [0, size]], -1)
            pool.wait_ge(mask_sem, n[0])
            pool.sem_inc(mask_sem, 1)

            def prepare(t, b):
                pool.wait_ge(cur_done, t + 1)
                pool.wait_ge(turned_done, t + 1)
                pool.tensor_tensor(cums[:], each(upto[:]), heads(cur[:, b, GATE]), ALU.mult).then_inc(cums_done, 1)
                pool.wait_ge(scaled, 3 * t + 1)
                pool.wait_ge(wu_done, t + 1)
                pool.tensor_tensor(kbg[:], qk_n[:, HEADS:], heads(cur[:, b, BETA_G]), ALU.mult).then_inc(kbg_done, 1)
                pool.wait_ge(rec_done, t + 1)
                pool.tensor_tensor(kdec[:, b], qk_n[:, HEADS:], heads(cur[:, b, K_DEC]), ALU.mult).then_inc(kdec_done, 1)
                pool.wait_ge(dec_done, t + 1)
                pool.tensor_tensor(dec[:, 0], dec[:, 0], each(below[:]), ALU.mult).then_inc(masked, 1)
                pool.tensor_tensor(dec[:, 1], dec[:, 1], each(upto[:]), ALU.mult).then_inc(masked, 1)
                pool.wait_ge(masked, 3 * t + 2)
                pool.tensor_tensor(dec[:, 0], dec[:, 0], heads(cur[:, b, BETA]), ALU.mult).then_inc(masked, 1)
                pool.wait_ge(back_copied, 2 * t + 2)
                pool.wait_ge(eg_done, t + 1)
                pool.tensor_tensor(qdT[:, b], qk_nT[:, 0:HEADS], eg[:, b], ALU.mult).then_inc(qd_done, 1)

            pool.sem_inc(kdec_done, 1)
            pool.sem_inc(qd_done, 1)
            pipeline(prepare, lambda t, b: None, lambda t, b: prepare(t + 1, 1 - b))(pool.Fori)

        @block.tensor
        def _(pe):
            def transposes(out, src, n0, count):
                for h in range(count):
                    last = pe.transpose(out[:, h], src[:, n0 + h], ident[:])
                return last

            def pre_scalars():
                pe.wait_ge(mask_sem, N_MASKS)
                pe.wait_ge(ba_loaded, 16)
                for t in range(TILES):
                    last = pe.transpose(b0[:].rearrange("p h f -> p (h f)")[:, 8 * t:8 * t + 8],
                                        ba_raw[:, t * P:(t + 1) * P], ident[0:8, 0:8])
                last.then_inc(pre, 1)
                pe.wait_ge(pre, PRE_GATE)
                pe.matmul(b1[:, 0, 0:64], upto[:], soft[:, 2].rearrange("p t h -> p (t h)"), start=True, stop=True)
                pe.matmul(b2[:, 0, 0:64], chunk[:], soft[:, 2].rearrange("p t h -> p (t h)"), start=True, stop=True).then_inc(pre, 1)
                pe.wait_ge(pre, PRE_GATE + 6)

            def p_turn(t, b):
                pe.wait_ge(loaded[b], 16 * (t - b) + 32)
                pe.wait_ge(banks_free, t + 1)
                transposes(b0, qkv[:, b], 0, HEADS)
                transposes(b1, qkv[:, b], HEADS, HEADS)
                transposes(b2, qkv[:, b], 2 * HEADS, HEADS)
                pe.wait_ge(cums_done, t + 1)
                pe.matmul(b3[:].rearrange("p h f -> p (h f)"), ones[:], cums[:].rearrange("p h f -> p (h f)"),
                          start=True, stop=True).then_inc(turned_done, 1)

            def p_back(t, b):
                pe.wait_ge(scaled, 3 * t + 3)
                transposes(b0, qk_n, 0, HEADS)
                transposes(b1, qk_n, HEADS, HEADS).then_inc(back_done, 1)

            def p_gram(t, b):
                pe.wait_ge(back_copied, 2 * t + 2)
                for h in range(HEADS):
                    pe.matmul(b0[:, h], qk_nT[:, HEADS + h], qk_nT[:, HEADS + h], start=True, stop=True)
                for h in range(HEADS):
                    last = pe.matmul(b1[:, h], qk_nT[:, HEADS + h], qk_nT[:, h], start=True, stop=True)
                last.then_inc(gram_done, 1)

            def p_first(t, b):
                pe.wait_ge(L_done, t + 1)
                transposes(b2, L, 0, HEADS).then_inc(LT_done, 1)

            def p_z(t, l):
                pe.wait_ge(u_step, (NL + 1) * t + l + 1)
                if l == 0:
                    pe.wait_ge(attn_done, t + 1)
                for h in range(HEADS):
                    last = pe.matmul(b0[:, h], L[:, h], U[:, h], start=True, stop=True)
                last.then_inc(zp_done, 1)
                transposes(b2, U, 0, HEADS).then_inc(tt_done, 1)

            def p_y(t, l):
                pe.wait_ge(t_copied, NL * t + l + 1)
                pe.wait_ge(z_done, (NL + 1) * t + l + 2)
                for h in range(HEADS):
                    last = pe.matmul(b1[:, h], T[:, h], Z[:, h], start=True, stop=True)
                last.then_inc(yp_done, 1)

            def p_wu(t, b):
                pe.wait_ge(u_step, (NL + 1) * (t + 1))
                pe.wait_ge(kbg_done, t + 1)
                for h in range(HEADS):
                    pe.matmul(b2[:, h], kbg[:, h], U[:, h], start=True, stop=True)
                for h in range(HEADS):
                    last = pe.matmul(b3[:, h], U[:, h], vb[:, h], start=True, stop=True)
                last.then_inc(wu_done, 1)

            def a_state(t, b, c):
                lo, hi = CHUNK * c, CHUNK * (c + 1)
                if c == 0:
                    pe.wait_ge(wu_copied, 2 * t + 2)
                    pe.wait_ge(qd_done, t + 2)
                    pe.wait_ge(on_done, t + 1)
                pe.wait_ge(s_done, 2 * t + c + 1)
                for h in range(HEADS):
                    last = pe.matmul(vs_ps[lo:hi, h], wT[:, b, h, lo:hi], S[:, h], start=True, stop=True)
                last.then_inc(ws_done, 1)
                for h in range(HEADS):
                    pe.matmul(o_ps[lo:hi, h], qdT[:, b, h, lo:hi], S[:, h], start=(h == 0), stop=False, skip_group_check=True)

            def a_update(t, b, c):
                lo, hi = CHUNK * c, CHUNK * (c + 1)
                pe.wait_ge(v_done, 2 * t + c + 1)
                if c == 0:
                    pe.wait_ge(kdec_done, t + 2)
                for h in range(HEADS):
                    last = pe.matmul(kv_ps[:, h], kdec[lo:hi, b, h], vnew[lo:hi, h], start=True, stop=True)
                last.then_inc(kv_done, 1)
                for h in range(HEADS):
                    last = pe.matmul(o_ps[lo:hi, h], attnT[lo:hi, b, h, lo:hi], vnew[lo:hi, h], start=False, stop=True,
                                     skip_group_check=True)
                last.then_inc(o_done, 1)

            def a_out(t, b):
                pe.wait_ge(on_done, t + 2)
                transposes(oT_ps, on, 0, HEADS).then_inc(oT_done, 1)

            def prepare(t, b):
                p_turn(t, b)
                p_back(t, b)
                p_gram(t, b)
                p_first(t, b)
                for l in range(NL):
                    p_z(t, l)
                    p_y(t, l)
                p_wu(t, b)

            def advance(t, b):
                for c in range(2):
                    a_state(t, b, c)
                    a_update(t, b, c)
                a_out(t, b)

            def both(t, b):
                n, m = t + 1, 1 - b
                p_turn(n, m)
                a_state(t, b, 0)
                p_back(n, m)
                a_update(t, b, 0)
                p_gram(n, m)
                a_state(t, b, 1)
                p_first(n, m)
                p_z(n, 0)
                a_update(t, b, 1)
                p_y(n, 0)
                p_z(n, 1)
                p_y(n, 1)
                p_z(n, 2)
                p_y(n, 2)
                a_out(t, b)
                for l in range(3, NL):
                    p_z(n, l)
                    p_y(n, l)
                p_wu(n, m)

            pe.sem_inc(turned_done, 1)
            pe.sem_inc(wu_done, 1)
            pre_scalars()
            pipeline(prepare, advance, both)(pe.Fori)

        @block.scalar
        def _(act):
            def pre_scalars():
                act.preload_act_table_set("natural_log_exp_and_others")
                act.wait_ge(small_loaded, 48)
                act.wait_ge(pre, 1)
                act.activation(ba[:].rearrange("p t c -> p (t c)"), b0[:, 0, :], ACT.Copy).then_inc(pre, 1)
                act.activation(rate[:], rate[:], ACT.Exp).then_inc(pre, 1)
                act.wait_ge(pre, 4)
                act.activation(soft[:, 1], soft[:, 0], ACT.Abs).then_inc(pre, 1)
                act.wait_ge(pre, 5)
                act.activation(soft[:, 1], soft[:, 1], ACT.Exp, scale=-1.0).then_inc(pre, 1)
                act.wait_ge(pre, 6)
                act.activation(soft[:, 1], soft[:, 1], ACT.Ln, bias=1.0).then_inc(pre, 1)
                act.activation(ba[:, :, 0:HEADS], ba[:, :, 0:HEADS], ACT.Exp, scale=-1.0).then_inc(pre, 1)
                act.wait_ge(pre, PRE_GATE + 1)
                act.activation(soft[:, 0].rearrange("p t h -> p (t h)"), b1[:, 0, 0:64], ACT.Exp).then_inc(pre, 1)
                act.wait_ge(pre, PRE_GATE + 4)
                act.activation(column(K_DEC), soft[:, 1], ACT.Exp).then_inc(pre, 1)

            def p_squares(t, b):
                act.wait_ge(turned_done, t + 2)
                act.wait_ge(rec_done, t + 1)
                act.activation(eg[:, b], b3[:], ACT.Exp).then_inc(eg_done, 1)
                act.activation(sq[:, 0:HEADS], b0[:], ACT.Square).then_inc(sq_done, 1)
                act.activation(sq[:, HEADS:], b1[:], ACT.Square).then_inc(sq_done, 1)

            def p_roots(t, b):
                act.wait_ge(ssq_done, t + 1)
                act.activation(rn[:, 0], ssq[:], ACT.Ln, bias=eps_l2[:, 0:1]).then_inc(log_done, 1)
                act.wait_ge(log_done, t + 1)
                act.activation(rn[:, 1], rn[:, 0], ACT.Exp, scale=-0.5).then_inc(root_done, 1)

            def p_decays(t, b):
                act.wait_ge(clamp_done, 2 * t + 2)
                act.activation(dec[:], dec[:], ACT.Exp).then_inc(dec_done, 1)

            def p_copy_back(t, b):
                act.wait_ge(back_done, t + 1)
                act.wait_ge(qd_done, t + 1)
                act.activation(qk_nT[:, 0:HEADS], b0[:], ACT.Copy, scale=float(P) ** -0.5).then_inc(back_copied, 1)
                act.activation(qk_nT[:, HEADS:], b1[:], ACT.Copy).then_inc(back_copied, 1)

            def p_copy_t(t, l):
                act.wait_ge(tt_done, NL * t + l + 1)
                act.activation(T[:], b2[:], ACT.Copy).then_inc(t_copied, 1)

            def p_copy_wu(t, b):
                act.wait_ge(wu_done, t + 2)
                act.activation(wT[:, b], b2[:], ACT.Copy).then_inc(wu_copied, 1)
                act.activation(u[:, b], b3[:], ACT.Copy).then_inc(wu_copied, 1)
                act.wait_ge(wu_copied, 2 * t + 2)
                act.sem_inc(banks_free, 1)

            def a_squares(t, b):
                act.wait_ge(o_done, 2 * t + 2)
                act.activation(osq[:], o_ps[:], ACT.Square).then_inc(osq_done, 1)

            def a_roots(t, b):
                act.wait_ge(ossq_done, t + 1)
                act.activation(orn[:, 0], ossq[:], ACT.Ln, bias=eps_l2[:, 0:1], scale=1.0 / P).then_inc(olog_done, 1)
                act.wait_ge(olog_done, t + 1)
                act.activation(orn[:, 1], orn[:, 0], ACT.Exp, scale=-0.5).then_inc(oroot_done, 1)

            def prepare(t, b):
                p_squares(t, b)
                p_roots(t, b)
                p_decays(t, b)
                p_copy_back(t, b)
                for l in range(NL):
                    p_copy_t(t, l)
                p_copy_wu(t, b)

            def advance(t, b):
                a_squares(t, b)
                a_roots(t, b)

            def both(t, b):
                n, m = t + 1, 1 - b
                p_squares(n, m)
                p_roots(n, m)
                p_decays(n, m)
                p_copy_back(n, m)
                p_copy_t(n, 0)
                p_copy_t(n, 1)
                a_squares(t, b)
                p_copy_t(n, 2)
                a_roots(t, b)
                p_copy_t(n, 3)
                p_copy_t(n, 4)
                p_copy_wu(n, m)

            act.wait_ge(const_sem, 4)
            act.sem_inc(banks_free, 1)
            pre_scalars()
            pipeline(prepare, advance, both)(act.Fori)

        @block.vector
        def _(dve):
            def pre_scalars():
                dve.memset(S[:], 0.0).then_inc(s_done, 1)
                dve.sem_inc(rec_done, 2)
                dve.sem_inc(on_done, 1)
                dve.wait_ge(pre, 3)
                dve.tensor_tensor(soft[:, 0], ba[:, :, HEADS:], bias[:].unsqueeze(1).broadcast_to([P, TILES, HEADS]),
                                  ALU.add).then_inc(pre, 1)
                dve.wait_ge(pre, 8)
                dve.scalar_tensor_tensor(soft[:, 1], soft[:, 0], 0.0, soft[:, 1], ALU.max, ALU.add).then_inc(pre, 1)
                dve.wait_ge(pre, 9)
                dve.scalar_tensor_tensor(soft[:, 2], soft[:, 1], -1.0, rate[:].unsqueeze(1).broadcast_to([P, TILES, HEADS]),
                                         ALU.mult, ALU.mult).then_inc(pre, 1)
                dve.tensor_scalar(ba[:, :, 0:HEADS], ba[:, :, 0:HEADS], 1.0, None, ALU.add).then_inc(pre, 1)
                dve.wait_ge(pre, 11)
                dve.reciprocal(column(BETA), ba[:, :, 0:HEADS]).then_inc(pre, 1)
                dve.tensor_copy(column(GATE), soft[:, 2]).then_inc(pre, 1)
                dve.wait_ge(pre, PRE_GATE + 2)
                view = lambda bank: bank[:, 0, 0:64].rearrange("p (t h) -> p t h", h=HEADS)
                dve.tensor_copy(column(GCUM), view(b1)).then_inc(pre, 1)
                dve.wait_ge(pre, PRE_GATE + 3)
                dve.tensor_tensor(soft[:, 1], view(b2), column(GCUM), ALU.subtract).then_inc(pre, 1)
                dve.tensor_tensor(column(BETA_G), column(BETA), soft[:, 0], ALU.mult).then_inc(pre, 1)
                dve.wait_ge(pre, PRE_GATE + 6)

            def p_scalars(t, b):
                dve.wait_ge(rec_done, t + 1)
                dve.tensor_scalar(cur[:, b].rearrange("p c h -> p (c h)"), scal[:, bass.ds(t, 1)].rearrange("p a c -> p (a c)"),
                                  1.0, None, ALU.mult).then_inc(cur_done, 1)

            def p_ssq(t, b):
                dve.wait_ge(sq_done, 2 * t + 2)
                dve.tensor_reduce(ssq[:], sq[:], AX.X, ALU.add).then_inc(ssq_done, 1)

            def p_difference(t, b):
                dve.wait_ge(cur_done, t + 1)
                dve.wait_ge(eg_done, t + 1)
                dve.tensor_tensor(dif[:], b3[:], heads(cur[:, b, GCUM]), ALU.subtract).then_inc(dif_done, 1)
                dve.wait_ge(dif_done, t + 1)
                dve.tensor_scalar(dec[:, 0], dif[:], 0.0, -1.0, ALU.max, ALU.mult).then_inc(clamp_done, 1)
                dve.tensor_scalar(dec[:, 1], dif[:], 0.0, None, ALU.min).then_inc(clamp_done, 1)

            def p_newton(t, b):
                dve.wait_ge(root_done, t + 1)
                dve.tensor_tensor(rn[:, 2], rn[:, 1], rn[:, 1], ALU.mult).then_inc(newton, 1)
                dve.tensor_scalar(ssq[:], ssq[:], RMS_EPS, -0.5, ALU.add, ALU.mult).then_inc(newton, 1)
                dve.wait_ge(newton, 4 * t + 2)
                dve.tensor_tensor(rn[:, 2], rn[:, 2], ssq[:], ALU.mult).then_inc(newton, 1)
                dve.wait_ge(newton, 4 * t + 3)
                dve.scalar_tensor_tensor(rn[:, 3], rn[:, 2], 1.5, rn[:, 1], ALU.add, ALU.mult).then_inc(newton, 1)
                dve.wait_ge(newton, 4 * t + 4)

            def p_scale(t, b):
                dve.wait_ge(kdec_done, t + 1)
                dve.tensor_tensor(qk_n[:, HEADS:], b1[:], heads(rn[:, 3, HEADS:]), ALU.mult).then_inc(scaled, 1)
                dve.tensor_tensor(qk_n[:, 0:HEADS], b0[:], heads(rn[:, 3, 0:HEADS]), ALU.mult).then_inc(scaled, 1)
                dve.tensor_tensor(vb[:], b2[:], heads(cur[:, b, BETA]), ALU.mult).then_inc(scaled, 1)

            def p_grams(t, b):
                dve.wait_ge(gram_done, t + 1)
                dve.wait_ge(masked, 3 * t + 3)
                dve.tensor_tensor(L[:], b0[:], dec[:, 0], ALU.mult).then_inc(L_done, 1)
                dve.tensor_tensor(attnT[:, b], b1[:], dec[:, 1], ALU.mult).then_inc(attn_done, 1)

            def p_first(t, b):
                dve.wait_ge(LT_done, t + 1)
                dve.tensor_tensor(Z[:], b2[:], each(corner[:, 0]), ALU.mult).then_inc(z_done, 1)
                dve.wait_ge(z_done, (NL + 1) * t + 1)
                dve.tensor_tensor(U[:], each(ident[:]), Z[:], ALU.subtract).then_inc(u_step, 1)

            def p_z(t, l):
                dve.wait_ge(zp_done, NL * t + l + 1)
                dve.tensor_tensor(Z[:], b0[:], each(corner[:, l + 1]), ALU.mult).then_inc(z_done, 1)

            def p_u(t, l):
                dve.wait_ge(yp_done, NL * t + l + 1)
                dve.tensor_tensor(U[:], U[:], b1[:], ALU.subtract).then_inc(u_step, 1)

            def a_v(t, b, c):
                lo, hi = CHUNK * c, CHUNK * (c + 1)
                dve.wait_ge(ws_done, 2 * t + c + 1)
                dve.tensor_tensor(vnew[lo:hi], u[lo:hi, b], vs_ps[lo:hi], ALU.subtract).then_inc(v_done, 1)
                dve.wait_ge(s_done, 2 * t + c + 1)
                dve.tensor_tensor(Sd[:], S[:], eg[:, b, :, hi - 1:hi].broadcast_to([P, HEADS, P]), ALU.mult).then_inc(sd_done, 1)

            def a_s(t, b, c):
                dve.wait_ge(sd_done, 2 * t + c + 1)
                dve.wait_ge(kv_done, 2 * t + c + 1)
                dve.tensor_tensor(S[:], Sd[:], kv_ps[:], ALU.add).then_inc(s_done, 1)

            def a_norm(t, b):
                dve.wait_ge(osq_done, t + 1)
                dve.tensor_reduce(ossq[:], osq[:], AX.X, ALU.add).then_inc(ossq_done, 1)
                dve.wait_ge(oroot_done, t + 1)
                dve.tensor_tensor(orn[:, 2], orn[:, 1], orn[:, 1], ALU.mult).then_inc(onewton, 1)
                dve.tensor_scalar(ossq[:], ossq[:], RMS_EPS * P, -0.5 / P, ALU.add, ALU.mult).then_inc(onewton, 1)
                dve.wait_ge(onewton, 4 * t + 2)
                dve.tensor_tensor(orn[:, 2], orn[:, 2], ossq[:], ALU.mult).then_inc(onewton, 1)
                dve.wait_ge(onewton, 4 * t + 3)
                dve.scalar_tensor_tensor(orn[:, 3], orn[:, 2], 1.5, orn[:, 1], ALU.add, ALU.mult).then_inc(onewton, 1)
                dve.wait_ge(onewton, 4 * t + 4)
                dve.tensor_tensor(on[:], o_ps[:], heads(orn[:, 3]), ALU.mult).then_inc(on_done, 1)

            def a_gate(t, b):
                dve.wait_ge(oT_done, t + 1)
                dve.wait_ge(mix_free, t + 1)
                dve.scalar_tensor_tensor(mix[:], oT_ps[:], gnorm[:, 0:1], zT[:, b], ALU.mult, ALU.mult).then_inc(mix_done, 1)
                dve.wait_ge(mix_done, t + 1)
                dve.sem_inc(rec_done, 1)

            def prepare(t, b):
                p_scalars(t, b)
                p_difference(t, b)
                p_ssq(t, b)
                p_newton(t, b)
                p_scale(t, b)
                p_grams(t, b)
                p_first(t, b)
                for l in range(NL):
                    p_z(t, l)
                    p_u(t, l)

            def advance(t, b):
                for c in range(2):
                    a_v(t, b, c)
                    a_s(t, b, c)
                a_norm(t, b)
                a_gate(t, b)

            def both(t, b):
                n, m = t + 1, 1 - b
                p_scalars(n, m)
                p_difference(n, m)
                a_v(t, b, 0)
                p_ssq(n, m)
                p_newton(n, m)
                p_scale(n, m)
                a_s(t, b, 0)
                p_grams(n, m)
                a_v(t, b, 1)
                p_first(n, m)
                p_z(n, 0)
                a_s(t, b, 1)
                p_u(n, 0)
                p_z(n, 1)
                p_u(n, 1)
                p_z(n, 2)
                a_norm(t, b)
                p_u(n, 2)
                for l in range(3, NL):
                    p_z(n, l)
                    p_u(n, l)
                a_gate(t, b)

            pre_scalars()
            pipeline(prepare, advance, both)(dve.Fori)


def attention(nc, made, mixT):
    QB = 2 * P
    NB = SEQ // QB
    blocks = [(0, j) for j in range(NB)] + [(1, j) for j in reversed(range(NB))]
    N = len(blocks)
    pairs = [j + 1 for _, j in blocks]
    groups = [j // 2 + 1 for _, j in blocks]
    pair0 = [sum(pairs[:n]) for n in range(N + 1)]
    group0 = [sum(2 * g for g in groups[:n]) for n in range(N + 1)]
    PAIRS, GROUPS = pair0[-1], group0[-1]
    ROUNDS = HEADS // 2
    S_RING, T_RING = 4, 3
    MASK = -1e30
    with ExitStack() as ctx:
        s = Scope(nc, ctx, "at")
        q_hi, q_lo, k_hi, k_lo, v_hi, v_lo, qr = (s.sb(n, [P, 2, SEQ], F32R) for n in
                                                  ("q_hi", "q_lo", "k_hi", "k_lo", "v_hi", "v_lo", "qr"))
        kr = s.sb("kr", [P, SEQ], F32R)
        kr_hi = s.sb("kr_hi", [P, SEQ], F32R)
        ident = s.sb("ident", [P, P])
        prob = s.sb("prob", [P, 2, 2, SEQ])
        negm = s.sb("negm", [P, 2, 2, 4])
        sums = s.sb("sums", [P, 2, 2, 4])
        top = s.sb("top", [P, 2, 2])
        fac = s.sb("fac", [P, 2, 2, 4])
        part = s.sb("part", [P, 2, 2, 4])
        total = s.sb("total", [P, 2, 2])
        scale = s.sb("scale", [P, 2, 2, 4])
        pT_hi = s.sb("pT_hi", [P, T_RING, 2 * QB], F32R)
        pT_lo = s.sb("pT_lo", [P, T_RING, 2 * QB], F32R)
        out = s.sb("out", [P, 2, QB])
        score_ps = s.ps("score_ps", [P, S_RING, NTOK])
        pT_ps = s.ps("pT_ps", [P, T_RING, 2 * QB])
        acc_ps = s.ps("acc_ps", [P, NTOK])

        C_EXP, C_TURN, C_LO, C_PV, C_OUT, C_FREE = S_RING, 2, T_RING, T_RING, 1, 2
        const_sem = s.sem("consts")
        kr_loaded = s.sem("kr_loaded")
        loaded = [s.sem(f"loaded{b}") for b in range(2)]
        score_done = s.sem("score_done")
        diag_done = s.sem("diag_done")
        max_done = s.sem("max_done")
        exp_done = s.sem("exp_done")
        top_done, gap_done, fac_done, part_done, total_done, inv_done = (
            s.sem(n) for n in ("top_done", "gap_done", "fac_done", "part_done", "total_done", "inv_done"))
        scale_done = s.sem("scale_done")
        scaled = s.sem("scaled")
        turned = s.sem("turned")
        hi_done = s.sem("hi_done")
        lo_done = s.sem("lo_done")
        pv_done = s.sem("pv_done")
        out_done = s.sem("out_done")
        out_free = s.sem("out_free")
        storing, stored = s.sem("storing"), s.sem("stored")
        block = ctx.enter_context(nc.Block())
        LOADS = 8
        many = [n for n in range(N) if groups[n] > 1]
        MANY = len(many)

        def widths(j, tile):
            keys = P * (2 * j + tile + 1)
            return [min(NTOK, keys - NTOK * g) for g in range(j // 2 + 1)]

        @block.gpsimd
        def _(pool):
            def load(h):
                b = h % 2
                for dst, name in ((q_hi, "qnT_hi"), (k_hi, "knT_hi"), (q_lo, "qnT_lo"), (k_lo, "knT_lo")):
                    pool.dma_start(dst[:, b], made[name][h]).then_inc(loaded[b], 16)
                pool.dma_start(qr[0:ROPE, b], made["qrT_lo"][h]).then_inc(loaded[b], 16)
                pool.dma_start(qr[ROPE:, b], made["qrT_hi"][h]).then_inc(loaded[b], 16)
                for dst, name in ((v_hi, "v_hi"), (v_lo, "v_lo")):
                    pool.dma_start(dst[:, b].rearrange("p (a n) -> p a n", n=P),
                                   made[name][:, :, P * h:P * h + P].rearrange("a p n -> p a n")).then_inc(loaded[b], 16)

            load(0)
            for dst, name in ((kr[0:ROPE], "krT_hi"), (kr[ROPE:], "krT_lo"), (kr_hi[ROPE:], "krT_hi")):
                pool.dma_start(dst, made[name]).then_inc(kr_loaded, 16)
            load(1)
            pool.memset(ident[:], 0.0).then_inc(const_sem, 1)
            pool.wait_ge(const_sem, 1)
            pool.affine_select(out=ident[:], in_=ident[:], compare_op=ALU.not_equal, fill=1.0, base=0, pattern=[[-1, P]],
                               channel_multiplier=1).then_inc(const_sem, 1)
            for i in range(ROUNDS):
                for n, (b, j) in enumerate(blocks):
                    if i + 1 < ROUNDS and n == NB + 1:
                        pool.wait_ge(pv_done, pair0[NB] + C_PV)
                        load(2 * (i + 1))
                    if i and n == 1:
                        pool.wait_ge(pv_done, PAIRS * i + C_PV)
                        load(2 * i + 1)
                    pool.wait_ge(scale_done, N * i + n + 1)
                    pb, g = n % 2, groups[n]
                    ops = []
                    for tile in range(2):
                        if g > 1:
                            view = prob[:, pb, tile, 0:NTOK * (g - 1)].rearrange("p (g n) -> p g n", n=NTOK)
                            ops.append((view, scale[:, pb, tile, 0:g - 1].unsqueeze(2).broadcast_to([P, g - 1, NTOK])))
                        w = widths(j, tile)[-1]
                        view = prob[:, pb, tile, NTOK * (g - 1):NTOK * (g - 1) + w]
                        ops.append((view, scale[:, pb, tile, g - 1:g].broadcast_to([P, w])))
                    for view, by in ops:
                        op = pool.tensor_tensor(view, view, by, ALU.mult)
                    op.then_inc(scaled, 1)

        @block.tensor
        def _(pe):
            def scores(i, n):
                b, j = blocks[n]
                if j == (0 if b == 0 else NB - 1):
                    pe.wait_ge(loaded[b], 16 * LOADS * i + 16 * LOADS)
                G = group0[n]
                for tile in range(2):
                    qs = slice(QB * j + P * tile, QB * j + P * tile + P)
                    for g, w in enumerate(widths(j, tile)):
                        pe.wait_ge(exp_done, GROUPS * i + (G + 1 - S_RING + C_EXP))
                        ks, acc = slice(NTOK * g, NTOK * g + w), score_ps[:, G % S_RING, 0:w]
                        pe.matmul(acc, q_lo[:, b, qs], k_hi[:, b, ks], start=True, stop=False)
                        pe.matmul(acc, qr[:, b, qs], kr[:, ks], start=False, stop=False)
                        pe.matmul(acc, qr[ROPE:, b, qs], kr_hi[ROPE:, ks], start=False, stop=False)
                        pe.matmul(acc, q_hi[:, b, qs], k_lo[:, b, ks], start=False, stop=False)
                        pe.matmul(acc, q_hi[:, b, qs], k_hi[:, b, ks], start=False, stop=True).then_inc(score_done, 1)
                        G += 1

            def turn(i, n, p):
                j, k = blocks[n][1], pair0[n] + p
                if p == 0:
                    pe.wait_ge(scaled, N * i + n + 1)
                pe.wait_ge(lo_done, PAIRS * i + (k + 1 - T_RING + C_LO))
                for kt in range(2):
                    for tile in range(2):
                        if p == j and kt > tile:
                            continue
                        at = QB * kt + P * (tile if p < j or kt == 0 else 0)
                        src = prob[:, n % 2, tile, P * (2 * p + kt):P * (2 * p + kt) + P]
                        last = pe.transpose(pT_ps[:, k % T_RING, at:at + P], src, ident[:])
                last.then_inc(turned, 1)

            def values(i, n, p):
                (b, j), k = blocks[n], pair0[n] + p
                if p == 0:
                    pe.wait_ge(out_done, N * i + (n + C_OUT))
                pe.wait_ge(lo_done, PAIRS * i + (k + 1 + C_LO))
                for kt in range(2):
                    diag = p == j and kt == 1
                    acc = acc_ps[:, P:QB] if diag else acc_ps[:, 0:QB]
                    ps = slice(QB * kt, QB * kt + (P if diag else QB))
                    vs = slice(P * (2 * p + kt), P * (2 * p + kt) + P)
                    r = k % T_RING
                    pe.matmul(acc, v_lo[:, b, vs], pT_hi[:, r, ps], start=(p == 0 and kt == 0), stop=False)
                    pe.matmul(acc, v_hi[:, b, vs], pT_lo[:, r, ps], start=False, stop=False)
                    last = pe.matmul(acc, v_hi[:, b, vs], pT_hi[:, r, ps], start=False, stop=diag)
                last.then_inc(pv_done, 1)

            pe.wait_ge(kr_loaded, 48)
            pe.wait_ge(const_sem, 2)
            pe.sem_inc(turned, C_TURN)
            pe.sem_inc(pv_done, C_PV)
            with pe.Fori(0, ROUNDS) as i:
                scores(i, 0)
                for n in range(N):
                    if n + 1 < N:
                        scores(i, n + 1)
                    for p in range(min(2, pairs[n])):
                        turn(i, n, p)
                    for p in range(pairs[n]):
                        if p + 2 < pairs[n]:
                            turn(i, n, p + 2)
                        values(i, n, p)

        @block.scalar
        def _(act):
            def exps(i, n):
                j, pb, G = blocks[n][1], n % 2, group0[n]
                act.wait_ge(turned, PAIRS * i + (pair0[n] - pairs[n - 1] + C_TURN))
                for tile in range(2):
                    for g, w in enumerate(widths(j, tile)):
                        act.wait_ge(max_done, GROUPS * i + (G + 1))
                        act.activation(prob[:, pb, tile, NTOK * g:NTOK * g + w], score_ps[:, G % S_RING, 0:w], ACT.Exp,
                                       bias=negm[:, pb, tile, g:g + 1], accum_out=sums[:, pb, tile, g:g + 1]).then_inc(exp_done, 1)
                        G += 1
                if groups[n] > 1:
                    m, gs = many.index(n), slice(0, groups[n])
                    act.wait_ge(gap_done, MANY * i + (m + 1))
                    act.activation(fac[:, pb, :, gs], part[:, pb, :, gs], ACT.Exp).then_inc(fac_done, 1)

            def copies(i, n):
                for p in range(pairs[n]):
                    k = pair0[n] + p
                    w = 2 * QB if p + 1 < pairs[n] else QB + P
                    act.wait_ge(turned, PAIRS * i + (k + 1 + C_TURN))
                    act.wait_ge(pv_done, PAIRS * i + (k + 1 - T_RING + C_PV))
                    act.activation(pT_hi[:, k % T_RING, 0:w], pT_ps[:, k % T_RING, 0:w], ACT.Copy).then_inc(hi_done, 1)
                act.wait_ge(pv_done, PAIRS * i + (pair0[n + 1] + C_PV))
                act.wait_ge(out_free, N * i + (n - 1 + C_FREE))
                act.activation(out[:, n % 2], acc_ps[:, 0:QB], ACT.Copy).then_inc(out_done, 1)

            act.preload_act_table(ACT.Exp)
            act.sem_inc(exp_done, C_EXP)
            act.sem_inc(out_done, C_OUT)
            with act.Fori(0, ROUNDS) as i:
                exps(i, 0)
                for n in range(N):
                    if n + 1 < N:
                        exps(i, n + 1)
                    copies(i, n)

        @block.vector
        def _(dve):
            def maxima(i, n):
                j, pb, G = blocks[n][1], n % 2, group0[n]
                for tile in range(2):
                    ws = widths(j, tile)
                    for g, w in enumerate(ws):
                        acc = score_ps[:, G % S_RING, 0:w]
                        dve.wait_ge(score_done, GROUPS * i + (G + 1))
                        if g + 1 == len(ws):
                            dve.memset(acc[0:CHUNK, w - CHUNK:w], MASK).then_inc(diag_done, 1)
                            dve.wait_ge(diag_done, 2 * N * i + (2 * n + tile + 1))
                        dve.tensor_reduce(negm[:, pb, tile, g:g + 1], acc, AX.X, ALU.max, negate=True).then_inc(max_done, 1)
                        G += 1
                dve.wait_ge(max_done, GROUPS * i + G)
                gs, g = slice(0, groups[n]), groups[n]
                if g == 1:
                    dve.wait_ge(exp_done, GROUPS * i + (G + C_EXP))
                    dve.reciprocal(scale[:, pb, :, gs], sums[:, pb, :, gs]).then_inc(scale_done, 1)
                    return
                m = many.index(n)
                dve.tensor_reduce(top[:, pb], negm[:, pb, :, gs], AX.X, ALU.min).then_inc(top_done, 1)
                dve.wait_ge(top_done, MANY * i + (m + 1))
                wide = top[:, pb].unsqueeze(2).broadcast_to([P, 2, g])
                dve.tensor_tensor(part[:, pb, :, gs], wide, negm[:, pb, :, gs], ALU.subtract).then_inc(gap_done, 1)
                dve.wait_ge(fac_done, MANY * i + (m + 1))
                dve.tensor_tensor(part[:, pb, :, gs], fac[:, pb, :, gs], sums[:, pb, :, gs], ALU.mult).then_inc(part_done, 1)
                dve.wait_ge(part_done, MANY * i + (m + 1))
                dve.tensor_reduce(total[:, pb], part[:, pb, :, gs], AX.X, ALU.add).then_inc(total_done, 1)
                dve.wait_ge(total_done, MANY * i + (m + 1))
                dve.reciprocal(total[:, pb], total[:, pb]).then_inc(inv_done, 1)
                dve.wait_ge(inv_done, MANY * i + (m + 1))
                wide = total[:, pb].unsqueeze(2).broadcast_to([P, 2, g])
                dve.tensor_tensor(scale[:, pb, :, gs], fac[:, pb, :, gs], wide, ALU.mult).then_inc(scale_done, 1)

            def lows(i, n):
                for p in range(pairs[n]):
                    k = pair0[n] + p
                    w = 2 * QB if p + 1 < pairs[n] else QB + P
                    r = k % T_RING
                    dve.wait_ge(hi_done, PAIRS * i + (k + 1))
                    dve.tensor_tensor(pT_lo[:, r, 0:w], pT_ps[:, r, 0:w], pT_hi[:, r, 0:w].bitcast(F32),
                                      ALU.subtract).then_inc(lo_done, 1)

            dve.sem_inc(lo_done, C_LO)
            with dve.Fori(0, ROUNDS) as i:
                maxima(i, 0)
                for n in range(N):
                    if n + 1 < N:
                        maxima(i, n + 1)
                    lows(i, n)

        @block.sync
        def _(sp):
            sp.sem_inc(out_free, C_FREE)
            with sp.Fori(0, ROUNDS) as i:
                for n, (b, j) in enumerate(blocks):
                    dst = mixT[bass.ds(2 * i + (HEADS + b), 1), :, QB * j:QB * (j + 1)].rearrange("a p t -> p (a t)")
                    sp.wait_ge(out_done, N * i + (n + 1 + C_OUT))
                    sp.sem_inc(storing, 1)
                    sp.dma_start(dst, out[:, n % 2]).then_inc(stored, 16)
                    sp.wait_ge(stored, 16 * N * i + 16 * (n + 1))
                    sp.sem_inc(out_free, 1)


def feed_in(nc, xT, w_gate_up, hid):
    with ExitStack() as ctx:
        s = Scope(nc, ctx, "ff")
        x_raw = s.sb("x_raw", [P, 2, SEQ])
        x_hi = s.sb("x_hi", [P, KD, SEQ], F32R)
        x_lo = s.sb("x_lo", [P, KD, SEQ], F32R)
        w_raw = s.sb("w_raw", [P, 2, KD * P])
        w_hi = s.sb("w_hi", [P, 2, KD * P], F32R)
        w_lo = s.sb("w_lo", [P, 2, KD * P], F32R)
        zero = s.sb("zero", [P, 1])
        out = s.sb("out", [P, 2, SEQ])
        h_ps = s.ps("h_ps", [P, 2, BLOCKS, NTOK])

        x_loaded = [s.sem(f"x_loaded{b}") for b in range(2)]
        x_hi_done, x_lo_done = s.sem("x_hi_done"), s.sem("x_lo_done")
        w_loaded = [s.sem(f"w_loaded{b}") for b in range(2)]
        w_hi_done, w_lo_done = s.sem("w_hi_done"), s.sem("w_lo_done")
        made = s.sem("made")
        gate_free, up_free = s.sem("gate_free"), s.sem("up_free")
        zeroed = s.sem("zeroed")
        silu_done = s.sem("silu_done")
        out_made = s.sem("out_made")
        out_free = s.sem("out_free")
        stored = [s.sem(f"stored{b}") for b in range(2)]
        block = ctx.enter_context(nc.Block())

        @block.sync
        def _(sp):
            for k in range(KD):
                if k >= 2:
                    sp.wait_ge(x_lo_done, k - 1)
                sp.dma_start(x_raw[:, k % 2, :], xT[k]).then_inc(x_loaded[k % 2], 16)
            sp.sem_inc(out_free, 2)
            with sp.Fori(0, FT // 2) as i:
                for b in range(2):
                    dst = hid[:, :, bass.ds(2 * i + b, 1), :].rearrange("t p a c -> p t (a c)")
                    sp.wait_ge(out_made, 2 * i + b + 1)
                    sp.dma_start(dst, out[:, b].rearrange("p (t c) -> p t c", c=P)).then_inc(stored[b], 16)
                    sp.wait_ge(stored[b], 16 * i + 16)
                    sp.sem_inc(out_free, 1)

        @block.gpsimd
        def _(pool):
            def load(m, b):
                pool.dma_start(w_raw[:, b, :], w_gate_up[bass.ds(m, 1)].rearrange("a p f -> p (a f)")).then_inc(w_loaded[b], 16)

            def split(i, b):
                m = 2 * i + b
                pool.wait_ge(w_loaded[b], 16 * i + 16)
                if b:
                    pool.wait_ge(up_free, i + 1)
                else:
                    pool.wait_ge(gate_free, i + 1)
                pool.tensor_tensor(w_hi[:, b, :], w_raw[:, b, :], zero[:, 0:1].broadcast_to([P, KD * P]),
                                   ALU.add).then_inc(w_hi_done, 1)
                pool.wait_ge(w_hi_done, m + 1)
                pool.tensor_tensor(w_lo[:, b, :], w_raw[:, b, :], w_hi[:, b, :].bitcast(F32),
                                   ALU.subtract).then_inc(w_lo_done, 1)

            pool.memset(zero[:, :], 0.0).then_inc(zeroed, 1)
            pool.wait_ge(zeroed, 1)
            load(0, 0)
            load(1, 1)
            with pool.Fori(0, FT - 1) as i:
                for b in range(2):
                    split(i, b)
                    pool.wait_ge(w_lo_done, 2 * i + b + 1)
                    load(2 * i + b + 2, b)
            for b in range(2):
                split(FT - 1, b)

        @block.tensor
        def _(pe):
            with pe.Fori(0, FT) as i:
                for b in range(2):
                    pe.wait_ge(w_lo_done, 2 * i + b + 1)
                    pe.wait_ge(up_free if b else gate_free, i + 1)
                    for k in range(KD):
                        pe.wait_ge(x_lo_done, k + 1)
                        ws = slice(k * P, (k + 1) * P)
                        for t in range(BLOCKS):
                            ts = slice(t * NTOK, (t + 1) * NTOK)
                            acc = h_ps[:, b, t, :]
                            pe.matmul(acc, w_lo[:, b, ws], x_hi[:, k, ts], start=(k == 0), stop=False)
                            pe.matmul(acc, w_hi[:, b, ws], x_lo[:, k, ts], start=False, stop=False)
                            last = pe.matmul(acc, w_hi[:, b, ws], x_hi[:, k, ts], start=False, stop=(k == KD - 1))
                    last.then_inc(made, 1)

        @block.scalar
        def _(act):
            act.sem_inc(gate_free, 1)
            for k in range(KD):
                act.wait_ge(x_loaded[k % 2], 16 * (k // 2 + 1))
                act.activation(x_hi[:, k, :], x_raw[:, k % 2, :], ACT.Copy).then_inc(x_hi_done, 1)
            act.preload_act_table(ACT.Silu)
            with act.Fori(0, FT // 2) as i:
                for b in range(2):
                    act.wait_ge(made, 4 * i + 2 * b + 1)
                    act.wait_ge(out_free, 2 * i + b + 1)
                    act.activation(out[:, b], h_ps[:, 0].rearrange("p a t -> p (a t)"), ACT.Silu).then_inc(silu_done, 1)
                    act.wait_ge(silu_done, 2 * i + b + 1)
                    act.sem_inc(gate_free, 1)

        @block.vector
        def _(dve):
            dve.sem_inc(up_free, 1)
            for k in range(KD):
                dve.wait_ge(x_hi_done, k + 1)
                dve.tensor_tensor(x_lo[:, k, :], x_raw[:, k % 2, :], x_hi[:, k, :].bitcast(F32),
                                  ALU.subtract).then_inc(x_lo_done, 1)
            with dve.Fori(0, FT // 2) as i:
                for b in range(2):
                    dve.wait_ge(made, 4 * i + 2 * b + 2)
                    dve.wait_ge(silu_done, 2 * i + b + 1)
                    dve.tensor_tensor(out[:, b], out[:, b], h_ps[:, 1].rearrange("p a t -> p (a t)"), ALU.mult).then_inc(out_made, 1)
                    dve.wait_ge(out_made, 2 * i + b + 1)
                    dve.sem_inc(up_free, 1)


def reached(eng, sem, count):
    if not (isinstance(count, int) and count <= 0):
        eng.wait_ge(sem, count)


def hold(eng, begun):
    eng.sem_inc(begun, 1)


def over_tiles(loop, first, tile, last):
    first(0, 0)
    tile(0, 1)
    tile(0, 2)
    with loop(1, TILES // 2 - 1) as i:
        tile(i, 1)
        tile(i, 2)
    tile(TILES // 2 - 1, 1)
    last(TILES // 2 - 1, 2)


class TokenProduct:

    def __init__(self, nc, s, K, lhs, weights, w_raw, accs):
        self.nc, self.K, self.lhs, self.weights, self.w_raw = nc, K, lhs, weights, w_raw
        self.CH = K // 2
        self.accs = accs
        self.w_hi = s.sb("w_hi", [P, K, D_MODEL], F32R)
        self.w_lo = s.sb("w_lo", [P, K, D_MODEL], F32R)
        self.a_raw = s.sb("a_raw", [P, 2, 2 * P])
        self.a_hi = s.sb("a_hi", [P, 2, 2 * P], F32R)
        self.a_lo = s.sb("a_lo", [P, 2, 2 * P], F32R)
        self.w_loaded = [s.sem(f"w_loaded{b}") for b in range(2)]
        self.w_hi_done, self.w_lo_done = s.sem("w_hi_done"), s.sem("w_lo_done")
        self.a_loaded = [s.sem(f"a_loaded{b}") for b in range(2)]
        self.a_hi_done, self.a_lo_done = s.sem("a_hi_done"), s.sem("a_lo_done")
        self.a_used = s.sem("a_used")

    def chunk(self, i, b, c):
        n = self.CH * b + c
        return 2 * self.CH * i + n, n % 2, self.CH * i + n // 2 + 1

    def product_done(self, eng, i, b):
        eng.wait_ge(self.a_used, 2 * self.CH * i + self.CH * (b + 1))

    def load_weights(self, eng):
        for k in range(self.K):
            reached(eng, self.w_lo_done, k - 1)
            eng.dma_start(self.w_raw[:, k % 2], self.weights[k]).then_inc(self.w_loaded[k % 2], 16)

    def load(self, eng, i, b):
        for c in range(self.CH):
            n, slot, _ = self.chunk(i, b, c)
            src = self.lhs(2 * i + b, 2 * c)
            reached(eng, self.a_lo_done, n - 1)
            eng.dma_start(self.a_raw[:, slot].rearrange("p (k t) -> p k t", k=2), src).then_inc(self.a_loaded[slot], 16)

    def high(self, act, i, b, c, with_weights=False):
        n, slot, loads = self.chunk(i, b, c)
        if with_weights:
            for k in (2 * c, 2 * c + 1):
                act.wait_ge(self.w_loaded[k % 2], 16 * (k // 2 + 1))
                act.activation(self.w_hi[:, k], self.w_raw[:, k % 2], ACT.Copy).then_inc(self.w_hi_done, 1)
        act.wait_ge(self.a_loaded[slot], 16 * loads)
        reached(act, self.a_used, n - 1)
        act.activation(self.a_hi[:, slot], self.a_raw[:, slot], ACT.Copy).then_inc(self.a_hi_done, 1)

    def low(self, dve, i, b, c, with_weights=False):
        n, slot, _ = self.chunk(i, b, c)
        if with_weights:
            for k in (2 * c, 2 * c + 1):
                dve.wait_ge(self.w_hi_done, k + 1)
                dve.tensor_tensor(self.w_lo[:, k], self.w_raw[:, k % 2], self.w_hi[:, k].bitcast(F32),
                                  ALU.subtract).then_inc(self.w_lo_done, 1)
        dve.wait_ge(self.a_hi_done, n + 1)
        dve.tensor_tensor(self.a_lo[:, slot], self.a_raw[:, slot], self.a_hi[:, slot].bitcast(F32),
                          ALU.subtract).then_inc(self.a_lo_done, 1)

    def product(self, pe, i, b, acc_free):
        reached(pe, acc_free, 2 * i + b - 1)
        for c in range(self.CH):
            n, slot, _ = self.chunk(i, b, c)
            if isinstance(i, int) and i == 0 and b == 0:
                pe.wait_ge(self.w_lo_done, 2 * c + 2)
            pe.wait_ge(self.a_lo_done, n + 1)
            for k in (2 * c, 2 * c + 1):
                k0, k1, acc = next(a for a in self.accs if a[0] <= k <= a[1])
                rows = slice(P * (k % 2), P * (k % 2) + P)
                for half in range(2):
                    cols = slice(NTOK * half, NTOK * (half + 1))
                    to = acc[:, b % 2, cols]
                    pe.matmul(to, self.a_lo[:, slot, rows], self.w_hi[:, k, cols], start=(k == k0), stop=False)
                    pe.matmul(to, self.a_hi[:, slot, rows], self.w_lo[:, k, cols], start=False, stop=False)
                    last = pe.matmul(to, self.a_hi[:, slot, rows], self.w_hi[:, k, cols], start=False, stop=(k == k1))
            last.then_inc(self.a_used, 1)


def project_norm(nc, stage, K, lhs, weights, res, gain, bias, x_out, xT_out):
    with ExitStack() as ctx:
        s = Scope(nc, ctx, stage)
        y = s.sb("y", [P, 2, D_MODEL])
        g_all = s.sb("g_all", [P, D_MODEL])
        b_all = s.sb("b_all", [P, D_MODEL])
        ident = s.sb("ident", [P, P])
        stats = s.sb("stats", [P, 2, 6])
        mean = s.sb("mean", [P, 2])
        eps = s.sb("eps", [P, 1])
        root = s.sb("root", [P, 4])
        rstd = root[:, 3:4]
        xT = s.sb("xT", [P, KD, P])
        acc = s.ps("acc", [P, 2, D_MODEL])
        xT_ps = s.ps("xT_ps", [P, KD, P])
        tp = TokenProduct(nc, s, K, lhs, weights, y, [(0, K - 1, acc)])

        const_sem = s.sem("consts")
        small_loaded = s.sem("small_loaded")
        res_loaded = [s.sem(f"res_loaded{b}") for b in range(2)]
        added = s.sem("added")
        stats_done, mean_done, root_done, newton, normed = (s.sem(n) for n in ("stats_done", "mean_done", "root_done", "newton", "normed"))
        gained, y_done = s.sem("gained"), s.sem("y_done")
        x_stored, xT_stored = [s.sem(f"x_stored{b}") for b in range(2)], s.sem("xT_stored")
        turned, xT_copied = s.sem("turned"), s.sem("xT_copied")
        dve_holds, pool_holds = s.sem("dve_holds"), s.sem("pool_holds")
        block = ctx.enter_context(nc.Block())
        LAST = TILES // 2 - 1

        @block.sync
        def _(sp):
            sp.dma_start(g_all[:], gain.partition_broadcast(P)).then_inc(small_loaded, 16)
            sp.dma_start(b_all[:], bias.partition_broadcast(P)).then_inc(small_loaded, 16)
            tp.load(sp, 0, 0)
            tp.load(sp, 0, 1)
            with sp.Fori(1, TILES // 2) as i:
                tp.load(sp, i, 0)
                tp.load(sp, i, 1)

        @block.gpsimd
        def _(pool):
            def load_res(t, b):
                pool.dma_start(y[:, b], res[bass.ds(P * t, P)]).then_inc(res_loaded[b], 16)

            def refill(i, b):
                pool.wait_ge(x_stored[b], 16 * i + 16)
                pool.wait_ge(turned, 2 * i + b + 1)
                hold(pool, pool_holds)
                load_res(2 * i + b + 2, b % 2)

            def finish(i, b):
                t, at = 2 * i + b, b % 2
                pool.wait_ge(normed, t + 1)
                pool.tensor_tensor(y[:, at], y[:, at], g_all[:], ALU.mult).then_inc(gained, 1)
                pool.wait_ge(gained, t + 1)
                pool.tensor_tensor(y[:, at], y[:, at], b_all[:], ALU.add).then_inc(y_done, 1)
                dst = x_out[bass.ds(P * t, P)]
                pool.wait_ge(y_done, t + 1)
                hold(pool, pool_holds)
                pool.dma_start(dst, y[:, at]).then_inc(x_stored[at], 16)

            pool.memset(ident[:], 0.0).then_inc(const_sem, 1)
            pool.wait_ge(const_sem, 1)
            pool.affine_select(out=ident[:], in_=ident[:], compare_op=ALU.not_equal, fill=1.0, base=0, pattern=[[-1, P]],
                               channel_multiplier=1).then_inc(const_sem, 1)
            pool.memset(eps[:], LN_EPS).then_inc(const_sem, 1)
            tp.load_weights(pool)
            pool.wait_ge(tp.w_lo_done, K)
            load_res(0, 0)
            load_res(1, 1)
            pool.wait_ge(small_loaded, 32)
            finish(0, 0)
            with pool.Fori(0, LAST) as i:
                finish(i, 1)
                refill(i, 0)
                finish(i, 2)
                refill(i, 1)
            finish(LAST, 1)
            for b in range(2):
                pool.wait_ge(x_stored[b], 16 * (TILES // 2))

        @block.tensor
        def _(pe):
            def turn(i, b):
                t = 2 * i + b
                pe.wait_ge(y_done, t + 1)
                reached(pe, xT_copied, t)
                for k in range(KD):
                    last = pe.transpose(xT_ps[:, k], y[:, b % 2, P * k:P * (k + 1)], ident[:])
                last.then_inc(turned, 1)

            def tile(i, b):
                tp.product(pe, i, b, added)
                turn(i, b - 1)

            over_tiles(pe.Fori, lambda i, b: tp.product(pe, i, b, added), tile, lambda i, b: turn(i, b - 1))

        @block.scalar
        def _(act):
            def out(i, b):
                t = 2 * i + b
                act.wait_ge(turned, t + 1)
                reached(act, xT_stored, 16 * t)
                act.activation(xT[:], xT_ps[:], ACT.Copy).then_inc(xT_copied, 1)
                dst = xT_out[:, :, bass.ds(P * t, P)].rearrange("a p t -> p a t")
                act.wait_ge(xT_copied, t + 1)
                act.dma_start(dst, xT[:]).then_inc(xT_stored, 16)

            def deviation(i, b):
                act.wait_ge(mean_done, 2 * i + b + 1)
                act.activation(root[:, 0:1], mean[:, 1:2], ACT.Sqrt, bias=eps[:, 0:1]).then_inc(root_done, 1)

            def tile(i, b):
                for c in range(tp.CH):
                    tp.high(act, i, b, c)
                    if c == 1:
                        if b == 2:
                            out(i, 0)
                        elif not (isinstance(i, int) and i == 0):
                            out(i - 1, 1)
                        deviation(i, b - 1)

            act.preload_act_table(ACT.Sqrt)
            act.wait_ge(const_sem, 3)

            over_tiles(act.Fori, lambda i, b: [tp.high(act, i, b, c, True) for c in range(tp.CH)], tile,
                       lambda i, b: [out(i, b - 2), deviation(i, b - 1), out(i, b - 1)])
            act.wait_ge(xT_stored, 16 * TILES)

        @block.vector
        def _(dve):
            def add(i, b):
                at = b % 2
                tp.product_done(dve, i, b)
                dve.wait_ge(res_loaded[at], 16 * i + 16 * (b // 2) + 16)
                dve.scalar_tensor_tensor(y[:, at], y[:, at], ALPHA, acc[:, at], ALU.mult, ALU.add).then_inc(added, 1)

            def norm(i, b):
                t, at = 2 * i + b, b % 2
                dve.wait_ge(added, t + 1)
                for half in range(2):
                    dve.bn_stats(stats[:, half], y[:, at, NTOK * half:NTOK * (half + 1)]).then_inc(stats_done, 1)
                dve.wait_ge(stats_done, 2 * t + 2)
                hold(dve, dve_holds)
                dve.bn_aggr(mean[:], stats[:].rearrange("p a c -> p (a c)")).then_inc(mean_done, 1)
                dve.wait_ge(root_done, t + 1)
                dve.tensor_scalar(mean[:, 1:2], mean[:, 1:2], LN_EPS, -0.5, ALU.add, ALU.mult).then_inc(newton, 1)
                dve.reciprocal(root[:, 1:2], root[:, 0:1]).then_inc(newton, 1)
                dve.wait_ge(newton, 4 * t + 2)
                dve.scalar_tensor_tensor(root[:, 2:3], root[:, 1:2], mean[:, 1:2], root[:, 1:2], ALU.mult, ALU.mult).then_inc(newton, 1)
                dve.wait_ge(newton, 4 * t + 3)
                dve.scalar_tensor_tensor(rstd, root[:, 2:3], 1.5, root[:, 1:2], ALU.add, ALU.mult).then_inc(newton, 1)
                dve.wait_ge(newton, 4 * t + 4)
                dve.tensor_scalar(y[:, at], y[:, at], mean[:, 0:1], rstd, ALU.subtract, ALU.mult).then_inc(normed, 1)

            def tile(i, b):
                for c in range(tp.CH):
                    tp.low(dve, i, b, c)
                    if c == 0:
                        add(i, b - 1)
                    if c == 1:
                        norm(i, b - 1)

            over_tiles(dve.Fori, lambda i, b: [tp.low(dve, i, b, c, True) for c in range(tp.CH)], tile,
                       lambda i, b: [add(i, b - 1), norm(i, b - 1)])


def embed(nc, lhs, weights, x, out):
    K = KD + PLE_DIM // P
    with ExitStack() as ctx:
        s = Scope(nc, ctx, "em")
        w_raw = s.sb("w_raw", [P, 2, D_MODEL])
        xt = s.sb("xt", [P, 2, D_MODEL])
        y = s.sb("y", [P, 2, D_MODEL])
        gate_ps = s.ps("gate_ps", [P, 2, D_MODEL])
        ple_ps = s.ps("ple_ps", [P, 2, D_MODEL])
        tp = TokenProduct(nc, s, K, lhs, weights, w_raw, [(0, KD - 1, gate_ps), (KD, K - 1, ple_ps)])
        x_loaded = [s.sem(f"x_loaded{b}") for b in range(2)]
        gate_done = s.sem("gate_done")
        gated = s.sem("gated")
        summed = s.sem("summed")
        pool_holds = s.sem("pool_holds")
        stored = [s.sem(f"stored{b}") for b in range(2)]
        block = ctx.enter_context(nc.Block())

        @block.sync
        def _(sp):
            tp.load(sp, 0, 0)
            tp.load(sp, 0, 1)
            with sp.Fori(1, TILES // 2) as i:
                tp.load(sp, i, 0)
                tp.load(sp, i, 1)

        @block.gpsimd
        def _(pool):
            def load_x(t, b):
                pool.dma_start(xt[:, b], x[bass.ds(P * t, P)]).then_inc(x_loaded[b], 16)

            def finish(i, b, more):
                t = 2 * i + b
                pool.wait_ge(x_loaded[b], 16 * i + 16)
                pool.wait_ge(gated, t + 1)
                pool.tensor_tensor(y[:, b], y[:, b], xt[:, b], ALU.add).then_inc(summed, 1)
                dst = out[bass.ds(P * t, P)]
                pool.wait_ge(summed, t + 1)
                hold(pool, pool_holds)
                pool.dma_start(dst, y[:, b]).then_inc(stored[b], 16)
                if more:
                    load_x(t + 2, b)

            tp.load_weights(pool)
            load_x(0, 0)
            load_x(1, 1)
            with pool.Fori(0, TILES // 2 - 1) as i:
                finish(i, 0, True)
                finish(i, 1, True)
            for b in range(2):
                finish(TILES // 2 - 1, b, False)
            for b in range(2):
                pool.wait_ge(stored[b], 16 * (TILES // 2))

        @block.tensor
        def _(pe):
            product = lambda i, b: tp.product(pe, i, b, gated)
            over_tiles(pe.Fori, product, product, lambda i, b: None)

        @block.scalar
        def _(act):
            def gate(i, b):
                at = b % 2
                tp.product_done(act, i, b)
                reached(act, stored[at], 16 * i + 16 * (b // 2))
                act.activation(y[:, at], gate_ps[:, at], ACT.Sigmoid).then_inc(gate_done, 1)

            def tile(i, b):
                for c in range(tp.CH):
                    tp.high(act, i, b, c)
                    if c == 1:
                        gate(i, b - 1)

            act.preload_act_table(ACT.Sigmoid)
            over_tiles(act.Fori, lambda i, b: [tp.high(act, i, b, c, True) for c in range(tp.CH)], tile,
                       lambda i, b: gate(i, b - 1))

        @block.vector
        def _(dve):
            def multiply(i, b):
                at = b % 2
                dve.wait_ge(gate_done, 2 * i + b + 1)
                dve.tensor_tensor(y[:, at], y[:, at], ple_ps[:, at], ALU.mult).then_inc(gated, 1)

            def tile(i, b):
                for c in range(tp.CH):
                    tp.low(dve, i, b, c)
                    if c == 1:
                        multiply(i, b - 1)

            over_tiles(dve.Fori, lambda i, b: [tp.low(dve, i, b, c, True) for c in range(tp.CH)], tile,
                       lambda i, b: multiply(i, b - 1))


def lay_in(x, w_in, conv_w):
    xT = np.ascontiguousarray(x[0].T.reshape(KD, P, SEQ).transpose(1, 0, 2))
    w = w_in[0]
    cuts = np.cumsum([4 * HEADS * P, HEADS, HEADS, Q_LORA, KV_LORA, ROPE])
    qkvz, b, a, cq, ckv, kr = np.split(w, cuts[:-1], axis=1)
    pad = np.zeros((D_MODEL, N_IN * P - w.shape[1]), w.dtype)
    w = np.concatenate([qkvz, cq, ckv, kr, b, a, pad], axis=1)
    w = w.reshape(KD, P, N_IN, P).transpose(2, 1, 0, 3).reshape(N_IN, P, KD * P)
    taps = conv_w[0].T.reshape(T_Z, P, CONV_WIDTH).transpose(1, 0, 2).reshape(P, T_Z * CONV_WIDTH)
    return xT, np.ascontiguousarray(w), np.ascontiguousarray(taps)


def lay_latents(w_uq, w_ukv, q_norm_g, kv_norm_g):
    uq = w_uq[0].reshape(KQ, P, HEADS, P + ROPE)
    uq = np.concatenate([uq[..., P:].reshape(KQ, P, -1), uq[..., :P].reshape(KQ, P, -1)], axis=2)
    ukv = w_ukv[0].reshape(KC, P, HEADS, 2, P).transpose(0, 1, 3, 2, 4).reshape(KC, P, -1)
    gains = np.concatenate([q_norm_g[0].reshape(KQ, P), kv_norm_g[0].reshape(KC, P)]).T
    return (np.ascontiguousarray(uq.transpose(1, 0, 2)), np.ascontiguousarray(ukv.transpose(1, 0, 2)),
            np.ascontiguousarray(gains))


def rotary_frequencies():
    f = ROPE_THETA ** (-np.arange(0, ROPE, 2) / ROPE)
    return np.tile(f.astype(np.float32), P // (ROPE // 2)).reshape(P, 1)


def lay_tail(w_gate_up, w_ple_gate, w_ple, p):
    gu = w_gate_up[0].reshape(KD, P, 2, FT, P).transpose(3, 2, 1, 0, 4).reshape(2 * FT, P, KD * P)
    ple = np.concatenate([w_ple_gate[0], w_ple[0]]).reshape(-1, P, D_MODEL)
    pT = p[0, 0].T.reshape(PLE_DIM // P, P, SEQ)
    return np.ascontiguousarray(gu), np.ascontiguousarray(ple), np.ascontiguousarray(pT)


def tokens_of(xT):
    return lambda t, k: xT[k:k + 2, :, bass.ds(P * t, P)].rearrange("a p t -> p a t")


def build(nc, a, out):
    def scratch(name, shape, dt=F32):
        return nc.dram_tensor(f"scratch_{name}", shape, dt, kind="Internal").ap()

    hT = scratch("hT", [N_IN, P, SEQ])
    shapes = {"qnT": [HEADS, P, SEQ], "qrT": [HEADS, ROPE, SEQ], "knT": [HEADS, P, SEQ], "krT": [ROPE, SEQ],
              "v": [TILES, P, HEADS * P]}
    made = {n + half: scratch(n + half, shape, F32R) for n, shape in shapes.items() for half in ("_hi", "_lo")}
    mixT = scratch("mixT", [2 * HEADS, P, SEQ])
    x1, x1T = scratch("x1", [SEQ, D_MODEL]), scratch("x1T", [KD, P, SEQ])
    hid = scratch("hid", [TILES, P, FT, P])
    x2, x2T = scratch("x2", [SEQ, D_MODEL]), scratch("x2T", [KD, P, SEQ])

    project_in(nc, a["xT"], a["w_in"], a["taps"], hT)
    latents(nc, hT, a["positions"][0], a["inv_freq"], a["w_uq"], a["w_ukv"], a["gains"], made)
    delta_rule(nc, hT, a["a_log"][0], a["dt_bias"][0], a["gdn_norm_g"], mixT)
    attention(nc, made, mixT)
    project_norm(nc, "op", KD, tokens_of(mixT), a["w_out"], a["x"], a["ln1_g"][0], a["ln1_b"][0], x1, x1T)
    feed_in(nc, x1T, a["w_gate_up"], hid)
    hidden = lambda t, k: hid[bass.ds(t, 1), :, k:k + 2, :].rearrange("x p a c -> p (x a) c")
    project_norm(nc, "fd", FT, hidden, a["w_down"], x1, a["ln2_g"][0], a["ln2_b"][0], x2, x2T)
    from_x, from_p = tokens_of(x2T), tokens_of(a["pT"])
    embed(nc, lambda t, k: from_x(t, k) if k < KD else from_p(t, k - KD), a["w_ple"], x2, out)


def lay_all(i):
    xT, w_in, taps = lay_in(i["x"], i["w_in"], i["conv_w"])
    uq, ukv, gains = lay_latents(i["w_uq"], i["w_ukv"], i["q_norm_g"], i["kv_norm_g"])
    gate_up, ple, pT = lay_tail(i["w_gate_up"], i["w_ple_gate"], i["w_ple"], i["p"])
    return {
        "x": i["x"][0], "xT": xT, "w_in": w_in, "taps": taps,
        "positions": i["positions"], "inv_freq": rotary_frequencies(), "w_uq": uq, "w_ukv": ukv, "gains": gains,
        "a_log": i["a_log"], "dt_bias": i["dt_bias"], "gdn_norm_g": i["gdn_norm_g"].reshape(P, 1),
        "w_out": i["w_out"][0].reshape(KD, P, D_MODEL), "ln1_g": i["ln1_g"], "ln1_b": i["ln1_b"],
        "w_gate_up": gate_up, "w_down": i["w_down"][0].reshape(FT, P, D_MODEL), "ln2_g": i["ln2_g"], "ln2_b": i["ln2_b"],
        "w_ple": ple, "pT": pT,
    }


def kernel(**inputs):
    import concourse.bacc as bacc
    from concourse.bass_utils import run_bass_kernel_spmd

    nc = bacc.Bacc("TRN2", target_bir_lowering=False, num_devices=1)
    arrays = {n: np.ascontiguousarray(v) for n, v in lay_all({n: np.asarray(v) for n, v in inputs.items()}).items()}
    a = {n: nc.dram_tensor(n, v.shape, mybir.dt.from_np(v.dtype), kind="ExternalInput").ap() for n, v in arrays.items()}
    out = nc.dram_tensor("out", [SEQ, D_MODEL], F32, kind="ExternalOutput").ap()
    build(nc, a, out)
    r = run_bass_kernel_spmd(nc, [arrays], core_ids=[0])
    return r.results[0]["out"].reshape(1, SEQ, D_MODEL)
```

```python
from contextlib import ExitStack

import numpy as np

import concourse.bass as bass
from concourse import mybir

F32 = mybir.dt.float32
F32R = mybir.dt.float32r
I32 = mybir.dt.int32
ACT = mybir.ActivationFunctionType
ALU = mybir.AluOpType
AX = mybir.AxisListType

P = 128
D_MODEL = 1024
SEQ = 2048
CHUNK = 64
PLE_DIM = 256
HEADS = 4
ROPE = 64
Q_LORA = 384
KV_LORA = 256
D_FF = 2816
CONV_WIDTH = 4
ROPE_THETA = 10000.0
ALPHA = 2.0 ** 0.25
LN_EPS = 1e-5
RMS_EPS = 1e-6
NTOK = 512
BLOCKS = SEQ // NTOK
TILES = SEQ // P
KD = D_MODEL // P
KQ = Q_LORA // P
KC = KV_LORA // P
FT = D_FF // P
T_Q, T_K, T_V, T_Z = 0, HEADS, 2 * HEADS, 3 * HEADS
T_CQ = 4 * HEADS
T_CKV = T_CQ + KQ
T_KR = T_CKV + KC
N_IN = T_KR + 1


class Scope:

    def __init__(self, nc, ctx, stage):
        self.nc, self.ctx, self.stage, self.sems = nc, ctx, stage, []
        ctx.callback(self.clear)

    def sb(self, name, shape, dt=F32):
        return self.ctx.enter_context(self.nc.sbuf_tensor(f"{self.stage}_{name}", shape, dt))

    def ps(self, name, shape):
        return self.ctx.enter_context(self.nc.psum_tensor(f"{self.stage}_{name}", shape, F32))

    def sem(self, name):
        self.sems.append(self.nc.alloc_semaphore(f"{self.stage}_{name}"))
        return self.sems[-1]

    def clear(self):
        self.nc.clear_and_free_semaphores(self.sems)
        self.nc.all_engine_barrier()


def reached(eng, sem, count):
    if not (isinstance(count, int) and count <= 0):
        eng.wait_ge(sem, count)


def project_in(nc, xT, w_in, conv_w, hT):
    with ExitStack() as ctx:
        s = Scope(nc, ctx, "in")
        x_raw = s.sb("x_raw", [P, 2, SEQ])
        x_hi = s.sb("x_hi", [P, KD, SEQ], F32R)
        x_lo = s.sb("x_lo", [P, KD, SEQ], F32R)
        w_raw = s.sb("w_raw", [P, 2, KD * P])
        w_hi = s.sb("w_hi", [P, 2, KD * P], F32R)
        w_lo = s.sb("w_lo", [P, 2, KD * P], F32R)
        taps = s.sb("taps", [P, T_Z * CONV_WIDTH])
        h_pad = s.sb("h_pad", [P, SEQ + CONV_WIDTH - 1])
        zero = s.sb("zero", [P, 1])
        conv = s.sb("conv", [P, SEQ])
        out = s.sb("out", [P, SEQ])
        h_ps = s.ps("h_ps", [P, 2, BLOCKS, NTOK])

        x_loaded = [s.sem(f"x_loaded{b}") for b in range(2)]
        x_hi_done = s.sem("x_hi_done")
        x_lo_done = s.sem("x_lo_done")
        w_loaded = [s.sem(f"w_loaded{b}") for b in range(2)]
        w_hi_done = s.sem("w_hi_done")
        w_lo_done = s.sem("w_lo_done")
        taps_loaded = s.sem("taps_loaded")
        h_made = s.sem("h_made")
        h_ps_free = s.sem("h_ps_free")
        zeroed = s.sem("zeroed")
        h_copied = s.sem("h_copied")
        conv_step = s.sem("conv_step")
        conv_free = s.sem("conv_free")
        out_made = s.sem("out_made")
        out_free = s.sem("out_free")
        stored = s.sem("stored")
        block = ctx.enter_context(nc.Block())

        @block.sync
        def _(sp):
            sp.dma_start(taps[:, :], conv_w).then_inc(taps_loaded, 16)
            for k in range(KD):
                if k >= 2:
                    sp.wait_ge(x_lo_done, k - 1)
                sp.dma_start(x_raw[:, k % 2, :], xT[:, k, :]).then_inc(x_loaded[k % 2], 16)
            sp.sem_inc(out_free, 1)
            with sp.Fori(0, N_IN) as m:
                sp.wait_ge(out_made, m + 1)
                sp.dma_start(hT[bass.ds(m, 1)].rearrange("a p t -> p (a t)"), out[:, :]).then_inc(stored, 16)
                sp.wait_ge(stored, 16 * m + 16)
                sp.sem_inc(out_free, 1)

        @block.gpsimd
        def _(pool):
            def load(m, b):
                pool.dma_start(w_raw[:, b, :], w_in[bass.ds(m, 1)].rearrange("a p f -> p (a f)")).then_inc(w_loaded[b], 16)

            def split(i, b):
                m = 2 * i + b
                pool.wait_ge(w_loaded[b], 16 * i + 16)
                pool.wait_ge(h_ps_free, m + 1)
                pool.tensor_tensor(w_hi[:, b, :], w_raw[:, b, :], zero[:, 0:1].broadcast_to([P, KD * P]),
                                   ALU.add).then_inc(w_hi_done, 1)
                pool.wait_ge(w_hi_done, m + 1)
                pool.tensor_tensor(w_lo[:, b, :], w_raw[:, b, :], w_hi[:, b, :].bitcast(F32),
                                   ALU.subtract).then_inc(w_lo_done, 1)

            pool.memset(zero[:, :], 0.0).then_inc(zeroed, 1)
            pool.wait_ge(zeroed, 1)
            load(0, 0)
            load(1, 1)
            with pool.Fori(0, N_IN // 2 - 1) as i:
                for b in range(2):
                    split(i, b)
                    pool.wait_ge(w_lo_done, 2 * i + b + 1)
                    load(2 * i + b + 2, b)
            for b in range(2):
                split(N_IN // 2 - 1, b)

        @block.tensor
        def _(pe):
            with pe.Fori(0, N_IN // 2) as i:
                for b in range(2):
                    m = 2 * i + b
                    pe.wait_ge(w_lo_done, m + 1)
                    pe.wait_ge(h_ps_free, m + 1)
                    for k in range(KD):
                        pe.wait_ge(x_lo_done, k + 1)
                        ws = slice(k * P, (k + 1) * P)
                        for t in range(BLOCKS):
                            ts = slice(t * NTOK, (t + 1) * NTOK)
                            acc = h_ps[:, b, t, :]
                            pe.matmul(acc, w_lo[:, b, ws], x_hi[:, k, ts], start=(k == 0), stop=False)
                            pe.matmul(acc, w_hi[:, b, ws], x_lo[:, k, ts], start=False, stop=False)
                            last = pe.matmul(acc, w_hi[:, b, ws], x_hi[:, k, ts], start=False, stop=(k == KD - 1))
                    last.then_inc(h_made, 1)

        @block.scalar
        def _(act):
            act.sem_inc(h_ps_free, 2)
            act.sem_inc(conv_free, 1)
            for k in range(KD):
                act.wait_ge(x_loaded[k % 2], 16 * (k // 2 + 1))
                act.activation(x_hi[:, k, :], x_raw[:, k % 2, :], ACT.Copy).then_inc(x_hi_done, 1)

            def conv_tile(i, b):
                m = 2 * i + b
                act.wait_ge(h_made, m + 1)
                act.wait_ge(conv_step, CONV_WIDTH * m + 1)
                act.activation(h_pad[:, CONV_WIDTH - 1:], h_ps[:, b].rearrange("p a t -> p (a t)"),
                               ACT.Copy).then_inc(h_copied, 1)
                act.wait_ge(h_copied, m + 1)
                act.sem_inc(h_ps_free, 1)
                act.wait_ge(conv_step, CONV_WIDTH * (m + 1) + 1)
                act.wait_ge(out_free, m + 1)
                act.activation(out[:, :], conv[:, :], ACT.Silu).then_inc(out_made, 1)
                act.wait_ge(out_made, m + 1)
                act.sem_inc(conv_free, 1)

            def plain_tile(i, b, func):
                m = 2 * i + b
                act.wait_ge(h_made, m + 1)
                act.wait_ge(out_free, m + 1)
                act.activation(out[:, :], h_ps[:, b].rearrange("p a t -> p (a t)"), func).then_inc(out_made, 1)
                act.wait_ge(out_made, m + 1)
                act.sem_inc(h_ps_free, 1)

            act.preload_act_table(ACT.Silu)
            for first, last, tile in ((0, T_Z, conv_tile),
                                      (T_Z, T_CQ, lambda i, b: plain_tile(i, b, ACT.Silu)),
                                      (T_CQ, N_IN, lambda i, b: plain_tile(i, b, ACT.Copy))):
                with act.Fori(first // 2, last // 2) as i:
                    for b in range(2):
                        tile(i, b)

        @block.vector
        def _(dve):
            for k in range(KD):
                dve.wait_ge(x_hi_done, k + 1)
                dve.tensor_tensor(x_lo[:, k, :], x_raw[:, k % 2, :], x_hi[:, k, :].bitcast(F32),
                                  ALU.subtract).then_inc(x_lo_done, 1)
            dve.wait_ge(taps_loaded, 16)
            dve.memset(h_pad[:, 0:CONV_WIDTH - 1], 0.0).then_inc(conv_step, 1)
            with dve.Fori(0, T_Z // 2) as i:
                for b in range(2):
                    m = 2 * i + b
                    dve.wait_ge(h_copied, m + 1)
                    for j in range(CONV_WIDTH):
                        if j == 0:
                            dve.wait_ge(conv_free, m + 1)
                            op = dve.tensor_scalar(conv[:, :], h_pad[:, 0:SEQ], taps[:, bass.ds(CONV_WIDTH * m, 1)], None, ALU.mult)
                        else:
                            dve.wait_ge(conv_step, CONV_WIDTH * m + j + 1)
                            op = dve.scalar_tensor_tensor(conv[:, :], h_pad[:, j:j + SEQ], taps[:, bass.ds(CONV_WIDTH * m + j, 1)],
                                                          conv[:, :], ALU.mult, ALU.add)
                        op.then_inc(conv_step, 1)


def split_resident(s, act, dve, name, raw, hi, lo, loaded):
    hi_done, lo_done = s.sem(f"{name}_hi_done"), s.sem(f"{name}_lo_done")

    def on_scalar():
        act.wait_ge(loaded, 16)
        act.activation(hi, raw, ACT.Copy).then_inc(hi_done, 1)

    def on_vector():
        dve.wait_ge(hi_done, 1)
        dve.tensor_tensor(lo, raw, hi.bitcast(F32), ALU.subtract).then_inc(lo_done, 1)

    return on_scalar, on_vector, lo_done


def latents(nc, hT, positions, inv_freq, w_uq, w_ukv, gains, made):
    NG = 14
    SCALE = float(P + ROPE) ** -0.5
    parts = [{n: made[n + half].bitcast(F32) for n in ("qnT", "qrT", "knT", "krT", "v")} for half in ("_hi", "_lo")]
    G_QN, G_KN, G_V = 2, 6, 10
    RING = 5
    MAGIC = 1.5 * 2.0 ** 23
    TWO_PI_1 = 6.28125
    TWO_PI_2 = float(np.float32(0.00193500518798828125))
    TWO_PI_3 = float(np.float32(2 * np.pi - TWO_PI_1 - TWO_PI_2))
    PI_IN = 3.1415925
    with ExitStack() as ctx:
        s = Scope(nc, ctx, "lat")
        NQ = 2 * P + HEADS * P
        NKV = 2 * HEADS * P
        uq_hi = s.sb("uq_hi", [P, KQ, NQ], F32R)
        uq_lo = s.sb("uq_lo", [P, KQ, NQ], F32R)
        ukv_hi = s.sb("ukv_hi", [P, KC, NKV], F32R)
        ukv_lo = s.sb("ukv_lo", [P, KC, NKV], F32R)
        gain = s.sb("gain", [P, KQ + KC])
        freq = s.sb("freq", [P, 1])
        ones = s.sb("ones", [P, P])
        half_pi = s.sb("half_pi", [P, 1])
        eps = s.sb("eps", [P, 1])
        turn = s.sb("turn", [P, P])
        cos = s.sb("cos", [P, SEQ])
        pos = cos[:].bitcast(I32)
        ang, turns, turns_hi, part = (s.sb(n, [P, NTOK]) for n in ("ang", "turns", "turns_hi", "part"))
        sin = s.sb("sin", [P, SEQ])
        lat = s.sb("lat", [P, 2, KQ + KC, NTOK])
        kr = s.sb("kr", [ROPE, 2, NTOK])
        sq = s.sb("sq", [P, KQ + KC, NTOK])
        rstd = s.sb("rstd", [P, 2, NTOK])
        nrm_hi = s.sb("nrm_hi", [P, 2, KQ + KC, NTOK], F32R)
        nrm_lo = s.sb("nrm_lo", [P, 2, KQ + KC, NTOK], F32R)
        raw_r = s.sb("raw_r", [P, 2, NTOK])
        out_hi = s.sb("out_hi", [P, NG - 2, NTOK], F32R)
        out_lo = s.sb("out_lo", [P, NG - 2, NTOK], F32R)
        flat_lo = out_lo[:].rearrange("p a t -> p (a t)").bitcast(F32)
        var, step_rs = sq[:, 0:2], sq[:, 2:4]
        uq_raw = flat_lo[:, 0:KQ * NQ].rearrange("p (k n) -> p k n", k=KQ)
        ukv_raw = flat_lo[:, KQ * NQ:KQ * NQ + KC * NKV].rearrange("p (k n) -> p k n", k=KC)
        rot_hi = s.sb("rot_hi", [P, 3, NTOK], F32R)
        rot_lo = s.sb("rot_lo", [P, 3, NTOK], F32R)
        rot = s.sb("rot", [P, NTOK])
        swapped = s.sb("swapped", [P, NTOK])
        ssq_ps = s.ps("ssq_ps", [P, 2, NTOK])
        ring = s.ps("ring", [P, RING, NTOK])
        turn_ps = s.ps("turn_ps", [P, NTOK])

        uq_loaded, ukv_loaded = s.sem("uq_loaded"), s.sem("ukv_loaded")
        small_loaded, pos_loaded = s.sem("small_loaded"), s.sem("pos_loaded")
        consts = s.sem("consts")
        table = s.sem("table")
        sin_done, abs_done, cos_done = s.sem("sin_done"), s.sem("abs_done"), s.sem("cos_done")
        lat_loaded = [s.sem(f"lat_loaded{b}") for b in range(2)]
        kr_loaded = [s.sem(f"kr_loaded{b}") for b in range(2)]
        sq_done = s.sem("sq_done")
        ssq_done = s.sem("ssq_done")
        var_done, log_done, root_done, newton = (s.sem(n) for n in ("var_done", "log_done", "root_done", "newton"))
        nrm_done = s.sem("nrm_done")
        nrm_hi_done = s.sem("nrm_hi_done")
        nrm_lo_done = s.sem("nrm_lo_done")
        group_done = s.sem("group_done")
        out_copied = s.sem("out_copied")
        out_lo_done = s.sem("out_lo_done")
        turned = s.sem("turned")
        cos_part = s.sem("cos_part")
        sin_part = s.sem("sin_part")
        rot_done = s.sem("rot_done")
        rot_hi_done, rot_lo_done = s.sem("rot_hi_done"), s.sem("rot_lo_done")
        q_stored, k_stored, v_stored, r_stored = (s.sem(n) for n in ("q_stored", "k_stored", "v_stored", "r_stored"))
        block = ctx.enter_context(nc.Block())
        tok = [slice(t * NTOK, (t + 1) * NTOK) for t in range(BLOCKS)]
        STEPS = 19
        ROTATE = (8, 10, 12)
        BANKS = NG - 2

        uq_act, uq_dve, uq_ready = split_resident(s, nc.scalar, nc.vector, "uq", uq_raw, uq_hi[:], uq_lo[:], uq_loaded)
        ukv_act, ukv_dve, ukv_ready = split_resident(s, nc.scalar, nc.vector, "ukv", ukv_raw, ukv_hi[:], ukv_lo[:], ukv_loaded)

        @block.sync
        def _(sp):
            def load(t):
                if t >= 2:
                    sp.wait_ge(nrm_lo_done, t - 1)
                sp.dma_start(lat[:, t % 2], hT[T_CQ:T_KR, :, tok[t]].rearrange("a p t -> p a t")).then_inc(lat_loaded[t % 2], 16)

            def load_kr(t):
                if t >= 2:
                    sp.wait_ge(rot_done, 3 * (t - 1))
                sp.dma_start(kr[:, t % 2], hT[T_KR, 0:ROPE, tok[t]]).then_inc(kr_loaded[t % 2], 16)

            load(0)
            sp.dma_start(gain[:], gains).then_inc(small_loaded, 16)
            sp.dma_start(freq[:], inv_freq).then_inc(small_loaded, 16)
            sp.dma_start(pos, positions.partition_broadcast(P)).then_inc(pos_loaded, 16)
            sp.dma_start(uq_raw, w_uq).then_inc(uq_loaded, 16)
            sp.dma_start(ukv_raw, w_ukv).then_inc(ukv_loaded, 16)
            load(1)
            load_kr(0)
            load_kr(1)
            for t in range(BLOCKS):
                if t + 2 < BLOCKS:
                    load(t + 2)
                for g0, name, sem in ((0, "qnT", q_stored), (4, "knT", k_stored), (8, "v", v_stored)):
                    sp.wait_ge(out_lo_done, BANKS * t + g0 + 4)
                    for part, src in zip(parts, (out_hi[:].bitcast(F32), out_lo[:].bitcast(F32))):
                        if name == "v":
                            dst = part["v"][4 * t:4 * t + 4].rearrange("a p n -> p a n")
                        else:
                            dst = part[name][:, :, tok[t]].rearrange("h p t -> p h t")
                        sp.dma_start(dst, src[:, g0:g0 + 4]).then_inc(sem, 16)
                sp.wait_ge(rot_lo_done, 3 * (t + 1))
                for part, src in zip(parts, (rot_hi[:].bitcast(F32), rot_lo[:].bitcast(F32))):
                    for g in range(2):
                        sp.dma_start(part["qrT"][2 * g:2 * g + 2, :, tok[t]].rearrange("h p t -> (h p) t"), src[:, g]).then_inc(r_stored, 16)
                    sp.dma_start(part["krT"][:, tok[t]], src[0:ROPE, 2]).then_inc(r_stored, 16)
                if t + 2 < BLOCKS:
                    load_kr(t + 2)
            for sem in (q_stored, k_stored, v_stored):
                sp.wait_ge(sem, 32 * BLOCKS)
            sp.wait_ge(r_stored, 96 * BLOCKS)

        @block.gpsimd
        def _(pool):
            pool.memset(ones[:], 1.0).then_inc(consts, 1)
            pool.memset(half_pi[:], float(np.pi / 2)).then_inc(consts, 1)
            pool.memset(eps[:], RMS_EPS).then_inc(consts, 1)
            pool.memset(turn[:], 0.0).then_inc(consts, 1)
            pool.wait_ge(consts, 4)
            for n, half in enumerate(range(0, P, ROPE)):
                view = turn[:, half:half + ROPE // 2]
                pool.affine_select(out=view, in_=view, compare_op=ALU.not_equal, fill=-1.0, base=-half - ROPE // 2,
                                   pattern=[[-1, ROPE // 2]], channel_multiplier=1).then_inc(consts, 1)
                view = turn[:, half + ROPE // 2:half + ROPE]
                pool.affine_select(out=view, in_=view, compare_op=ALU.not_equal, fill=1.0, base=-half,
                                   pattern=[[-1, ROPE // 2]], channel_multiplier=1).then_inc(consts, 1)

            pool.wait_ge(small_loaded, 32)
            pool.wait_ge(pos_loaded, 16)
            for t in range(BLOCKS):
                steps = [
                    lambda: pool.tensor_copy(ang[:], pos[:, tok[t]]),
                    lambda: pool.tensor_scalar(ang[:], ang[:], freq[:, 0:1], None, ALU.mult),
                    lambda: pool.tensor_scalar(turns[:], ang[:], float(1 / (2 * np.pi)), MAGIC, ALU.mult, ALU.add),
                    lambda: pool.tensor_scalar(turns[:], turns[:], -MAGIC, None, ALU.add),
                    lambda: pool.tensor_scalar(turns_hi[:], turns[:], 2048 * MAGIC, -2048 * MAGIC, ALU.add, ALU.add),
                    lambda: pool.tensor_tensor(turns[:], turns[:], turns_hi[:], ALU.subtract),
                ]
                for value in (TWO_PI_1, TWO_PI_2, TWO_PI_3):
                    for whole in (turns_hi, turns):
                        steps.append(lambda value=value, whole=whole: pool.tensor_scalar(part[:], whole[:], value, None, ALU.mult))
                        steps.append(lambda: pool.tensor_tensor(ang[:], ang[:], part[:], ALU.subtract))
                steps.append(lambda: pool.tensor_scalar(ang[:], ang[:], PI_IN, -PI_IN, ALU.min, ALU.max))
                assert len(steps) == STEPS
                if t:
                    pool.wait_ge(cos_done, t)
                for n, step in enumerate(steps):
                    if n:
                        pool.wait_ge(table, STEPS * t + n)
                    step().then_inc(table, 1)

        @block.tensor
        def _(pe):
            def sums(t):
                pe.wait_ge(sq_done, t + 1)
                pe.wait_ge(consts, 8)
                if t:
                    pe.wait_ge(var_done, 2 * t)
                for c, (k0, k1) in enumerate(((0, KQ), (KQ, KQ + KC))):
                    for k in range(k0, k1):
                        last = pe.matmul(ssq_ps[:, c], ones[:], sq[:, k], start=(k == k0), stop=(k == k1 - 1))
                last.then_inc(ssq_done, 1)

            def group(t, g):
                b, n = t % 2, NG * t + g
                if n >= RING:
                    pe.wait_ge(out_copied, n - RING + 1)
                    lows = BANKS * ((n - RING) // NG) + max((n - RING) % NG - 1, 0)
                    if lows:
                        pe.wait_ge(out_lo_done, lows)
                acc = ring[:, n % RING]
                if g < G_KN:
                    cols, ks, k0 = slice(g * P, (g + 1) * P), range(KQ), 0
                    whi, wlo = uq_hi, uq_lo
                else:
                    cols, ks, k0 = slice((g - G_KN) * P, (g - G_KN + 1) * P), range(KC), KQ
                    whi, wlo = ukv_hi, ukv_lo
                for k in ks:
                    if g < G_V:
                        ops = [(wlo[:, k, cols], nrm_hi[:, b, k0 + k]), (whi[:, k, cols], nrm_lo[:, b, k0 + k]),
                               (whi[:, k, cols], nrm_hi[:, b, k0 + k])]
                    else:
                        ts, vs = slice((g - G_V) * P, (g - G_V + 1) * P), slice(HEADS * P, NKV)
                        ops = [(nrm_lo[:, b, k0 + k, ts], whi[:, k, vs]), (nrm_hi[:, b, k0 + k, ts], wlo[:, k, vs]),
                               (nrm_hi[:, b, k0 + k, ts], whi[:, k, vs])]
                    for n, (stay, move) in enumerate(ops):
                        last = pe.matmul(acc, stay, move, start=(k == 0 and n == 0), stop=(k == ks[-1] and n == 2))
                last.then_inc(group_done, 1)

            def swap(t, g):
                if 3 * t + g:
                    pe.wait_ge(sin_part, 3 * t + g)
                rows = P if g < 2 else ROPE
                if g < 2:
                    pe.wait_ge(out_copied, NG * t + g + 1)
                else:
                    pe.wait_ge(kr_loaded[t % 2], 16 * (t // 2 + 1))
                src = raw_r[:, g] if g < 2 else kr[:, t % 2]
                pe.matmul(turn_ps[0:rows], turn[0:rows, 0:rows], src, start=True, stop=True).then_inc(turned, 1)

            sums(0)
            pe.wait_ge(uq_ready, 1)
            pe.wait_ge(ukv_ready, 1)
            for t in range(BLOCKS):
                pe.wait_ge(nrm_lo_done, t + 1)
                for g in range(NG):
                    group(t, g)
                    if g == 3 and t + 1 < BLOCKS:
                        sums(t + 1)
                    if g + 1 in ROTATE:
                        swap(t, ROTATE.index(g + 1))

        @block.scalar
        def _(act):
            def squares(t):
                act.wait_ge(lat_loaded[t % 2], 16 * (t // 2 + 1))
                if t:
                    act.wait_ge(newton, 3 * t)
                act.activation(sq[:], lat[:, t % 2], ACT.Square).then_inc(sq_done, 1)

            def roots(t):
                act.wait_ge(ssq_done, t + 1)
                if t:
                    act.wait_ge(nrm_done, (KQ + KC) * t)
                for c, width in enumerate((Q_LORA, KV_LORA)):
                    act.activation(var[:, c], ssq_ps[:, c], ACT.Identity, scale=1.0 / width, bias=eps[:, 0:1]).then_inc(var_done, 1)
                act.wait_ge(var_done, 2 * t + 2)
                act.preload_act_table_set("natural_log_exp_and_others")
                act.activation(rstd[:], var, ACT.Ln).then_inc(log_done, 1)
                act.wait_ge(log_done, t + 1)
                act.activation(rstd[:], rstd[:], ACT.Exp, scale=-0.5).then_inc(root_done, 1)

            def angles(t):
                act.wait_ge(table, STEPS * (t + 1))
                act.activation(sin[:, tok[t]], ang[:], ACT.Sin).then_inc(sin_done, 1)
                act.activation(cos[:, tok[t]], ang[:], ACT.Abs).then_inc(abs_done, 1)
                act.wait_ge(abs_done, t + 1)
                act.activation(cos[:, tok[t]], cos[:, tok[t]], ACT.Sin, scale=-1.0, bias=half_pi[:, 0:1]).then_inc(cos_done, 1)

            def high(t):
                act.wait_ge(nrm_done, (KQ + KC) * (t + 1))
                if t >= 2:
                    act.wait_ge(group_done, NG * (t - 1))
                act.activation(nrm_hi[:, t % 2], lat[:, t % 2], ACT.Copy).then_inc(nrm_hi_done, 1)

            act.wait_ge(consts, 8)
            squares(0)
            uq_act()
            ukv_act()
            roots(0)
            high(0)
            angles(0)
            for t in range(BLOCKS):
                for g in range(NG):
                    n = NG * t + g
                    act.wait_ge(group_done, n + 1)
                    if t and g == 0:
                        act.wait_ge(rot_done, 3 * t)
                    if t and g in (G_QN, G_KN, G_V):
                        sem = {G_QN: q_stored, G_KN: k_stored, G_V: v_stored}[g]
                        act.wait_ge(sem, 32 * t)
                    to = raw_r[:, g] if g < G_QN else out_hi[:, g - G_QN]
                    act.activation(to, ring[:, n % RING], ACT.Copy, scale=SCALE if g < G_KN else 1.0).then_inc(out_copied, 1)
                    if g == 1 and t + 1 < BLOCKS:
                        squares(t + 1)
                    if g == 4 and t + 1 < BLOCKS:
                        roots(t + 1)
                    if g in ROTATE:
                        r = ROTATE.index(g)
                        rows = P if r < 2 else ROPE
                        act.wait_ge(rot_done, 3 * t + r + 1)
                        if t and r == 0:
                            act.wait_ge(r_stored, 96 * t)
                        act.activation(rot_hi[0:rows, r], rot[0:rows], ACT.Copy).then_inc(rot_hi_done, 1)
                    if g == 9 and t + 1 < BLOCKS:
                        high(t + 1)
                    if g == 13 and t + 1 < BLOCKS:
                        angles(t + 1)

        @block.vector
        def _(dve):
            def norm(t):
                b = t % 2
                dve.wait_ge(root_done, t + 1)
                dve.tensor_tensor(step_rs, rstd[:], rstd[:], ALU.mult).then_inc(newton, 1)
                dve.wait_ge(newton, 3 * t + 1)
                dve.scalar_tensor_tensor(step_rs, step_rs, -0.5, var, ALU.mult, ALU.mult).then_inc(newton, 1)
                dve.wait_ge(newton, 3 * t + 2)
                dve.scalar_tensor_tensor(rstd[:], step_rs, 1.5, rstd[:], ALU.add, ALU.mult).then_inc(newton, 1)
                dve.wait_ge(newton, 3 * t + 3)
                for k in range(KQ + KC):
                    dve.scalar_tensor_tensor(lat[:, b, k], lat[:, b, k], gain[:, k:k + 1], rstd[:, int(k >= KQ)],
                                             ALU.mult, ALU.mult).then_inc(nrm_done, 1)

            def low(t):
                dve.wait_ge(nrm_hi_done, t + 1)
                dve.tensor_tensor(nrm_lo[:, t % 2], lat[:, t % 2], nrm_hi[:, t % 2].bitcast(F32), ALU.subtract).then_inc(nrm_lo_done, 1)

            def rotate(t, g):
                rows = P if g < 2 else ROPE
                src = raw_r[:, g] if g < 2 else kr[:, t % 2]
                n = 3 * t + g
                if g < 2:
                    dve.wait_ge(out_copied, NG * t + g + 1)
                else:
                    dve.wait_ge(kr_loaded[t % 2], 16 * (t // 2 + 1))
                dve.wait_ge(cos_done, t + 1)
                if n:
                    dve.wait_ge(rot_lo_done, n)
                dve.tensor_tensor(rot[0:rows], src, cos[0:rows, tok[t]], ALU.mult).then_inc(cos_part, 1)
                dve.wait_ge(turned, n + 1)
                dve.tensor_tensor(swapped[0:rows], turn_ps[0:rows], sin[0:rows, tok[t]], ALU.mult).then_inc(sin_part, 1)
                dve.wait_ge(cos_part, n + 1)
                dve.wait_ge(sin_part, n + 1)
                dve.tensor_tensor(rot[0:rows], rot[0:rows], swapped[0:rows], ALU.add).then_inc(rot_done, 1)

            def rotate_low(t, g):
                rows = P if g < 2 else ROPE
                dve.wait_ge(rot_hi_done, 3 * t + g + 1)
                dve.tensor_tensor(rot_lo[0:rows, g], rot[0:rows], rot_hi[0:rows, g].bitcast(F32), ALU.subtract).then_inc(rot_lo_done, 1)

            def low_out(t, g):
                n = NG * t + g
                dve.wait_ge(out_copied, n + 1)
                dve.scalar_tensor_tensor(out_lo[:, g - G_QN], ring[:, n % RING], SCALE if g < G_KN else 1.0,
                                         out_hi[:, g - G_QN].bitcast(F32), ALU.mult, ALU.subtract).then_inc(out_lo_done, 1)

            uq_dve()
            ukv_dve()
            dve.wait_ge(small_loaded, 32)
            norm(0)
            low(0)
            for t in range(BLOCKS):
                for g in range(G_QN, NG):
                    low_out(t, g)
                    if g + 1 in ROTATE:
                        rotate(t, ROTATE.index(g + 1))
                    if g in ROTATE:
                        rotate_low(t, ROTATE.index(g))
                    if g == 5 and t + 1 < BLOCKS:
                        norm(t + 1)
                    if g == 11 and t + 1 < BLOCKS:
                        low(t + 1)


def delta_rule(nc, hT, a_log, dt_bias, norm_g, mixT):
    LEVELS = (2, 4, 8, 16, 32)
    BETA, GCUM, BETA_G, K_DEC, GATE = range(5)
    with ExitStack() as ctx:
        s = Scope(nc, ctx, "dr")
        qkv = s.sb("qkv", [P, 2, 3 * HEADS, P])
        zT = s.sb("zT", [P, 2, HEADS, P])
        ba_raw = s.sb("ba_raw", [2 * HEADS, SEQ])
        ba = s.sb("ba", [P, TILES, 2 * HEADS])
        bias = s.sb("bias", [P, HEADS])
        rate = s.sb("rate", [P, HEADS])
        gnorm = s.sb("gnorm", [P, 1])
        soft = s.sb("soft", [P, 3, TILES, HEADS])
        scal = s.sb("scal", [P, TILES, 5 * HEADS])
        cur = s.sb("cur", [P, 2, 5, HEADS])
        ident = s.sb("ident", [P, P])
        ones = s.sb("ones", [P, P])
        upto = s.sb("upto", [P, P])
        below = s.sb("below", [P, P])
        chunk = s.sb("chunk", [P, P])
        corner = s.sb("corner", [P, 1 + len(LEVELS), P])
        eps_l2 = s.sb("eps_l2", [P, 1])
        cums = s.sb("cums", [P, HEADS, P])
        eg = s.sb("eg", [P, 2, HEADS, P])
        sq = s.sb("sq", [P, 2 * HEADS, P])
        ssq = s.sb("ssq", [P, 2 * HEADS])
        rn = s.sb("rn", [P, 4, 2 * HEADS])
        qk_n = s.sb("qk_n", [P, 2 * HEADS, P])
        vb = s.sb("vb", [P, HEADS, P])
        kbg = s.sb("kbg", [P, HEADS, P])
        kdec = s.sb("kdec", [P, 2, HEADS, P])
        qk_nT = s.sb("qk_nT", [P, 2 * HEADS, P])
        dif = s.sb("dif", [P, HEADS, P])
        dec = s.sb("dec", [P, 2, HEADS, P])
        L = s.sb("L", [P, HEADS, P])
        Z = s.sb("Z", [P, HEADS, P])
        U = s.sb("U", [P, HEADS, P])
        T = s.sb("T", [P, HEADS, P])
        attnT = s.sb("attnT", [P, 2, HEADS, P])
        wT = s.sb("wT", [P, 2, HEADS, P])
        u = s.sb("u", [P, 2, HEADS, P])
        qdT = s.sb("qdT", [P, 2, HEADS, P])
        S = s.sb("S", [P, HEADS, P])
        Sd = s.sb("Sd", [P, HEADS, P])
        vnew = s.sb("vnew", [P, HEADS, P])
        osq = s.sb("osq", [P, HEADS, P])
        ossq = s.sb("ossq", [P, HEADS])
        orn = s.sb("orn", [P, 4, HEADS])
        on = s.sb("on", [P, HEADS, P])
        mix = s.sb("mix", [P, HEADS, P])
        b0, b1, b2, b3, vs_ps, o_ps, kv_ps, oT_ps = [s.ps(f"b{n}", [P, HEADS, P]) for n in range(8)]

        const_sem, mask_sem = s.sem("consts"), s.sem("masks")
        small_loaded, ba_loaded = s.sem("small_loaded"), s.sem("ba_loaded")
        pre = s.sem("pre")
        loaded = [s.sem(f"loaded{b}") for b in range(2)]
        z_loaded = [s.sem(f"z_loaded{b}") for b in range(2)]
        cur_done = s.sem("cur_done")
        cums_done = s.sem("cums_done")
        qk_turned = s.sem("qk_turned")
        turned_done = s.sem("turned_done")
        sq_done, eg_done = s.sem("sq_done"), s.sem("eg_done")
        ssq_done, log_done, root_done = s.sem("ssq_done"), s.sem("log_done"), s.sem("root_done")
        newton = s.sem("newton")
        scaled = s.sem("scaled")
        dif_done, clamp_done, dec_done = s.sem("dif_done"), s.sem("clamp_done"), s.sem("dec_done")
        kbg_done, kdec_done = s.sem("kbg_done"), s.sem("kdec_done")
        masked = s.sem("masked")
        back_done, back_copied = s.sem("back_done"), s.sem("back_copied")
        gram_done = s.sem("gram_done")
        L_done, attn_done = s.sem("L_done"), s.sem("attn_done")
        LT_done, tt_done, t_copied, zp_done, z_done, yp_done, u_step, wu_done, wu_copied = (
            [s.sem(f"{n}{g}") for g in range(2)] for n in
            ("LT_done", "tt_done", "t_copied", "zp_done", "z_done", "yp_done", "u_step", "wu_done", "wu_copied"))
        qd_done = s.sem("qd_done")
        s_zero = s.sem("s_zero")
        ws_done, v_done, sd_done, kv_done, s_done = (s.sem(n) for n in ("ws_done", "v_done", "sd_done", "kv_done", "s_done"))
        o_done = s.sem("o_done")
        osq_done, ossq_done, olog_done, oroot_done, onewton = (s.sem(n) for n in ("osq_done", "ossq_done", "olog_done", "oroot_done", "onewton"))
        on_done, oT_done, mix_done, mix_free, stored = (s.sem(n) for n in ("on_done", "oT_done", "mix_done", "mix_free", "stored"))
        rec_done = s.sem("rec_done")
        block = ctx.enter_context(nc.Block())
        NL = len(LEVELS)
        PAIR = [slice(0, 2), slice(2, 4)]
        zy_ps, T_ps = [b0, b1], [b2, b3]
        N_MASKS = 5 + 2 * (1 + NL) + 1
        PRE_GATE = 13

        def column(c):
            return scal[:].rearrange("p t (c h) -> p t c h", c=5)[:, :, c, :]

        def heads(ap):
            return ap.unsqueeze(2).broadcast_to([P, ap.shape[1], P])

        def each(ap):
            return ap.unsqueeze(1).broadcast_to([P, HEADS, P])

        def twice(ap):
            return ap.unsqueeze(1).broadcast_to([P, 2, P])

        def pipeline(prepare, advance, both):
            def run(loop):
                prepare(0, 0)
                with loop(0, TILES // 2 - 1) as i:
                    both(2 * i, 0)
                    both(2 * i + 1, 1)
                both(TILES - 2, 0)
                advance(TILES - 1, 1)
            return run

        @block.sync
        def _(sp):
            def load(t, b):
                src = hT[T_Q:T_Z, :, bass.ds(P * t, P)].rearrange("a p t -> p a t")
                sp.dma_start(qkv[:, b], src).then_inc(loaded[b], 16)

            def load_z(t, b):
                src = hT[T_Z:T_CQ, :, bass.ds(P * t, P)].rearrange("a p t -> p a t")
                sp.dma_start(zT[:, b], src).then_inc(z_loaded[b], 16)

            def step(t, b, more=True, more_z=True):
                if more:
                    sp.wait_ge(turned_done, t + 3)
                    load(t + 3, 1 - b)
                sp.wait_ge(mix_done, t + 1)
                sp.dma_start(mixT[0:HEADS, :, bass.ds(P * t, P)].rearrange("a p t -> p a t"), mix[:]).then_inc(stored, 16)
                if more_z:
                    load_z(t + 2, b)
                sp.wait_ge(stored, 16 * t + 16)
                sp.sem_inc(mix_free, 1)

            sp.dma_start(ba_raw[:], hT[T_KR, ROPE:ROPE + 2 * HEADS, :]).then_inc(ba_loaded, 16)
            sp.dma_start(bias[:], dt_bias.partition_broadcast(P)).then_inc(small_loaded, 16)
            sp.dma_start(rate[:], a_log.partition_broadcast(P)).then_inc(small_loaded, 16)
            sp.dma_start(gnorm[:], norm_g).then_inc(small_loaded, 16)
            sp.sem_inc(mix_free, 1)
            for t in range(2):
                load(t, t)
            for t in range(2):
                load_z(t, t)
            sp.wait_ge(turned_done, 2)
            load(2, 0)
            with sp.Fori(0, TILES // 2 - 2) as i:
                step(2 * i, 0)
                step(2 * i + 1, 1)
            step(TILES - 4, 0)
            step(TILES - 3, 1, more=False)
            step(TILES - 2, 0, more=False, more_z=False)
            step(TILES - 1, 1, more=False, more_z=False)

        @block.gpsimd
        def _(pool):
            n = [0]

            def put(out, in_, op, fill, base, pattern, mult):
                if n[0]:
                    pool.wait_ge(mask_sem, n[0])
                pool.affine_select(out=out, in_=in_, compare_op=op, fill=fill, base=base, pattern=pattern,
                                   channel_multiplier=mult).then_inc(mask_sem, 1)
                n[0] += 1

            pool.memset(ident[:], 0.0).then_inc(const_sem, 1)
            pool.memset(ones[:], 1.0).then_inc(const_sem, 1)
            pool.memset(eps_l2[:], RMS_EPS).then_inc(const_sem, 1)
            pool.memset(corner[:], 0.0).then_inc(const_sem, 1)
            pool.wait_ge(const_sem, 4)
            put(ident[:], ident[:], ALU.not_equal, 1.0, 0, [[-1, P]], 1)
            halves = lambda ap: ap.rearrange("p (c f) -> p c f", c=2)
            put(halves(chunk[:]), halves(ones[:]), ALU.is_ge, 0.0, 0, [[-CHUNK, 2], [0, CHUNK]], 1)
            put(halves(chunk[:]), halves(chunk[:]), ALU.is_ge, 0.0, CHUNK - 1, [[CHUNK, 2], [0, CHUNK]], -1)
            put(upto[:], chunk[:], ALU.is_ge, 0.0, 0, [[1, P]], -1)
            put(below[:], chunk[:], ALU.is_gt, 0.0, 0, [[-1, P]], 1)
            for l, size in enumerate((1,) + LEVELS):
                blocks = P // (2 * size)
                right = lambda ap: ap.rearrange("p (n h r) -> p n h r", h=2, r=size)[:, :, 1, :]
                put(right(corner[:, l]), right(ones[:]), ALU.is_ge, 0.0, 0, [[-2 * size, blocks], [0, size]], 1)
                put(right(corner[:, l]), right(corner[:, l]), ALU.is_ge, 0.0, size - 1, [[2 * size, blocks], [0, size]], -1)
            pool.wait_ge(mask_sem, n[0])
            pool.sem_inc(mask_sem, 1)

            def prepare(t, b):
                pool.wait_ge(cur_done, t + 1)
                pool.wait_ge(turned_done, t + 1)
                pool.tensor_tensor(cums[:], each(upto[:]), heads(cur[:, b, GATE]), ALU.mult).then_inc(cums_done, 1)
                pool.wait_ge(dec_done, t + 1)
                pool.tensor_tensor(dec[:, 0], dec[:, 0], each(below[:]), ALU.mult).then_inc(masked, 1)
                pool.wait_ge(masked, 3 * t + 1)
                pool.tensor_tensor(dec[:, 0], dec[:, 0], heads(cur[:, b, BETA]), ALU.mult).then_inc(masked, 1)
                pool.tensor_tensor(dec[:, 1], dec[:, 1], each(upto[:]), ALU.mult).then_inc(masked, 1)
                pool.wait_ge(scaled, 3 * t + 1)
                for g in range(2):
                    reached(pool, wu_done[g], t)
                pool.tensor_tensor(kbg[:], qk_n[:, HEADS:], heads(cur[:, b, BETA_G]), ALU.mult).then_inc(kbg_done, 1)
                pool.wait_ge(rec_done, t + 1)
                pool.tensor_tensor(kdec[:, b], qk_n[:, HEADS:], heads(cur[:, b, K_DEC]), ALU.mult).then_inc(kdec_done, 1)
                pool.wait_ge(back_copied, 2 * t + 2)
                pool.wait_ge(eg_done, t + 1)
                pool.tensor_tensor(qdT[:, b], qk_nT[:, 0:HEADS], eg[:, b], ALU.mult).then_inc(qd_done, 1)

            pool.sem_inc(kdec_done, 1)
            pool.sem_inc(qd_done, 1)
            pipeline(prepare, lambda t, b: None, lambda t, b: prepare(t + 1, 1 - b))(pool.Fori)

        @block.tensor
        def _(pe):
            def transposes(out, src, n0, count):
                for h in range(count):
                    last = pe.transpose(out[:, h], src[:, n0 + h], ident[:])
                return last

            def pre_scalars():
                pe.wait_ge(mask_sem, N_MASKS)
                pe.wait_ge(ba_loaded, 16)
                for t in range(TILES):
                    last = pe.transpose(b0[:].rearrange("p h f -> p (h f)")[:, 8 * t:8 * t + 8],
                                        ba_raw[:, t * P:(t + 1) * P], ident[0:8, 0:8])
                last.then_inc(pre, 1)
                pe.wait_ge(pre, PRE_GATE)
                pe.matmul(b1[:, 0, 0:64], upto[:], soft[:, 2].rearrange("p t h -> p (t h)"), start=True, stop=True)
                pe.matmul(b2[:, 0, 0:64], chunk[:], soft[:, 2].rearrange("p t h -> p (t h)"), start=True, stop=True).then_inc(pre, 1)
                pe.wait_ge(pre, PRE_GATE + 6)

            def p_turn(t, b):
                pe.wait_ge(loaded[b], 8 * (t - b) + 16)
                transposes(b0, qkv[:, b], 0, HEADS)
                transposes(b1, qkv[:, b], HEADS, HEADS).then_inc(qk_turned, 1)

            def p_turn_v(t, b):
                for g in range(2):
                    reached(pe, wu_copied[g], 2 * t)
                transposes(b2, qkv[:, b], 2 * HEADS, HEADS)
                pe.wait_ge(cums_done, t + 1)
                pe.matmul(b3[:].rearrange("p h f -> p (h f)"), ones[:], cums[:].rearrange("p h f -> p (h f)"),
                          start=True, stop=True).then_inc(turned_done, 1)

            def p_back(t, b):
                pe.wait_ge(scaled, 3 * t + 3)
                transposes(b0, qk_n, 0, HEADS)
                transposes(b1, qk_n, HEADS, HEADS).then_inc(back_done, 1)

            def p_gram(t, b):
                pe.wait_ge(back_copied, 2 * t + 2)
                for h in range(HEADS):
                    pe.matmul(b0[:, h], qk_nT[:, HEADS + h], qk_nT[:, HEADS + h], start=True, stop=True)
                for h in range(HEADS):
                    last = pe.matmul(b1[:, h], qk_nT[:, HEADS + h], qk_nT[:, h], start=True, stop=True)
                last.then_inc(gram_done, 1)

            def p_first(t, g):
                if g == 0:
                    pe.wait_ge(L_done, t + 1)
                for h in range(2):
                    last = pe.transpose(T_ps[g][:, h], L[:, 2 * g + h], ident[:])
                last.then_inc(LT_done[g], 1)

            def p_z(t, l, g):
                pe.wait_ge(u_step[g], (NL + 1) * t + l + 1)
                if l == 0 and g == 1:
                    pe.wait_ge(attn_done, t + 1)
                for h in range(2):
                    last = pe.transpose(T_ps[g][:, h], U[:, 2 * g + h], ident[:])
                last.then_inc(tt_done[g], 1)
                for h in range(2):
                    last = pe.matmul(zy_ps[g][:, h], L[:, 2 * g + h], U[:, 2 * g + h], start=True, stop=True)
                last.then_inc(zp_done[g], 1)

            def p_y(t, l, g):
                pe.wait_ge(t_copied[g], NL * t + l + 1)
                pe.wait_ge(z_done[g], (NL + 1) * t + l + 2)
                for h in range(2):
                    last = pe.matmul(zy_ps[g][:, h], T[:, 2 * g + h], Z[:, 2 * g + h], start=True, stop=True)
                last.then_inc(yp_done[g], 1)

            def p_levels(t, l0, l1):
                for l in range(l0, l1):
                    for g in range(2):
                        p_z(t, l, g)
                    for g in range(2):
                        p_y(t, l, g)

            def p_wu(t, g):
                pe.wait_ge(u_step[g], (NL + 1) * (t + 1))
                pe.wait_ge(kbg_done, t + 1)
                for h in range(2):
                    pe.matmul(T_ps[g][:, h], kbg[:, 2 * g + h], U[:, 2 * g + h], start=True, stop=True)
                for h in range(2):
                    last = pe.matmul(T_ps[g][:, 2 + h], U[:, 2 * g + h], vb[:, 2 * g + h], start=True, stop=True)
                last.then_inc(wu_done[g], 1)

            def a_state(t, b, c):
                lo, hi = CHUNK * c, CHUNK * (c + 1)
                if c == 0:
                    for g in range(2):
                        pe.wait_ge(wu_copied[g], 2 * t + 2)
                    pe.wait_ge(qd_done, t + 2)
                    pe.wait_ge(on_done, t + 1)
                pe.wait_ge(s_done, 2 * t + c + 1)
                for h in range(HEADS):
                    last = pe.matmul(vs_ps[lo:hi, h], wT[:, b, h, lo:hi], S[:, h], start=True, stop=True)
                last.then_inc(ws_done, 1)
                for h in range(HEADS):
                    pe.matmul(o_ps[lo:hi, h], qdT[:, b, h, lo:hi], S[:, h], start=(h == 0), stop=False, skip_group_check=True)

            def a_update(t, b, c):
                lo, hi = CHUNK * c, CHUNK * (c + 1)
                pe.wait_ge(v_done, 2 * t + c + 1)
                if c == 0:
                    pe.wait_ge(kdec_done, t + 2)
                for h in range(HEADS):
                    last = pe.matmul(kv_ps[:, h], kdec[lo:hi, b, h], vnew[lo:hi, h], start=True, stop=True)
                last.then_inc(kv_done, 1)
                for h in range(HEADS):
                    last = pe.matmul(o_ps[lo:hi, h], attnT[lo:hi, b, h, lo:hi], vnew[lo:hi, h], start=False, stop=True,
                                     skip_group_check=True)
                last.then_inc(o_done, 1)

            def a_out(t, b):
                pe.wait_ge(on_done, t + 2)
                transposes(oT_ps, on, 0, HEADS).then_inc(oT_done, 1)

            def prepare(t, b):
                p_turn(t, b)
                p_turn_v(t, b)
                p_back(t, b)
                p_gram(t, b)
                for g in range(2):
                    p_first(t, g)
                p_levels(t, 0, NL)
                for g in range(2):
                    p_wu(t, g)

            def advance(t, b):
                for c in range(2):
                    a_state(t, b, c)
                    a_update(t, b, c)
                a_out(t, b)

            def both(t, b):
                n, m = t + 1, 1 - b
                p_turn(n, m)
                a_state(t, b, 0)
                p_turn_v(n, m)
                a_update(t, b, 0)
                a_state(t, b, 1)
                p_back(n, m)
                a_update(t, b, 1)
                p_gram(n, m)
                for g in range(2):
                    p_first(n, g)
                p_levels(n, 0, 3)
                a_out(t, b)
                p_levels(n, 3, NL)
                for g in range(2):
                    p_wu(n, g)

            pe.sem_inc(turned_done, 1)
            pre_scalars()
            pipeline(prepare, advance, both)(pe.Fori)

        @block.scalar
        def _(act):
            def pre_scalars():
                act.preload_act_table_set("natural_log_exp_and_others")
                act.wait_ge(small_loaded, 48)
                act.wait_ge(pre, 1)
                act.activation(ba[:].rearrange("p t c -> p (t c)"), b0[:, 0, :], ACT.Copy).then_inc(pre, 1)
                act.activation(rate[:], rate[:], ACT.Exp).then_inc(pre, 1)
                act.wait_ge(pre, 4)
                act.activation(soft[:, 1], soft[:, 0], ACT.Abs).then_inc(pre, 1)
                act.wait_ge(pre, 5)
                act.activation(soft[:, 1], soft[:, 1], ACT.Exp, scale=-1.0).then_inc(pre, 1)
                act.wait_ge(pre, 6)
                act.activation(soft[:, 1], soft[:, 1], ACT.Ln, bias=1.0).then_inc(pre, 1)
                act.activation(ba[:, :, 0:HEADS], ba[:, :, 0:HEADS], ACT.Exp, scale=-1.0).then_inc(pre, 1)
                act.wait_ge(pre, PRE_GATE + 1)
                act.activation(soft[:, 0].rearrange("p t h -> p (t h)"), b1[:, 0, 0:64], ACT.Exp).then_inc(pre, 1)
                act.wait_ge(pre, PRE_GATE + 4)
                act.activation(column(K_DEC), soft[:, 1], ACT.Exp).then_inc(pre, 1)

            def p_squares(t, b):
                act.wait_ge(qk_turned, t + 1)
                act.activation(sq[:, 0:HEADS], b0[:], ACT.Square).then_inc(sq_done, 1)
                act.activation(sq[:, HEADS:], b1[:], ACT.Square).then_inc(sq_done, 1)
                act.wait_ge(turned_done, t + 2)
                act.wait_ge(rec_done, t + 1)
                act.activation(eg[:, b], b3[:], ACT.Exp).then_inc(eg_done, 1)

            def p_roots(t, b):
                act.wait_ge(ssq_done, t + 1)
                act.activation(rn[:, 0], ssq[:], ACT.Ln, bias=eps_l2[:, 0:1]).then_inc(log_done, 1)
                act.wait_ge(log_done, t + 1)
                act.activation(rn[:, 1], rn[:, 0], ACT.Exp, scale=-0.5).then_inc(root_done, 1)

            def p_decays(t, b):
                act.wait_ge(clamp_done, 2 * t + 2)
                act.activation(dec[:], dec[:], ACT.Exp).then_inc(dec_done, 1)

            def p_copy_back(t, b):
                act.wait_ge(back_done, t + 1)
                act.wait_ge(qd_done, t + 1)
                act.activation(qk_nT[:, 0:HEADS], b0[:], ACT.Copy, scale=float(P) ** -0.5).then_inc(back_copied, 1)
                act.activation(qk_nT[:, HEADS:], b1[:], ACT.Copy).then_inc(back_copied, 1)

            def p_copy_t(t, l0, l1):
                for l in range(l0, l1):
                    for g in range(2):
                        act.wait_ge(tt_done[g], NL * t + l + 1)
                        act.activation(T[:, PAIR[g]], T_ps[g][:, 0:2], ACT.Copy).then_inc(t_copied[g], 1)

            def p_copy_wu(t, b):
                for g in range(2):
                    act.wait_ge(wu_done[g], t + 1)
                    act.activation(wT[:, b, PAIR[g]], T_ps[g][:, 0:2], ACT.Copy).then_inc(wu_copied[g], 1)
                    act.activation(u[:, b, PAIR[g]], T_ps[g][:, 2:4], ACT.Copy).then_inc(wu_copied[g], 1)

            def a_squares(t, b):
                act.wait_ge(o_done, 2 * t + 2)
                act.activation(osq[:], o_ps[:], ACT.Square).then_inc(osq_done, 1)

            def a_roots(t, b):
                act.wait_ge(ossq_done, t + 1)
                act.activation(orn[:, 0], ossq[:], ACT.Ln, bias=eps_l2[:, 0:1], scale=1.0 / P).then_inc(olog_done, 1)
                act.wait_ge(olog_done, t + 1)
                act.activation(orn[:, 1], orn[:, 0], ACT.Exp, scale=-0.5).then_inc(oroot_done, 1)

            def prepare(t, b):
                p_squares(t, b)
                p_roots(t, b)
                p_decays(t, b)
                p_copy_back(t, b)
                p_copy_t(t, 0, NL)
                p_copy_wu(t, b)

            def advance(t, b):
                a_squares(t, b)
                a_roots(t, b)

            def both(t, b):
                n, m = t + 1, 1 - b
                p_squares(n, m)
                p_roots(n, m)
                p_decays(n, m)
                p_copy_back(n, m)
                a_squares(t, b)
                p_copy_t(n, 0, 1)
                a_roots(t, b)
                p_copy_t(n, 1, NL)
                p_copy_wu(n, m)

            act.wait_ge(const_sem, 4)
            pre_scalars()
            pipeline(prepare, advance, both)(act.Fori)

        @block.vector
        def _(dve):
            def pre_scalars():
                dve.memset(S[:], 0.0).then_inc(s_done, 1)
                dve.sem_inc(rec_done, 2)
                dve.sem_inc(on_done, 1)
                dve.wait_ge(pre, 3)
                dve.tensor_tensor(soft[:, 0], ba[:, :, HEADS:], bias[:].unsqueeze(1).broadcast_to([P, TILES, HEADS]),
                                  ALU.add).then_inc(pre, 1)
                dve.wait_ge(pre, 8)
                dve.scalar_tensor_tensor(soft[:, 1], soft[:, 0], 0.0, soft[:, 1], ALU.max, ALU.add).then_inc(pre, 1)
                dve.wait_ge(pre, 9)
                dve.scalar_tensor_tensor(soft[:, 2], soft[:, 1], -1.0, rate[:].unsqueeze(1).broadcast_to([P, TILES, HEADS]),
                                         ALU.mult, ALU.mult).then_inc(pre, 1)
                dve.tensor_scalar(ba[:, :, 0:HEADS], ba[:, :, 0:HEADS], 1.0, None, ALU.add).then_inc(pre, 1)
                dve.wait_ge(pre, 11)
                dve.reciprocal(column(BETA), ba[:, :, 0:HEADS]).then_inc(pre, 1)
                dve.tensor_copy(column(GATE), soft[:, 2]).then_inc(pre, 1)
                dve.wait_ge(pre, PRE_GATE + 2)
                view = lambda bank: bank[:, 0, 0:64].rearrange("p (t h) -> p t h", h=HEADS)
                dve.tensor_copy(column(GCUM), view(b1)).then_inc(pre, 1)
                dve.wait_ge(pre, PRE_GATE + 3)
                dve.tensor_tensor(soft[:, 1], view(b2), column(GCUM), ALU.subtract).then_inc(pre, 1)
                dve.tensor_tensor(column(BETA_G), column(BETA), soft[:, 0], ALU.mult).then_inc(pre, 1)
                dve.wait_ge(pre, PRE_GATE + 6)

            def p_scalars(t, b):
                dve.wait_ge(rec_done, t + 1)
                dve.tensor_scalar(cur[:, b].rearrange("p c h -> p (c h)"), scal[:, bass.ds(t, 1)].rearrange("p a c -> p (a c)"),
                                  1.0, None, ALU.mult).then_inc(cur_done, 1)

            def p_ssq(t, b):
                dve.wait_ge(sq_done, 2 * t + 2)
                dve.tensor_reduce(ssq[:], sq[:], AX.X, ALU.add).then_inc(ssq_done, 1)

            def p_difference(t, b):
                dve.wait_ge(cur_done, t + 1)
                dve.wait_ge(eg_done, t + 1)
                dve.tensor_tensor(dif[:], b3[:], heads(cur[:, b, GCUM]), ALU.subtract).then_inc(dif_done, 1)
                dve.wait_ge(dif_done, t + 1)
                dve.tensor_scalar(dec[:, 0], dif[:], 0.0, -1.0, ALU.max, ALU.mult).then_inc(clamp_done, 1)
                dve.tensor_scalar(dec[:, 1], dif[:], 0.0, None, ALU.min).then_inc(clamp_done, 1)

            def p_newton(t, b):
                dve.wait_ge(root_done, t + 1)
                dve.tensor_tensor(rn[:, 2], rn[:, 1], rn[:, 1], ALU.mult).then_inc(newton, 1)
                dve.tensor_scalar(ssq[:], ssq[:], RMS_EPS, -0.5, ALU.add, ALU.mult).then_inc(newton, 1)
                dve.wait_ge(newton, 4 * t + 2)
                dve.tensor_tensor(rn[:, 2], rn[:, 2], ssq[:], ALU.mult).then_inc(newton, 1)
                dve.wait_ge(newton, 4 * t + 3)
                dve.scalar_tensor_tensor(rn[:, 3], rn[:, 2], 1.5, rn[:, 1], ALU.add, ALU.mult).then_inc(newton, 1)
                dve.wait_ge(newton, 4 * t + 4)

            def p_scale(t, b):
                dve.wait_ge(kdec_done, t + 1)
                dve.tensor_tensor(qk_n[:, HEADS:], b1[:], heads(rn[:, 3, HEADS:]), ALU.mult).then_inc(scaled, 1)
                dve.tensor_tensor(qk_n[:, 0:HEADS], b0[:], heads(rn[:, 3, 0:HEADS]), ALU.mult).then_inc(scaled, 1)

            def p_scale_v(t, b):
                dve.tensor_tensor(vb[:], b2[:], heads(cur[:, b, BETA]), ALU.mult).then_inc(scaled, 1)

            def p_grams(t, b):
                dve.wait_ge(gram_done, t + 1)
                dve.wait_ge(masked, 3 * t + 3)
                dve.tensor_tensor(L[:], b0[:], dec[:, 0], ALU.mult).then_inc(L_done, 1)
                dve.tensor_tensor(attnT[:, b], b1[:], dec[:, 1], ALU.mult).then_inc(attn_done, 1)

            def p_first(t, g):
                pair = PAIR[g]
                dve.wait_ge(LT_done[g], t + 1)
                dve.tensor_tensor(Z[:, pair], T_ps[g][:, 0:2], twice(corner[:, 0]), ALU.mult).then_inc(z_done[g], 1)
                dve.wait_ge(z_done[g], (NL + 1) * t + 1)
                dve.tensor_tensor(U[:, pair], twice(ident[:]), Z[:, pair], ALU.subtract).then_inc(u_step[g], 1)

            def p_levels(t, l0, l1):
                for l in range(l0, l1):
                    for g in range(2):
                        dve.wait_ge(zp_done[g], NL * t + l + 1)
                        dve.tensor_tensor(Z[:, PAIR[g]], zy_ps[g][:, 0:2], twice(corner[:, l + 1]), ALU.mult).then_inc(z_done[g], 1)
                    for g in range(2):
                        dve.wait_ge(yp_done[g], NL * t + l + 1)
                        dve.tensor_tensor(U[:, PAIR[g]], U[:, PAIR[g]], zy_ps[g][:, 0:2], ALU.subtract).then_inc(u_step[g], 1)

            def a_v(t, b, c):
                lo, hi = CHUNK * c, CHUNK * (c + 1)
                dve.wait_ge(ws_done, 2 * t + c + 1)
                dve.tensor_tensor(vnew[lo:hi], u[lo:hi, b], vs_ps[lo:hi], ALU.subtract).then_inc(v_done, 1)
                dve.wait_ge(s_done, 2 * t + c + 1)
                dve.tensor_tensor(Sd[:], S[:], eg[:, b, :, hi - 1:hi].broadcast_to([P, HEADS, P]), ALU.mult).then_inc(sd_done, 1)

            def a_s(t, b, c):
                dve.wait_ge(sd_done, 2 * t + c + 1)
                dve.wait_ge(kv_done, 2 * t + c + 1)
                dve.tensor_tensor(S[:], Sd[:], kv_ps[:], ALU.add).then_inc(s_done, 1)

            def a_ssq(t, b):
                dve.wait_ge(osq_done, t + 1)
                dve.tensor_reduce(ossq[:], osq[:], AX.X, ALU.add).then_inc(ossq_done, 1)

            def a_norm(t, b):
                dve.wait_ge(oroot_done, t + 1)
                dve.tensor_tensor(orn[:, 2], orn[:, 1], orn[:, 1], ALU.mult).then_inc(onewton, 1)
                dve.tensor_scalar(ossq[:], ossq[:], RMS_EPS * P, -0.5 / P, ALU.add, ALU.mult).then_inc(onewton, 1)
                dve.wait_ge(onewton, 4 * t + 2)
                dve.tensor_tensor(orn[:, 2], orn[:, 2], ossq[:], ALU.mult).then_inc(onewton, 1)
                dve.wait_ge(onewton, 4 * t + 3)
                dve.scalar_tensor_tensor(orn[:, 3], orn[:, 2], 1.5, orn[:, 1], ALU.add, ALU.mult).then_inc(onewton, 1)
                dve.wait_ge(onewton, 4 * t + 4)
                dve.tensor_tensor(on[:], o_ps[:], heads(orn[:, 3]), ALU.mult).then_inc(on_done, 1)

            def a_gate(t, b):
                dve.wait_ge(oT_done, t + 1)
                dve.wait_ge(z_loaded[b], 8 * (t - b) + 16)
                dve.wait_ge(mix_free, t + 1)
                dve.scalar_tensor_tensor(mix[:], oT_ps[:], gnorm[:, 0:1], zT[:, b], ALU.mult, ALU.mult).then_inc(mix_done, 1)
                dve.wait_ge(mix_done, t + 1)
                dve.sem_inc(rec_done, 1)

            def prepare(t, b):
                p_scalars(t, b)
                p_ssq(t, b)
                p_difference(t, b)
                p_newton(t, b)
                p_scale(t, b)
                p_scale_v(t, b)
                p_grams(t, b)
                for g in range(2):
                    p_first(t, g)
                p_levels(t, 0, NL)

            def advance(t, b):
                for c in range(2):
                    a_v(t, b, c)
                    a_s(t, b, c)
                a_ssq(t, b)
                a_norm(t, b)
                a_gate(t, b)

            def both(t, b):
                n, m = t + 1, 1 - b
                p_scalars(n, m)
                a_v(t, b, 0)
                p_ssq(n, m)
                p_difference(n, m)
                a_s(t, b, 0)
                p_newton(n, m)
                p_scale(n, m)
                a_v(t, b, 1)
                p_scale_v(n, m)
                a_s(t, b, 1)
                p_grams(n, m)
                for g in range(2):
                    p_first(n, g)
                p_levels(n, 0, 1)
                a_ssq(t, b)
                p_levels(n, 1, 2)
                a_norm(t, b)
                p_levels(n, 2, 4)
                a_gate(t, b)
                p_levels(n, 4, NL)

            pre_scalars()
            pipeline(prepare, advance, both)(dve.Fori)


def attention(nc, made, mixT):
    QB = 2 * P
    NB = SEQ // QB
    blocks = [(0, j) for j in range(NB)] + [(1, j) for j in reversed(range(NB))]
    N = len(blocks)
    pairs = [j + 1 for _, j in blocks]
    groups = [j // 2 + 1 for _, j in blocks]
    pair0 = [sum(pairs[:n]) for n in range(N + 1)]
    group0 = [sum(2 * g for g in groups[:n]) for n in range(N + 1)]
    PAIRS, GROUPS = pair0[-1], group0[-1]
    ROUNDS = HEADS // 2
    S_RING, T_RING = 4, 3
    MASK = -1e30
    with ExitStack() as ctx:
        s = Scope(nc, ctx, "at")
        q_hi, q_lo, k_hi, k_lo, v_hi, v_lo, qr = (s.sb(n, [P, 2, SEQ], F32R) for n in
                                                  ("q_hi", "q_lo", "k_hi", "k_lo", "v_hi", "v_lo", "qr"))
        kr = s.sb("kr", [P, SEQ], F32R)
        kr_hi = s.sb("kr_hi", [P, SEQ], F32R)
        ident = s.sb("ident", [P, P])
        prob = s.sb("prob", [P, 2, 2, SEQ])
        negm = s.sb("negm", [P, 2, 2, 4])
        sums = s.sb("sums", [P, 2, 2, 4])
        top = s.sb("top", [P, 2, 2])
        fac = s.sb("fac", [P, 2, 2, 4])
        part = s.sb("part", [P, 2, 2, 4])
        total = s.sb("total", [P, 2, 2])
        scale = s.sb("scale", [P, 2, 2, 4])
        pT_hi = s.sb("pT_hi", [P, T_RING, 2 * QB], F32R)
        pT_lo = s.sb("pT_lo", [P, T_RING, 2 * QB], F32R)
        out = s.sb("out", [P, 2, QB])
        score_ps = s.ps("score_ps", [P, S_RING, NTOK])
        pT_ps = s.ps("pT_ps", [P, T_RING, 2 * QB])
        acc_ps = s.ps("acc_ps", [P, NTOK])

        C_EXP, C_TURN, C_LO, C_PV, C_OUT, C_FREE = S_RING, 2, T_RING, T_RING, 1, 2
        const_sem = s.sem("consts")
        kr_loaded = s.sem("kr_loaded")
        loaded = [s.sem(f"loaded{b}") for b in range(2)]
        score_done = s.sem("score_done")
        diag_done = s.sem("diag_done")
        max_done = s.sem("max_done")
        exp_done = s.sem("exp_done")
        top_done, gap_done, fac_done, part_done, total_done, inv_done = (
            s.sem(n) for n in ("top_done", "gap_done", "fac_done", "part_done", "total_done", "inv_done"))
        scale_done = s.sem("scale_done")
        scaled = s.sem("scaled")
        turned = s.sem("turned")
        hi_done = s.sem("hi_done")
        lo_done = s.sem("lo_done")
        pv_done = s.sem("pv_done")
        out_done = s.sem("out_done")
        out_free = s.sem("out_free")
        storing, stored = s.sem("storing"), s.sem("stored")
        block = ctx.enter_context(nc.Block())
        LOADS = 8
        many = [n for n in range(N) if groups[n] > 1]
        MANY = len(many)

        def widths(j, tile):
            keys = P * (2 * j + tile + 1)
            return [min(NTOK, keys - NTOK * g) for g in range(j // 2 + 1)]

        @block.gpsimd
        def _(pool):
            def load(h):
                b = h % 2
                for dst, name in ((q_hi, "qnT_hi"), (k_hi, "knT_hi"), (q_lo, "qnT_lo"), (k_lo, "knT_lo")):
                    pool.dma_start(dst[:, b], made[name][h]).then_inc(loaded[b], 16)
                pool.dma_start(qr[0:ROPE, b], made["qrT_lo"][h]).then_inc(loaded[b], 16)
                pool.dma_start(qr[ROPE:, b], made["qrT_hi"][h]).then_inc(loaded[b], 16)
                for dst, name in ((v_hi, "v_hi"), (v_lo, "v_lo")):
                    pool.dma_start(dst[:, b].rearrange("p (a n) -> p a n", n=P),
                                   made[name][:, :, P * h:P * h + P].rearrange("a p n -> p a n")).then_inc(loaded[b], 16)

            load(0)
            for dst, name in ((kr[0:ROPE], "krT_hi"), (kr[ROPE:], "krT_lo"), (kr_hi[ROPE:], "krT_hi")):
                pool.dma_start(dst, made[name]).then_inc(kr_loaded, 16)
            load(1)
            pool.memset(ident[:], 0.0).then_inc(const_sem, 1)
            pool.wait_ge(const_sem, 1)
            pool.affine_select(out=ident[:], in_=ident[:], compare_op=ALU.not_equal, fill=1.0, base=0, pattern=[[-1, P]],
                               channel_multiplier=1).then_inc(const_sem, 1)
            for i in range(ROUNDS):
                for n, (b, j) in enumerate(blocks):
                    if i + 1 < ROUNDS and n == NB + 1:
                        pool.wait_ge(pv_done, pair0[NB] + C_PV)
                        load(2 * (i + 1))
                    if i and n == 1:
                        pool.wait_ge(pv_done, PAIRS * i + C_PV)
                        load(2 * i + 1)
                    pool.wait_ge(scale_done, N * i + n + 1)
                    pb, g = n % 2, groups[n]
                    ops = []
                    for tile in range(2):
                        if g > 1:
                            view = prob[:, pb, tile, 0:NTOK * (g - 1)].rearrange("p (g n) -> p g n", n=NTOK)
                            ops.append((view, scale[:, pb, tile, 0:g - 1].unsqueeze(2).broadcast_to([P, g - 1, NTOK])))
                        w = widths(j, tile)[-1]
                        view = prob[:, pb, tile, NTOK * (g - 1):NTOK * (g - 1) + w]
                        ops.append((view, scale[:, pb, tile, g - 1:g].broadcast_to([P, w])))
                    for view, by in ops:
                        op = pool.tensor_tensor(view, view, by, ALU.mult)
                    op.then_inc(scaled, 1)

        @block.tensor
        def _(pe):
            def scores(i, n):
                b, j = blocks[n]
                if j == (0 if b == 0 else NB - 1):
                    pe.wait_ge(loaded[b], 16 * LOADS * i + 16 * LOADS)
                G = group0[n]
                for tile in range(2):
                    qs = slice(QB * j + P * tile, QB * j + P * tile + P)
                    for g, w in enumerate(widths(j, tile)):
                        pe.wait_ge(exp_done, GROUPS * i + (G + 1 - S_RING + C_EXP))
                        ks, acc = slice(NTOK * g, NTOK * g + w), score_ps[:, G % S_RING, 0:w]
                        pe.matmul(acc, q_lo[:, b, qs], k_hi[:, b, ks], start=True, stop=False)
                        pe.matmul(acc, qr[:, b, qs], kr[:, ks], start=False, stop=False)
                        pe.matmul(acc, qr[ROPE:, b, qs], kr_hi[ROPE:, ks], start=False, stop=False)
                        pe.matmul(acc, q_hi[:, b, qs], k_lo[:, b, ks], start=False, stop=False)
                        pe.matmul(acc, q_hi[:, b, qs], k_hi[:, b, ks], start=False, stop=True).then_inc(score_done, 1)
                        G += 1

            def turn(i, n, p):
                j, k = blocks[n][1], pair0[n] + p
                if p == 0:
                    pe.wait_ge(scaled, N * i + n + 1)
                pe.wait_ge(lo_done, PAIRS * i + (k + 1 - T_RING + C_LO))
                for kt in range(2):
                    for tile in range(2):
                        if p == j and kt > tile:
                            continue
                        at = QB * kt + P * (tile if p < j or kt == 0 else 0)
                        src = prob[:, n % 2, tile, P * (2 * p + kt):P * (2 * p + kt) + P]
                        last = pe.transpose(pT_ps[:, k % T_RING, at:at + P], src, ident[:])
                last.then_inc(turned, 1)

            def values(i, n, p):
                (b, j), k = blocks[n], pair0[n] + p
                if p == 0:
                    pe.wait_ge(out_done, N * i + (n + C_OUT))
                pe.wait_ge(lo_done, PAIRS * i + (k + 1 + C_LO))
                for kt in range(2):
                    diag = p == j and kt == 1
                    acc = acc_ps[:, P:QB] if diag else acc_ps[:, 0:QB]
                    ps = slice(QB * kt, QB * kt + (P if diag else QB))
                    vs = slice(P * (2 * p + kt), P * (2 * p + kt) + P)
                    r = k % T_RING
                    pe.matmul(acc, v_lo[:, b, vs], pT_hi[:, r, ps], start=(p == 0 and kt == 0), stop=False)
                    pe.matmul(acc, v_hi[:, b, vs], pT_lo[:, r, ps], start=False, stop=False)
                    last = pe.matmul(acc, v_hi[:, b, vs], pT_hi[:, r, ps], start=False, stop=diag)
                last.then_inc(pv_done, 1)

            pe.wait_ge(kr_loaded, 48)
            pe.wait_ge(const_sem, 2)
            pe.sem_inc(turned, C_TURN)
            pe.sem_inc(pv_done, C_PV)
            with pe.Fori(0, ROUNDS) as i:
                scores(i, 0)
                for n in range(N):
                    if n + 1 < N:
                        scores(i, n + 1)
                    for p in range(min(2, pairs[n])):
                        turn(i, n, p)
                    for p in range(pairs[n]):
                        if p + 2 < pairs[n]:
                            turn(i, n, p + 2)
                        values(i, n, p)

        @block.scalar
        def _(act):
            def exps(i, n):
                j, pb, G = blocks[n][1], n % 2, group0[n]
                act.wait_ge(turned, PAIRS * i + (pair0[n] - pairs[n - 1] + C_TURN))
                for tile in range(2):
                    for g, w in enumerate(widths(j, tile)):
                        act.wait_ge(max_done, GROUPS * i + (G + 1))
                        act.activation(prob[:, pb, tile, NTOK * g:NTOK * g + w], score_ps[:, G % S_RING, 0:w], ACT.Exp,
                                       bias=negm[:, pb, tile, g:g + 1], accum_out=sums[:, pb, tile, g:g + 1]).then_inc(exp_done, 1)
                        G += 1
                if groups[n] > 1:
                    m, gs = many.index(n), slice(0, groups[n])
                    act.wait_ge(gap_done, MANY * i + (m + 1))
                    act.activation(fac[:, pb, :, gs], part[:, pb, :, gs], ACT.Exp).then_inc(fac_done, 1)

            def copies(i, n):
                for p in range(pairs[n]):
                    k = pair0[n] + p
                    w = 2 * QB if p + 1 < pairs[n] else QB + P
                    act.wait_ge(turned, PAIRS * i + (k + 1 + C_TURN))
                    act.wait_ge(pv_done, PAIRS * i + (k + 1 - T_RING + C_PV))
                    act.activation(pT_hi[:, k % T_RING, 0:w], pT_ps[:, k % T_RING, 0:w], ACT.Copy).then_inc(hi_done, 1)
                act.wait_ge(pv_done, PAIRS * i + (pair0[n + 1] + C_PV))
                act.wait_ge(out_free, N * i + (n - 1 + C_FREE))
                act.activation(out[:, n % 2], acc_ps[:, 0:QB], ACT.Copy).then_inc(out_done, 1)

            act.preload_act_table(ACT.Exp)
            act.sem_inc(exp_done, C_EXP)
            act.sem_inc(out_done, C_OUT)
            with act.Fori(0, ROUNDS) as i:
                exps(i, 0)
                for n in range(N):
                    if n + 1 < N:
                        exps(i, n + 1)
                    copies(i, n)

        @block.vector
        def _(dve):
            def maxima(i, n):
                j, pb, G = blocks[n][1], n % 2, group0[n]
                for tile in range(2):
                    ws = widths(j, tile)
                    for g, w in enumerate(ws):
                        acc = score_ps[:, G % S_RING, 0:w]
                        dve.wait_ge(score_done, GROUPS * i + (G + 1))
                        if g + 1 == len(ws):
                            dve.memset(acc[0:CHUNK, w - CHUNK:w], MASK).then_inc(diag_done, 1)
                            dve.wait_ge(diag_done, 2 * N * i + (2 * n + tile + 1))
                        dve.tensor_reduce(negm[:, pb, tile, g:g + 1], acc, AX.X, ALU.max, negate=True).then_inc(max_done, 1)
                        G += 1
                dve.wait_ge(max_done, GROUPS * i + G)
                gs, g = slice(0, groups[n]), groups[n]
                if g == 1:
                    dve.wait_ge(exp_done, GROUPS * i + (G + C_EXP))
                    dve.reciprocal(scale[:, pb, :, gs], sums[:, pb, :, gs]).then_inc(scale_done, 1)
                    return
                m = many.index(n)
                dve.tensor_reduce(top[:, pb], negm[:, pb, :, gs], AX.X, ALU.min).then_inc(top_done, 1)
                dve.wait_ge(top_done, MANY * i + (m + 1))
                wide = top[:, pb].unsqueeze(2).broadcast_to([P, 2, g])
                dve.tensor_tensor(part[:, pb, :, gs], wide, negm[:, pb, :, gs], ALU.subtract).then_inc(gap_done, 1)
                dve.wait_ge(fac_done, MANY * i + (m + 1))
                dve.tensor_tensor(part[:, pb, :, gs], fac[:, pb, :, gs], sums[:, pb, :, gs], ALU.mult).then_inc(part_done, 1)
                dve.wait_ge(part_done, MANY * i + (m + 1))
                dve.tensor_reduce(total[:, pb], part[:, pb, :, gs], AX.X, ALU.add).then_inc(total_done, 1)
                dve.wait_ge(total_done, MANY * i + (m + 1))
                dve.reciprocal(total[:, pb], total[:, pb]).then_inc(inv_done, 1)
                dve.wait_ge(inv_done, MANY * i + (m + 1))
                wide = total[:, pb].unsqueeze(2).broadcast_to([P, 2, g])
                dve.tensor_tensor(scale[:, pb, :, gs], fac[:, pb, :, gs], wide, ALU.mult).then_inc(scale_done, 1)

            def lows(i, n):
                for p in range(pairs[n]):
                    k = pair0[n] + p
                    w = 2 * QB if p + 1 < pairs[n] else QB + P
                    r = k % T_RING
                    dve.wait_ge(hi_done, PAIRS * i + (k + 1))
                    dve.tensor_tensor(pT_lo[:, r, 0:w], pT_ps[:, r, 0:w], pT_hi[:, r, 0:w].bitcast(F32),
                                      ALU.subtract).then_inc(lo_done, 1)

            dve.sem_inc(lo_done, C_LO)
            with dve.Fori(0, ROUNDS) as i:
                maxima(i, 0)
                for n in range(N):
                    if n + 1 < N:
                        maxima(i, n + 1)
                    lows(i, n)

        @block.sync
        def _(sp):
            sp.sem_inc(out_free, C_FREE)
            with sp.Fori(0, ROUNDS) as i:
                for n, (b, j) in enumerate(blocks):
                    dst = mixT[bass.ds(2 * i + (HEADS + b), 1), :, QB * j:QB * (j + 1)].rearrange("a p t -> p (a t)")
                    sp.wait_ge(out_done, N * i + (n + 1 + C_OUT))
                    sp.sem_inc(storing, 1)
                    sp.dma_start(dst, out[:, n % 2]).then_inc(stored, 16)
                    sp.wait_ge(stored, 16 * N * i + 16 * (n + 1))
                    sp.sem_inc(out_free, 1)


def feed_in(nc, xT, w_gate_up, hid):
    with ExitStack() as ctx:
        s = Scope(nc, ctx, "ff")
        x_raw = s.sb("x_raw", [P, 2, SEQ])
        x_hi = s.sb("x_hi", [P, KD, SEQ], F32R)
        x_lo = s.sb("x_lo", [P, KD, SEQ], F32R)
        w_raw = s.sb("w_raw", [P, 2, KD * P])
        w_hi = s.sb("w_hi", [P, 2, KD * P], F32R)
        w_lo = s.sb("w_lo", [P, 2, KD * P], F32R)
        zero = s.sb("zero", [P, 1])
        out = s.sb("out", [P, 2, SEQ])
        h_ps = s.ps("h_ps", [P, 2, BLOCKS, NTOK])

        x_loaded = [s.sem(f"x_loaded{b}") for b in range(2)]
        x_hi_done, x_lo_done = s.sem("x_hi_done"), s.sem("x_lo_done")
        w_loaded = [s.sem(f"w_loaded{b}") for b in range(2)]
        w_hi_done, w_lo_done = s.sem("w_hi_done"), s.sem("w_lo_done")
        made = s.sem("made")
        gate_free, up_free = s.sem("gate_free"), s.sem("up_free")
        zeroed = s.sem("zeroed")
        silu_done = s.sem("silu_done")
        out_made = s.sem("out_made")
        out_free = s.sem("out_free")
        stored = [s.sem(f"stored{b}") for b in range(2)]
        block = ctx.enter_context(nc.Block())

        @block.sync
        def _(sp):
            for k in range(KD):
                if k >= 2:
                    sp.wait_ge(x_lo_done, k - 1)
                sp.dma_start(x_raw[:, k % 2, :], xT[k]).then_inc(x_loaded[k % 2], 16)
            sp.sem_inc(out_free, 2)
            with sp.Fori(0, FT // 2) as i:
                for b in range(2):
                    dst = hid[:, :, bass.ds(2 * i + b, 1), :].rearrange("t p a c -> p t (a c)")
                    sp.wait_ge(out_made, 2 * i + b + 1)
                    sp.dma_start(dst, out[:, b].rearrange("p (t c) -> p t c", c=P)).then_inc(stored[b], 16)
                    sp.wait_ge(stored[b], 16 * i + 16)
                    sp.sem_inc(out_free, 1)

        @block.gpsimd
        def _(pool):
            def load(m, b):
                pool.dma_start(w_raw[:, b, :], w_gate_up[bass.ds(m, 1)].rearrange("a p f -> p (a f)")).then_inc(w_loaded[b], 16)

            def split(i, b):
                m = 2 * i + b
                pool.wait_ge(w_loaded[b], 16 * i + 16)
                if b:
                    pool.wait_ge(up_free, i + 1)
                else:
                    pool.wait_ge(gate_free, i + 1)
                pool.tensor_tensor(w_hi[:, b, :], w_raw[:, b, :], zero[:, 0:1].broadcast_to([P, KD * P]),
                                   ALU.add).then_inc(w_hi_done, 1)
                pool.wait_ge(w_hi_done, m + 1)
                pool.tensor_tensor(w_lo[:, b, :], w_raw[:, b, :], w_hi[:, b, :].bitcast(F32),
                                   ALU.subtract).then_inc(w_lo_done, 1)

            pool.memset(zero[:, :], 0.0).then_inc(zeroed, 1)
            pool.wait_ge(zeroed, 1)
            load(0, 0)
            load(1, 1)
            with pool.Fori(0, FT - 1) as i:
                for b in range(2):
                    split(i, b)
                    pool.wait_ge(w_lo_done, 2 * i + b + 1)
                    load(2 * i + b + 2, b)
            for b in range(2):
                split(FT - 1, b)

        @block.tensor
        def _(pe):
            with pe.Fori(0, FT) as i:
                for b in range(2):
                    pe.wait_ge(w_lo_done, 2 * i + b + 1)
                    pe.wait_ge(up_free if b else gate_free, i + 1)
                    for k in range(KD):
                        pe.wait_ge(x_lo_done, k + 1)
                        ws = slice(k * P, (k + 1) * P)
                        for t in range(BLOCKS):
                            ts = slice(t * NTOK, (t + 1) * NTOK)
                            acc = h_ps[:, b, t, :]
                            pe.matmul(acc, w_lo[:, b, ws], x_hi[:, k, ts], start=(k == 0), stop=False)
                            pe.matmul(acc, w_hi[:, b, ws], x_lo[:, k, ts], start=False, stop=False)
                            last = pe.matmul(acc, w_hi[:, b, ws], x_hi[:, k, ts], start=False, stop=(k == KD - 1))
                    last.then_inc(made, 1)

        @block.scalar
        def _(act):
            act.sem_inc(gate_free, 1)
            for k in range(KD):
                act.wait_ge(x_loaded[k % 2], 16 * (k // 2 + 1))
                act.activation(x_hi[:, k, :], x_raw[:, k % 2, :], ACT.Copy).then_inc(x_hi_done, 1)
            act.preload_act_table(ACT.Silu)
            with act.Fori(0, FT // 2) as i:
                for b in range(2):
                    act.wait_ge(made, 4 * i + 2 * b + 1)
                    act.wait_ge(out_free, 2 * i + b + 1)
                    act.activation(out[:, b], h_ps[:, 0].rearrange("p a t -> p (a t)"), ACT.Silu).then_inc(silu_done, 1)
                    act.wait_ge(silu_done, 2 * i + b + 1)
                    act.sem_inc(gate_free, 1)

        @block.vector
        def _(dve):
            dve.sem_inc(up_free, 1)
            for k in range(KD):
                dve.wait_ge(x_hi_done, k + 1)
                dve.tensor_tensor(x_lo[:, k, :], x_raw[:, k % 2, :], x_hi[:, k, :].bitcast(F32),
                                  ALU.subtract).then_inc(x_lo_done, 1)
            with dve.Fori(0, FT // 2) as i:
                for b in range(2):
                    dve.wait_ge(made, 4 * i + 2 * b + 2)
                    dve.wait_ge(silu_done, 2 * i + b + 1)
                    dve.tensor_tensor(out[:, b], out[:, b], h_ps[:, 1].rearrange("p a t -> p (a t)"), ALU.mult).then_inc(out_made, 1)
                    dve.wait_ge(out_made, 2 * i + b + 1)
                    dve.sem_inc(up_free, 1)


def hold(eng, begun):
    eng.sem_inc(begun, 1)


def over_tiles(loop, first, tile, last):
    first(0, 0)
    tile(0, 1)
    tile(0, 2)
    with loop(1, TILES // 2 - 1) as i:
        tile(i, 1)
        tile(i, 2)
    tile(TILES // 2 - 1, 1)
    last(TILES // 2 - 1, 2)


class TokenProduct:

    def __init__(self, nc, s, K, lhs, weights, w_raw, accs):
        self.nc, self.K, self.lhs, self.weights, self.w_raw = nc, K, lhs, weights, w_raw
        self.CH = K // 2
        self.accs = accs
        self.w_hi = s.sb("w_hi", [P, K, D_MODEL], F32R)
        self.w_lo = s.sb("w_lo", [P, K, D_MODEL], F32R)
        self.a_raw = s.sb("a_raw", [P, 2, 2 * P])
        self.a_hi = s.sb("a_hi", [P, 2, 2 * P], F32R)
        self.a_lo = s.sb("a_lo", [P, 2, 2 * P], F32R)
        self.w_loaded = [s.sem(f"w_loaded{b}") for b in range(len(w_raw))]
        self.w_hi_done, self.w_lo_done = s.sem("w_hi_done"), s.sem("w_lo_done")
        self.a_loaded = [s.sem(f"a_loaded{b}") for b in range(2)]
        self.a_hi_done, self.a_lo_done = s.sem("a_hi_done"), s.sem("a_lo_done")
        self.a_used = s.sem("a_used")

    def chunk(self, i, b, c):
        n = self.CH * b + c
        return 2 * self.CH * i + n, n % 2, self.CH * i + n // 2 + 1

    def product_done(self, eng, i, b):
        eng.wait_ge(self.a_used, 2 * self.CH * i + self.CH * (b + 1))

    def load_weights(self, eng):
        for k in range(self.K):
            ring = len(self.w_raw)
            reached(eng, self.w_lo_done, k + 1 - ring)
            eng.dma_start(self.w_raw[k % ring], self.weights[k]).then_inc(self.w_loaded[k % ring], 16)

    def load(self, eng, i, b):
        for c in range(self.CH):
            n, slot, _ = self.chunk(i, b, c)
            src = self.lhs(2 * i + b, 2 * c)
            reached(eng, self.a_lo_done, n - 1)
            eng.dma_start(self.a_raw[:, slot].rearrange("p (k t) -> p k t", k=2), src).then_inc(self.a_loaded[slot], 16)

    def high(self, act, i, b, c, with_weights=False):
        n, slot, loads = self.chunk(i, b, c)
        if with_weights:
            for k in (2 * c, 2 * c + 1):
                ring = len(self.w_raw)
                act.wait_ge(self.w_loaded[k % ring], 16 * (k // ring + 1))
                act.activation(self.w_hi[:, k], self.w_raw[k % ring], ACT.Copy).then_inc(self.w_hi_done, 1)
        act.wait_ge(self.a_loaded[slot], 16 * loads)
        reached(act, self.a_used, n - 1)
        act.activation(self.a_hi[:, slot], self.a_raw[:, slot], ACT.Copy).then_inc(self.a_hi_done, 1)

    def low(self, dve, i, b, c, with_weights=False):
        n, slot, _ = self.chunk(i, b, c)
        if with_weights:
            for k in (2 * c, 2 * c + 1):
                dve.wait_ge(self.w_hi_done, k + 1)
                dve.tensor_tensor(self.w_lo[:, k], self.w_raw[k % len(self.w_raw)], self.w_hi[:, k].bitcast(F32),
                                  ALU.subtract).then_inc(self.w_lo_done, 1)
        dve.wait_ge(self.a_hi_done, n + 1)
        dve.tensor_tensor(self.a_lo[:, slot], self.a_raw[:, slot], self.a_hi[:, slot].bitcast(F32),
                          ALU.subtract).then_inc(self.a_lo_done, 1)

    def product(self, pe, i, b, acc_free):
        reached(pe, acc_free, 2 * i + b - 1)
        for c in range(self.CH):
            n, slot, _ = self.chunk(i, b, c)
            if isinstance(i, int) and i == 0 and b == 0:
                pe.wait_ge(self.w_lo_done, 2 * c + 2)
            pe.wait_ge(self.a_lo_done, n + 1)
            for k in (2 * c, 2 * c + 1):
                k0, k1, acc = next(a for a in self.accs if a[0] <= k <= a[1])
                rows = slice(P * (k % 2), P * (k % 2) + P)
                for half in range(2):
                    cols = slice(NTOK * half, NTOK * (half + 1))
                    to = acc[:, b % 2, cols]
                    pe.matmul(to, self.a_lo[:, slot, rows], self.w_hi[:, k, cols], start=(k == k0), stop=False)
                    pe.matmul(to, self.a_hi[:, slot, rows], self.w_lo[:, k, cols], start=False, stop=False)
                    last = pe.matmul(to, self.a_hi[:, slot, rows], self.w_hi[:, k, cols], start=False, stop=(k == k1))
            last.then_inc(self.a_used, 1)


def project_norm(nc, stage, K, lhs, weights, res, gain, bias, x_out, xT_out):
    with ExitStack() as ctx:
        s = Scope(nc, ctx, stage)
        y = s.sb("y", [P, 2, D_MODEL])
        old = s.sb("old", [P, D_MODEL])
        g_all = s.sb("g_all", [P, D_MODEL])
        b_all = s.sb("b_all", [P, D_MODEL])
        ident = s.sb("ident", [P, P])
        stats = s.sb("stats", [P, 2, 6])
        mean = s.sb("mean", [P, 2])
        eps = s.sb("eps", [P, 1])
        root = s.sb("root", [P, 4])
        rstd = root[:, 3:4]
        xT = s.sb("xT", [P, KD, P])
        acc = s.ps("acc", [P, 2, D_MODEL])
        xT_ps = s.ps("xT_ps", [P, KD, P])
        w_raw = [y[:, 0], y[:, 1], old[:], xT[:].rearrange("p k t -> p (k t)")]
        tp = TokenProduct(nc, s, K, lhs, weights, w_raw, [(0, K - 1, acc)])

        const_sem = s.sem("consts")
        small_loaded = s.sem("small_loaded")
        res_loaded = s.sem("res_loaded")
        added = s.sem("added")
        stats_done, mean_done, root_done, newton, normed = (s.sem(n) for n in ("stats_done", "mean_done", "root_done", "newton", "normed"))
        gained, y_done = s.sem("gained"), s.sem("y_done")
        x_stored, xT_stored = [s.sem(f"x_stored{b}") for b in range(2)], s.sem("xT_stored")
        turned, xT_copied = s.sem("turned"), s.sem("xT_copied")
        dve_holds, pool_holds, sp_holds = s.sem("dve_holds"), s.sem("pool_holds"), s.sem("sp_holds")
        block = ctx.enter_context(nc.Block())
        LAST = TILES // 2 - 1

        @block.sync
        def _(sp):
            sp.dma_start(g_all[:], gain.partition_broadcast(P)).then_inc(small_loaded, 16)
            sp.dma_start(b_all[:], bias.partition_broadcast(P)).then_inc(small_loaded, 16)
            def tile(i, b):
                t = 2 * i + b
                tp.load(sp, i, b)
                if isinstance(i, int) and t == 0:
                    sp.wait_ge(tp.w_lo_done, K)
                reached(sp, added, t)
                hold(sp, sp_holds)
                sp.dma_start(old[:], res[bass.ds(P * t, P)]).then_inc(res_loaded, 16)

            tile(0, 0)
            tile(0, 1)
            with sp.Fori(1, TILES // 2) as i:
                tile(i, 0)
                tile(i, 1)

        @block.gpsimd
        def _(pool):
            def finish(i, b):
                t, at = 2 * i + b, b % 2
                pool.wait_ge(normed, t + 1)
                pool.tensor_tensor(y[:, at], y[:, at], g_all[:], ALU.mult).then_inc(gained, 1)
                pool.wait_ge(gained, t + 1)
                pool.tensor_tensor(y[:, at], y[:, at], b_all[:], ALU.add).then_inc(y_done, 1)
                dst = x_out[bass.ds(P * t, P)]
                pool.wait_ge(y_done, t + 1)
                hold(pool, pool_holds)
                pool.dma_start(dst, y[:, at]).then_inc(x_stored[at], 16)

            pool.memset(ident[:], 0.0).then_inc(const_sem, 1)
            pool.wait_ge(const_sem, 1)
            pool.affine_select(out=ident[:], in_=ident[:], compare_op=ALU.not_equal, fill=1.0, base=0, pattern=[[-1, P]],
                               channel_multiplier=1).then_inc(const_sem, 1)
            pool.memset(eps[:], LN_EPS).then_inc(const_sem, 1)
            tp.load_weights(pool)
            pool.wait_ge(small_loaded, 32)
            finish(0, 0)
            with pool.Fori(0, LAST) as i:
                finish(i, 1)
                finish(i, 2)
            finish(LAST, 1)
            for b in range(2):
                pool.wait_ge(x_stored[b], 16 * (TILES // 2))

        @block.tensor
        def _(pe):
            def turn(i, b):
                t = 2 * i + b
                pe.wait_ge(y_done, t + 1)
                reached(pe, xT_copied, t)
                for k in range(KD):
                    last = pe.transpose(xT_ps[:, k], y[:, b % 2, P * k:P * (k + 1)], ident[:])
                last.then_inc(turned, 1)

            def tile(i, b):
                tp.product(pe, i, b, added)
                turn(i, b - 1)

            over_tiles(pe.Fori, lambda i, b: tp.product(pe, i, b, added), tile, lambda i, b: turn(i, b - 1))

        @block.scalar
        def _(act):
            def out(i, b):
                t = 2 * i + b
                act.wait_ge(turned, t + 1)
                reached(act, xT_stored, 16 * t)
                act.activation(xT[:], xT_ps[:], ACT.Copy).then_inc(xT_copied, 1)
                dst = xT_out[:, :, bass.ds(P * t, P)].rearrange("a p t -> p a t")
                act.wait_ge(xT_copied, t + 1)
                act.dma_start(dst, xT[:]).then_inc(xT_stored, 16)

            def deviation(i, b):
                act.wait_ge(mean_done, 2 * i + b + 1)
                act.activation(root[:, 0:1], mean[:, 1:2], ACT.Sqrt, bias=eps[:, 0:1]).then_inc(root_done, 1)

            def tile(i, b):
                for c in range(tp.CH):
                    tp.high(act, i, b, c)
                    if c == 1:
                        if b == 2:
                            out(i, 0)
                        elif not (isinstance(i, int) and i == 0):
                            out(i - 1, 1)
                        deviation(i, b - 1)

            act.preload_act_table(ACT.Sqrt)
            act.wait_ge(const_sem, 3)

            over_tiles(act.Fori, lambda i, b: [tp.high(act, i, b, c, True) for c in range(tp.CH)], tile,
                       lambda i, b: [out(i, b - 2), deviation(i, b - 1), out(i, b - 1)])
            act.wait_ge(xT_stored, 16 * TILES)

        @block.vector
        def _(dve):
            def add(i, b):
                at = b % 2
                tp.product_done(dve, i, b)
                dve.wait_ge(res_loaded, 32 * i + 16 * b + 16)
                reached(dve, x_stored[at], 16 * i + 16 * (b // 2))
                reached(dve, turned, 2 * i + b - 1)
                dve.scalar_tensor_tensor(y[:, at], old[:], ALPHA, acc[:, at], ALU.mult, ALU.add).then_inc(added, 1)

            def norm(i, b):
                t, at = 2 * i + b, b % 2
                dve.wait_ge(added, t + 1)
                for half in range(2):
                    dve.bn_stats(stats[:, half], y[:, at, NTOK * half:NTOK * (half + 1)]).then_inc(stats_done, 1)
                dve.wait_ge(stats_done, 2 * t + 2)
                hold(dve, dve_holds)
                dve.bn_aggr(mean[:], stats[:].rearrange("p a c -> p (a c)")).then_inc(mean_done, 1)
                dve.wait_ge(root_done, t + 1)
                dve.tensor_scalar(mean[:, 1:2], mean[:, 1:2], LN_EPS, -0.5, ALU.add, ALU.mult).then_inc(newton, 1)
                dve.reciprocal(root[:, 1:2], root[:, 0:1]).then_inc(newton, 1)
                dve.wait_ge(newton, 4 * t + 2)
                dve.scalar_tensor_tensor(root[:, 2:3], root[:, 1:2], mean[:, 1:2], root[:, 1:2], ALU.mult, ALU.mult).then_inc(newton, 1)
                dve.wait_ge(newton, 4 * t + 3)
                dve.scalar_tensor_tensor(rstd, root[:, 2:3], 1.5, root[:, 1:2], ALU.add, ALU.mult).then_inc(newton, 1)
                dve.wait_ge(newton, 4 * t + 4)
                dve.tensor_scalar(y[:, at], y[:, at], mean[:, 0:1], rstd, ALU.subtract, ALU.mult).then_inc(normed, 1)

            def tile(i, b):
                for c in range(tp.CH):
                    tp.low(dve, i, b, c)
                    if c == 0:
                        add(i, b - 1)
                    if c == 1:
                        norm(i, b - 1)

            over_tiles(dve.Fori, lambda i, b: [tp.low(dve, i, b, c, True) for c in range(tp.CH)], tile,
                       lambda i, b: [add(i, b - 1), norm(i, b - 1)])


def embed(nc, lhs, weights, x, out):
    K = KD + PLE_DIM // P
    with ExitStack() as ctx:
        s = Scope(nc, ctx, "em")
        w_raw = s.sb("w_raw", [P, 4, D_MODEL])
        xt = s.sb("xt", [P, 2, D_MODEL])
        y = s.sb("y", [P, 2, D_MODEL])
        gate_ps = s.ps("gate_ps", [P, 2, D_MODEL])
        ple_ps = s.ps("ple_ps", [P, 2, D_MODEL])
        tp = TokenProduct(nc, s, K, lhs, weights, [w_raw[:, n] for n in range(4)], [(0, KD - 1, gate_ps), (KD, K - 1, ple_ps)])
        x_loaded = [s.sem(f"x_loaded{b}") for b in range(2)]
        gate_done = s.sem("gate_done")
        gated = s.sem("gated")
        summed = s.sem("summed")
        pool_holds = s.sem("pool_holds")
        stored = [s.sem(f"stored{b}") for b in range(2)]
        block = ctx.enter_context(nc.Block())

        @block.sync
        def _(sp):
            tp.load(sp, 0, 0)
            tp.load(sp, 0, 1)
            with sp.Fori(1, TILES // 2) as i:
                tp.load(sp, i, 0)
                tp.load(sp, i, 1)

        @block.gpsimd
        def _(pool):
            def load_x(t, b):
                pool.dma_start(xt[:, b], x[bass.ds(P * t, P)]).then_inc(x_loaded[b], 16)

            def finish(i, b, more):
                t = 2 * i + b
                pool.wait_ge(x_loaded[b], 16 * i + 16)
                pool.wait_ge(gated, t + 1)
                pool.tensor_tensor(y[:, b], y[:, b], xt[:, b], ALU.add).then_inc(summed, 1)
                dst = out[bass.ds(P * t, P)]
                pool.wait_ge(summed, t + 1)
                hold(pool, pool_holds)
                pool.dma_start(dst, y[:, b]).then_inc(stored[b], 16)
                if more:
                    load_x(t + 2, b)

            tp.load_weights(pool)
            load_x(0, 0)
            load_x(1, 1)
            with pool.Fori(0, TILES // 2 - 1) as i:
                finish(i, 0, True)
                finish(i, 1, True)
            for b in range(2):
                finish(TILES // 2 - 1, b, False)
            for b in range(2):
                pool.wait_ge(stored[b], 16 * (TILES // 2))

        @block.tensor
        def _(pe):
            product = lambda i, b: tp.product(pe, i, b, gated)
            over_tiles(pe.Fori, product, product, lambda i, b: None)

        @block.scalar
        def _(act):
            def gate(i, b):
                at = b % 2
                tp.product_done(act, i, b)
                reached(act, stored[at], 16 * i + 16 * (b // 2))
                act.activation(y[:, at], gate_ps[:, at], ACT.Sigmoid).then_inc(gate_done, 1)

            def tile(i, b):
                for c in range(tp.CH):
                    tp.high(act, i, b, c)
                    if c == 1:
                        gate(i, b - 1)

            act.preload_act_table(ACT.Sigmoid)
            over_tiles(act.Fori, lambda i, b: [tp.high(act, i, b, c, True) for c in range(tp.CH)], tile,
                       lambda i, b: gate(i, b - 1))

        @block.vector
        def _(dve):
            def multiply(i, b):
                at = b % 2
                dve.wait_ge(gate_done, 2 * i + b + 1)
                dve.tensor_tensor(y[:, at], y[:, at], ple_ps[:, at], ALU.mult).then_inc(gated, 1)

            def tile(i, b):
                for c in range(tp.CH):
                    tp.low(dve, i, b, c)
                    if c == 1:
                        multiply(i, b - 1)

            over_tiles(dve.Fori, lambda i, b: [tp.low(dve, i, b, c, True) for c in range(tp.CH)], tile,
                       lambda i, b: multiply(i, b - 1))


def lay_in(x, w_in, conv_w):
    xT = np.ascontiguousarray(x[0].T.reshape(KD, P, SEQ).transpose(1, 0, 2))
    w = w_in[0]
    cuts = np.cumsum([4 * HEADS * P, HEADS, HEADS, Q_LORA, KV_LORA, ROPE])
    qkvz, b, a, cq, ckv, kr = np.split(w, cuts[:-1], axis=1)
    pad = np.zeros((D_MODEL, N_IN * P - w.shape[1]), w.dtype)
    w = np.concatenate([qkvz, cq, ckv, kr, b, a, pad], axis=1)
    w = w.reshape(KD, P, N_IN, P).transpose(2, 1, 0, 3).reshape(N_IN, P, KD * P)
    taps = conv_w[0].T.reshape(T_Z, P, CONV_WIDTH).transpose(1, 0, 2).reshape(P, T_Z * CONV_WIDTH)
    return xT, np.ascontiguousarray(w), np.ascontiguousarray(taps)


def lay_latents(w_uq, w_ukv, q_norm_g, kv_norm_g):
    uq = w_uq[0].reshape(KQ, P, HEADS, P + ROPE)
    uq = np.concatenate([uq[..., P:].reshape(KQ, P, -1), uq[..., :P].reshape(KQ, P, -1)], axis=2)
    ukv = w_ukv[0].reshape(KC, P, HEADS, 2, P).transpose(0, 1, 3, 2, 4).reshape(KC, P, -1)
    gains = np.concatenate([q_norm_g[0].reshape(KQ, P), kv_norm_g[0].reshape(KC, P)]).T
    return (np.ascontiguousarray(uq.transpose(1, 0, 2)), np.ascontiguousarray(ukv.transpose(1, 0, 2)),
            np.ascontiguousarray(gains))


def rotary_frequencies():
    f = ROPE_THETA ** (-np.arange(0, ROPE, 2) / ROPE)
    return np.tile(f.astype(np.float32), P // (ROPE // 2)).reshape(P, 1)


def lay_tail(w_gate_up, w_ple_gate, w_ple, p):
    gu = w_gate_up[0].reshape(KD, P, 2, FT, P).transpose(3, 2, 1, 0, 4).reshape(2 * FT, P, KD * P)
    ple = np.concatenate([w_ple_gate[0], w_ple[0]]).reshape(-1, P, D_MODEL)
    pT = p[0, 0].T.reshape(PLE_DIM // P, P, SEQ)
    return np.ascontiguousarray(gu), np.ascontiguousarray(ple), np.ascontiguousarray(pT)


def tokens_of(xT):
    return lambda t, k: xT[k:k + 2, :, bass.ds(P * t, P)].rearrange("a p t -> p a t")


def build(nc, a, out):
    def scratch(name, shape, dt=F32):
        return nc.dram_tensor(f"scratch_{name}", shape, dt, kind="Internal").ap()

    hT = scratch("hT", [N_IN, P, SEQ])
    shapes = {"qnT": [HEADS, P, SEQ], "qrT": [HEADS, ROPE, SEQ], "knT": [HEADS, P, SEQ], "krT": [ROPE, SEQ],
              "v": [TILES, P, HEADS * P]}
    made = {n + half: scratch(n + half, shape, F32R) for n, shape in shapes.items() for half in ("_hi", "_lo")}
    mixT = scratch("mixT", [2 * HEADS, P, SEQ])
    x1, x1T = scratch("x1", [SEQ, D_MODEL]), scratch("x1T", [KD, P, SEQ])
    hid = scratch("hid", [TILES, P, FT, P])
    x2, x2T = scratch("x2", [SEQ, D_MODEL]), scratch("x2T", [KD, P, SEQ])

    project_in(nc, a["xT"], a["w_in"], a["taps"], hT)
    latents(nc, hT, a["positions"][0], a["inv_freq"], a["w_uq"], a["w_ukv"], a["gains"], made)
    delta_rule(nc, hT, a["a_log"][0], a["dt_bias"][0], a["gdn_norm_g"], mixT)
    attention(nc, made, mixT)
    project_norm(nc, "op", KD, tokens_of(mixT), a["w_out"], a["x"], a["ln1_g"][0], a["ln1_b"][0], x1, x1T)
    feed_in(nc, x1T, a["w_gate_up"], hid)
    hidden = lambda t, k: hid[bass.ds(t, 1), :, k:k + 2, :].rearrange("x p a c -> p (x a) c")
    project_norm(nc, "fd", FT, hidden, a["w_down"], x1, a["ln2_g"][0], a["ln2_b"][0], x2, x2T)
    from_x, from_p = tokens_of(x2T), tokens_of(a["pT"])
    embed(nc, lambda t, k: from_x(t, k) if k < KD else from_p(t, k - KD), a["w_ple"], x2, out)


def lay_all(i):
    xT, w_in, taps = lay_in(i["x"], i["w_in"], i["conv_w"])
    uq, ukv, gains = lay_latents(i["w_uq"], i["w_ukv"], i["q_norm_g"], i["kv_norm_g"])
    gate_up, ple, pT = lay_tail(i["w_gate_up"], i["w_ple_gate"], i["w_ple"], i["p"])
    return {
        "x": i["x"][0], "xT": xT, "w_in": w_in, "taps": taps,
        "positions": i["positions"], "inv_freq": rotary_frequencies(), "w_uq": uq, "w_ukv": ukv, "gains": gains,
        "a_log": i["a_log"], "dt_bias": i["dt_bias"], "gdn_norm_g": i["gdn_norm_g"].reshape(P, 1),
        "w_out": i["w_out"][0].reshape(KD, P, D_MODEL), "ln1_g": i["ln1_g"], "ln1_b": i["ln1_b"],
        "w_gate_up": gate_up, "w_down": i["w_down"][0].reshape(FT, P, D_MODEL), "ln2_g": i["ln2_g"], "ln2_b": i["ln2_b"],
        "w_ple": ple, "pT": pT,
    }


def kernel(**inputs):
    import concourse.bacc as bacc
    from concourse.bass_utils import run_bass_kernel_spmd

    nc = bacc.Bacc("TRN2", target_bir_lowering=False, num_devices=1)
    arrays = {n: np.ascontiguousarray(v) for n, v in lay_all({n: np.asarray(v) for n, v in inputs.items()}).items()}
    a = {n: nc.dram_tensor(n, v.shape, mybir.dt.from_np(v.dtype), kind="ExternalInput").ap() for n, v in arrays.items()}
    out = nc.dram_tensor("out", [SEQ, D_MODEL], F32, kind="ExternalOutput").ap()
    build(nc, a, out)
    r = run_bass_kernel_spmd(nc, [arrays], core_ids=[0])
    return r.results[0]["out"].reshape(1, SEQ, D_MODEL)
```

```python
from contextlib import ExitStack

import numpy as np

import concourse.bass as bass
from concourse import mybir

F32 = mybir.dt.float32
F32R = mybir.dt.float32r
I32 = mybir.dt.int32
ACT = mybir.ActivationFunctionType
ALU = mybir.AluOpType
AX = mybir.AxisListType

P = 128
D_MODEL = 1024
SEQ = 2048
CHUNK = 64
PLE_DIM = 256
HEADS = 4
ROPE = 64
Q_LORA = 384
KV_LORA = 256
D_FF = 2816
CONV_WIDTH = 4
ROPE_THETA = 10000.0
ALPHA = 2.0 ** 0.25
LN_EPS = 1e-5
RMS_EPS = 1e-6
NTOK = 512
BLOCKS = SEQ // NTOK
TILES = SEQ // P
KD = D_MODEL // P
KQ = Q_LORA // P
KC = KV_LORA // P
FT = D_FF // P
T_Q, T_K, T_V, T_Z = 0, HEADS, 2 * HEADS, 3 * HEADS
T_CQ = 4 * HEADS
T_CKV = T_CQ + KQ
T_KR = T_CKV + KC
N_IN = T_KR + 1


class Scope:

    def __init__(self, nc, ctx, stage):
        self.nc, self.ctx, self.stage, self.sems = nc, ctx, stage, []
        ctx.callback(self.clear)

    def sb(self, name, shape, dt=F32):
        return self.ctx.enter_context(self.nc.sbuf_tensor(f"{self.stage}_{name}", shape, dt))

    def ps(self, name, shape):
        return self.ctx.enter_context(self.nc.psum_tensor(f"{self.stage}_{name}", shape, F32))

    def sem(self, name):
        self.sems.append(self.nc.alloc_semaphore(f"{self.stage}_{name}"))
        return self.sems[-1]

    def clear(self):
        self.nc.clear_and_free_semaphores(self.sems)
        self.nc.all_engine_barrier()


def reached(eng, sem, count):
    if not (isinstance(count, int) and count <= 0):
        eng.wait_ge(sem, count)


def project_in(nc, xT, w_in, conv_w, hT):
    with ExitStack() as ctx:
        s = Scope(nc, ctx, "in")
        x_raw = s.sb("x_raw", [P, 2, SEQ])
        x_hi = s.sb("x_hi", [P, KD, SEQ], F32R)
        x_lo = s.sb("x_lo", [P, KD, SEQ], F32R)
        w_raw = s.sb("w_raw", [P, 2, KD * P])
        w_hi = s.sb("w_hi", [P, 2, KD * P], F32R)
        w_lo = s.sb("w_lo", [P, 2, KD * P], F32R)
        taps = s.sb("taps", [P, T_Z * CONV_WIDTH])
        h_pad = s.sb("h_pad", [P, SEQ + CONV_WIDTH - 1])
        zero = s.sb("zero", [P, 1])
        conv = s.sb("conv", [P, SEQ])
        out = s.sb("out", [P, SEQ])
        h_ps = s.ps("h_ps", [P, 2, BLOCKS, NTOK])

        x_loaded = [s.sem(f"x_loaded{b}") for b in range(2)]
        x_hi_done = s.sem("x_hi_done")
        x_lo_done = s.sem("x_lo_done")
        w_loaded = [s.sem(f"w_loaded{b}") for b in range(2)]
        w_hi_done = s.sem("w_hi_done")
        w_lo_done = s.sem("w_lo_done")
        taps_loaded = s.sem("taps_loaded")
        h_made = s.sem("h_made")
        h_ps_free = s.sem("h_ps_free")
        zeroed = s.sem("zeroed")
        h_copied = s.sem("h_copied")
        conv_step = s.sem("conv_step")
        conv_free = s.sem("conv_free")
        out_made = s.sem("out_made")
        out_free = s.sem("out_free")
        stored = s.sem("stored")
        block = ctx.enter_context(nc.Block())

        @block.sync
        def _(sp):
            sp.dma_start(taps[:, :], conv_w).then_inc(taps_loaded, 16)
            for k in range(KD):
                if k >= 2:
                    sp.wait_ge(x_lo_done, k - 1)
                sp.dma_start(x_raw[:, k % 2, :], xT[:, k, :]).then_inc(x_loaded[k % 2], 16)
            sp.sem_inc(out_free, 1)
            with sp.Fori(0, N_IN) as m:
                sp.wait_ge(out_made, m + 1)
                sp.dma_start(hT[bass.ds(m, 1)].rearrange("a p t -> p (a t)"), out[:, :]).then_inc(stored, 16)
                sp.wait_ge(stored, 16 * m + 16)
                sp.sem_inc(out_free, 1)

        @block.gpsimd
        def _(pool):
            def load(m, b):
                pool.dma_start(w_raw[:, b, :], w_in[bass.ds(m, 1)].rearrange("a p f -> p (a f)")).then_inc(w_loaded[b], 16)

            def split(i, b):
                m = 2 * i + b
                pool.wait_ge(w_loaded[b], 16 * i + 16)
                pool.wait_ge(h_ps_free, m + 1)
                pool.tensor_tensor(w_hi[:, b, :], w_raw[:, b, :], zero[:, 0:1].broadcast_to([P, KD * P]),
                                   ALU.add).then_inc(w_hi_done, 1)
                pool.wait_ge(w_hi_done, m + 1)
                pool.tensor_tensor(w_lo[:, b, :], w_raw[:, b, :], w_hi[:, b, :].bitcast(F32),
                                   ALU.subtract).then_inc(w_lo_done, 1)

            pool.memset(zero[:, :], 0.0).then_inc(zeroed, 1)
            pool.wait_ge(zeroed, 1)
            load(0, 0)
            load(1, 1)
            with pool.Fori(0, N_IN // 2 - 1) as i:
                for b in range(2):
                    split(i, b)
                    pool.wait_ge(w_lo_done, 2 * i + b + 1)
                    load(2 * i + b + 2, b)
            for b in range(2):
                split(N_IN // 2 - 1, b)

        @block.tensor
        def _(pe):
            def products(b, k):
                ws = slice(k * P, (k + 1) * P)
                for t in range(BLOCKS):
                    ts = slice(t * NTOK, (t + 1) * NTOK)
                    acc = h_ps[:, b, t, :]
                    pe.matmul(acc, w_lo[:, b, ws], x_hi[:, k, ts], start=(k == 0), stop=False)
                    pe.matmul(acc, w_hi[:, b, ws], x_lo[:, k, ts], start=False, stop=False)
                    last = pe.matmul(acc, w_hi[:, b, ws], x_hi[:, k, ts], start=False, stop=(k == KD - 1))
                return last

            for k in range(KD):
                pe.wait_ge(x_lo_done, k + 1)
                for b in range(2):
                    if k == 0:
                        pe.wait_ge(w_lo_done, b + 1)
                    last = products(b, k)
                    if k == KD - 1:
                        last.then_inc(h_made, 1)
            with pe.Fori(1, N_IN // 2) as i:
                for b in range(2):
                    m = 2 * i + b
                    pe.wait_ge(w_lo_done, m + 1)
                    pe.wait_ge(h_ps_free, m + 1)
                    for k in range(KD):
                        last = products(b, k)
                    last.then_inc(h_made, 1)

        @block.scalar
        def _(act):
            act.sem_inc(h_ps_free, 2)
            act.sem_inc(conv_free, 1)
            for k in range(KD):
                act.wait_ge(x_loaded[k % 2], 16 * (k // 2 + 1))
                act.activation(x_hi[:, k, :], x_raw[:, k % 2, :], ACT.Copy).then_inc(x_hi_done, 1)

            def conv_tile(i, b):
                m = 2 * i + b
                act.wait_ge(h_made, m + 1)
                act.wait_ge(conv_step, CONV_WIDTH * m + 1)
                act.activation(h_pad[:, CONV_WIDTH - 1:], h_ps[:, b].rearrange("p a t -> p (a t)"),
                               ACT.Copy).then_inc(h_copied, 1)
                act.wait_ge(h_copied, m + 1)
                act.sem_inc(h_ps_free, 1)
                act.wait_ge(conv_step, CONV_WIDTH * (m + 1) + 1)
                act.wait_ge(out_free, m + 1)
                act.activation(out[:, :], conv[:, :], ACT.Silu).then_inc(out_made, 1)
                act.wait_ge(out_made, m + 1)
                act.sem_inc(conv_free, 1)

            def plain_tile(i, b, func):
                m = 2 * i + b
                act.wait_ge(h_made, m + 1)
                act.wait_ge(out_free, m + 1)
                act.activation(out[:, :], h_ps[:, b].rearrange("p a t -> p (a t)"), func).then_inc(out_made, 1)
                act.wait_ge(out_made, m + 1)
                act.sem_inc(h_ps_free, 1)

            act.preload_act_table(ACT.Silu)
            for first, last, tile in ((0, T_Z, conv_tile),
                                      (T_Z, T_CQ, lambda i, b: plain_tile(i, b, ACT.Silu)),
                                      (T_CQ, N_IN, lambda i, b: plain_tile(i, b, ACT.Copy))):
                with act.Fori(first // 2, last // 2) as i:
                    for b in range(2):
                        tile(i, b)

        @block.vector
        def _(dve):
            for k in range(KD):
                dve.wait_ge(x_hi_done, k + 1)
                dve.tensor_tensor(x_lo[:, k, :], x_raw[:, k % 2, :], x_hi[:, k, :].bitcast(F32),
                                  ALU.subtract).then_inc(x_lo_done, 1)
            dve.wait_ge(taps_loaded, 16)
            dve.memset(h_pad[:, 0:CONV_WIDTH - 1], 0.0).then_inc(conv_step, 1)
            with dve.Fori(0, T_Z // 2) as i:
                for b in range(2):
                    m = 2 * i + b
                    dve.wait_ge(h_copied, m + 1)
                    for j in range(CONV_WIDTH):
                        if j == 0:
                            dve.wait_ge(conv_free, m + 1)
                            op = dve.tensor_scalar(conv[:, :], h_pad[:, 0:SEQ], taps[:, bass.ds(CONV_WIDTH * m, 1)], None, ALU.mult)
                        else:
                            dve.wait_ge(conv_step, CONV_WIDTH * m + j + 1)
                            op = dve.scalar_tensor_tensor(conv[:, :], h_pad[:, j:j + SEQ], taps[:, bass.ds(CONV_WIDTH * m + j, 1)],
                                                          conv[:, :], ALU.mult, ALU.add)
                        op.then_inc(conv_step, 1)


def split_resident(s, act, dve, name, raw, hi, lo, loaded):
    hi_done, lo_done = s.sem(f"{name}_hi_done"), s.sem(f"{name}_lo_done")

    def on_scalar():
        act.wait_ge(loaded, 16)
        act.activation(hi, raw, ACT.Copy).then_inc(hi_done, 1)

    def on_vector():
        dve.wait_ge(hi_done, 1)
        dve.tensor_tensor(lo, raw, hi.bitcast(F32), ALU.subtract).then_inc(lo_done, 1)

    return on_scalar, on_vector, lo_done


def latents(nc, hT, positions, inv_freq, w_uq, w_ukv, gains, made):
    NG = 14
    SCALE = float(P + ROPE) ** -0.5
    G_QN, G_KN, G_V = 2, 6, 10
    RING = 5
    MAGIC = 1.5 * 2.0 ** 23
    TWO_PI_1 = 6.28125
    TWO_PI_2 = float(np.float32(0.00193500518798828125))
    TWO_PI_3 = float(np.float32(2 * np.pi - TWO_PI_1 - TWO_PI_2))
    PI_IN = 3.1415925
    with ExitStack() as ctx:
        s = Scope(nc, ctx, "lat")
        NQ = 2 * P + HEADS * P
        KL = KQ + KC
        NKV = 2 * HEADS * P
        uq_hi = s.sb("uq_hi", [P, KQ, NQ], F32R)
        uq_lo = s.sb("uq_lo", [P, KQ, NQ], F32R)
        ukv_hi = s.sb("ukv_hi", [P, KC, NKV], F32R)
        ukv_lo = s.sb("ukv_lo", [P, KC, NKV], F32R)
        gain = s.sb("gain", [P, KQ + KC])
        freq = s.sb("freq", [P, 1])
        ones = s.sb("ones", [P, P])
        half_pi = s.sb("half_pi", [P, 1])
        eps = s.sb("eps", [P, 1])
        turn = s.sb("turn", [P, P])
        cos = s.sb("cos", [P, SEQ])
        pos = cos[:].bitcast(I32)
        ang, turns, turns_hi, part = (s.sb(n, [P, NTOK]) for n in ("ang", "turns", "turns_hi", "part"))
        sin = s.sb("sin", [P, SEQ])
        lat = s.sb("lat", [P, 2, KQ + KC, NTOK])
        kr = s.sb("kr", [ROPE, 2, NTOK])
        sq = s.sb("sq", [P, KQ + KC, NTOK])
        rstd = s.sb("rstd", [P, 2, NTOK])
        nrm_hi = s.sb("nrm_hi", [P, 2, KQ + KC, NTOK], F32R)
        nrm_lo = s.sb("nrm_lo", [P, 2, KQ + KC, NTOK], F32R)
        raw_r = s.sb("raw_r", [P, 2, NTOK])
        out = s.sb("out", [P, NG - 2, NTOK])
        flat = out[:].rearrange("p a t -> p (a t)")
        var, step_rs = sq[:, 0:2], sq[:, 2:4]
        uq_raw = flat[:, 0:KQ * NQ].rearrange("p (k n) -> p k n", k=KQ)
        ukv_raw = flat[:, KQ * NQ:KQ * NQ + KC * NKV].rearrange("p (k n) -> p k n", k=KC)
        rot = s.sb("rot", [P, 3, NTOK])
        swapped = s.sb("swapped", [P, NTOK])
        ssq_ps = s.ps("ssq_ps", [P, 2, NTOK])
        ring = s.ps("ring", [P, RING, NTOK])
        turn_ps = s.ps("turn_ps", [P, NTOK])

        uq_loaded, ukv_loaded = s.sem("uq_loaded"), s.sem("ukv_loaded")
        small_loaded, pos_loaded = s.sem("small_loaded"), s.sem("pos_loaded")
        consts = s.sem("consts")
        table = s.sem("table")
        sin_done, abs_done, cos_done = s.sem("sin_done"), s.sem("abs_done"), s.sem("cos_done")
        lat_loaded = [s.sem(f"lat_loaded{b}") for b in range(2)]
        kr_loaded = [s.sem(f"kr_loaded{b}") for b in range(2)]
        sq_done = s.sem("sq_done")
        ssq_done = s.sem("ssq_done")
        var_done, log_done, root_done, newton = (s.sem(n) for n in ("var_done", "log_done", "root_done", "newton"))
        nrm_done = s.sem("nrm_done")
        nrm_hi_done = s.sem("nrm_hi_done")
        nrm_lo_done = s.sem("nrm_lo_done")
        group_done = s.sem("group_done")
        out_copied = s.sem("out_copied")
        turned = s.sem("turned")
        cos_part = s.sem("cos_part")
        sin_part = s.sem("sin_part")
        rot_done = s.sem("rot_done")
        q_stored, k_stored, v_stored, r_stored = (s.sem(n) for n in ("q_stored", "k_stored", "v_stored", "r_stored"))
        block = ctx.enter_context(nc.Block())
        tok = [slice(t * NTOK, (t + 1) * NTOK) for t in range(BLOCKS)]
        STEPS = 19
        ROTATE = (8, 10, 12)

        uq_act, uq_dve, uq_ready = split_resident(s, nc.scalar, nc.vector, "uq", uq_raw, uq_hi[:], uq_lo[:], uq_loaded)
        ukv_act, ukv_dve, ukv_ready = split_resident(s, nc.scalar, nc.vector, "ukv", ukv_raw, ukv_hi[:], ukv_lo[:], ukv_loaded)

        @block.sync
        def _(sp):
            def load(t):
                if t >= 2:
                    sp.wait_ge(nrm_lo_done, KL * (t - 1))
                sp.dma_start(lat[:, t % 2], hT[T_CQ:T_KR, :, tok[t]].rearrange("a p t -> p a t")).then_inc(lat_loaded[t % 2], 16)

            def load_kr(t):
                if t >= 2:
                    sp.wait_ge(rot_done, 3 * (t - 1))
                sp.dma_start(kr[:, t % 2], hT[T_KR, 0:ROPE, tok[t]]).then_inc(kr_loaded[t % 2], 16)

            load(0)
            sp.dma_start(gain[:], gains).then_inc(small_loaded, 16)
            sp.dma_start(freq[:], inv_freq).then_inc(small_loaded, 16)
            sp.dma_start(pos, positions.partition_broadcast(P)).then_inc(pos_loaded, 16)
            sp.dma_start(uq_raw, w_uq).then_inc(uq_loaded, 16)
            sp.dma_start(ukv_raw, w_ukv).then_inc(ukv_loaded, 16)
            load(1)
            load_kr(0)
            load_kr(1)
            for t in range(BLOCKS):
                if t + 2 < BLOCKS:
                    load(t + 2)
                for g0, name, sem in ((0, "qnT", q_stored), (4, "knT", k_stored), (8, "v", v_stored)):
                    sp.wait_ge(out_copied, NG * t + G_QN + g0 + 4)
                    if name == "v":
                        dst = made["v"][4 * t:4 * t + 4].rearrange("a p n -> p a n")
                    else:
                        dst = made[name][:, :, tok[t]].rearrange("h p t -> p h t")
                    sp.dma_start(dst, out[:, g0:g0 + 4]).then_inc(sem, 16)
                sp.wait_ge(rot_done, 3 * (t + 1))
                for g in range(2):
                    sp.dma_start(made["qrT"][2 * g:2 * g + 2, :, tok[t]].rearrange("h p t -> (h p) t"), rot[:, g]).then_inc(r_stored, 16)
                sp.dma_start(made["krT"][:, tok[t]], rot[0:ROPE, 2]).then_inc(r_stored, 16)
                if t + 2 < BLOCKS:
                    load_kr(t + 2)
            for sem in (q_stored, k_stored, v_stored):
                sp.wait_ge(sem, 16 * BLOCKS)
            sp.wait_ge(r_stored, 48 * BLOCKS)

        @block.gpsimd
        def _(pool):
            pool.memset(ones[:], 1.0).then_inc(consts, 1)
            pool.memset(half_pi[:], float(np.pi / 2)).then_inc(consts, 1)
            pool.memset(eps[:], RMS_EPS).then_inc(consts, 1)
            pool.memset(turn[:], 0.0).then_inc(consts, 1)
            pool.wait_ge(consts, 4)
            for n, half in enumerate(range(0, P, ROPE)):
                view = turn[:, half:half + ROPE // 2]
                pool.affine_select(out=view, in_=view, compare_op=ALU.not_equal, fill=-1.0, base=-half - ROPE // 2,
                                   pattern=[[-1, ROPE // 2]], channel_multiplier=1).then_inc(consts, 1)
                view = turn[:, half + ROPE // 2:half + ROPE]
                pool.affine_select(out=view, in_=view, compare_op=ALU.not_equal, fill=1.0, base=-half,
                                   pattern=[[-1, ROPE // 2]], channel_multiplier=1).then_inc(consts, 1)

            pool.wait_ge(small_loaded, 32)
            pool.wait_ge(pos_loaded, 16)
            for t in range(BLOCKS):
                steps = [
                    lambda: pool.tensor_copy(ang[:], pos[:, tok[t]]),
                    lambda: pool.tensor_scalar(ang[:], ang[:], freq[:, 0:1], None, ALU.mult),
                    lambda: pool.tensor_scalar(turns[:], ang[:], float(1 / (2 * np.pi)), MAGIC, ALU.mult, ALU.add),
                    lambda: pool.tensor_scalar(turns[:], turns[:], -MAGIC, None, ALU.add),
                    lambda: pool.tensor_scalar(turns_hi[:], turns[:], 2048 * MAGIC, -2048 * MAGIC, ALU.add, ALU.add),
                    lambda: pool.tensor_tensor(turns[:], turns[:], turns_hi[:], ALU.subtract),
                ]
                for value in (TWO_PI_1, TWO_PI_2, TWO_PI_3):
                    for whole in (turns_hi, turns):
                        steps.append(lambda value=value, whole=whole: pool.tensor_scalar(part[:], whole[:], value, None, ALU.mult))
                        steps.append(lambda: pool.tensor_tensor(ang[:], ang[:], part[:], ALU.subtract))
                steps.append(lambda: pool.tensor_scalar(ang[:], ang[:], PI_IN, -PI_IN, ALU.min, ALU.max))
                assert len(steps) == STEPS
                if t:
                    pool.wait_ge(cos_done, t)
                for n, step in enumerate(steps):
                    if n:
                        pool.wait_ge(table, STEPS * t + n)
                    step().then_inc(table, 1)

        @block.tensor
        def _(pe):
            def sums(t):
                pe.wait_ge(sq_done, t + 1)
                pe.wait_ge(consts, 8)
                if t:
                    pe.wait_ge(var_done, 2 * t)
                for c, (k0, k1) in enumerate(((0, KQ), (KQ, KQ + KC))):
                    for k in range(k0, k1):
                        last = pe.matmul(ssq_ps[:, c], ones[:], sq[:, k], start=(k == k0), stop=(k == k1 - 1))
                last.then_inc(ssq_done, 1)

            def group(t, g):
                b, n = t % 2, NG * t + g
                if n >= RING:
                    pe.wait_ge(out_copied, n - RING + 1)
                acc = ring[:, n % RING]
                if g < G_KN:
                    cols, ks, k0 = slice(g * P, (g + 1) * P), range(KQ), 0
                    whi, wlo = uq_hi, uq_lo
                else:
                    cols, ks, k0 = slice((g - G_KN) * P, (g - G_KN + 1) * P), range(KC), KQ
                    whi, wlo = ukv_hi, ukv_lo
                for k in ks:
                    if g in (0, G_KN):
                        pe.wait_ge(nrm_lo_done, KL * t + k0 + k + 1)
                    if g < G_V:
                        ops = [(wlo[:, k, cols], nrm_hi[:, b, k0 + k]), (whi[:, k, cols], nrm_lo[:, b, k0 + k]),
                               (whi[:, k, cols], nrm_hi[:, b, k0 + k])]
                    else:
                        ts, vs = slice((g - G_V) * P, (g - G_V + 1) * P), slice(HEADS * P, NKV)
                        ops = [(nrm_lo[:, b, k0 + k, ts], whi[:, k, vs]), (nrm_hi[:, b, k0 + k, ts], wlo[:, k, vs]),
                               (nrm_hi[:, b, k0 + k, ts], whi[:, k, vs])]
                    for n, (stay, move) in enumerate(ops):
                        last = pe.matmul(acc, stay, move, start=(k == 0 and n == 0), stop=(k == ks[-1] and n == 2))
                last.then_inc(group_done, 1)

            def swap(t, g):
                if 3 * t + g:
                    pe.wait_ge(sin_part, 3 * t + g)
                rows = P if g < 2 else ROPE
                if g < 2:
                    pe.wait_ge(out_copied, NG * t + g + 1)
                else:
                    pe.wait_ge(kr_loaded[t % 2], 16 * (t // 2 + 1))
                src = raw_r[:, g] if g < 2 else kr[:, t % 2]
                pe.matmul(turn_ps[0:rows], turn[0:rows, 0:rows], src, start=True, stop=True).then_inc(turned, 1)

            sums(0)
            pe.wait_ge(uq_ready, 1)
            pe.wait_ge(ukv_ready, 1)
            for t in range(BLOCKS):
                for g in range(NG):
                    group(t, g)
                    if g == 3 and t + 1 < BLOCKS:
                        sums(t + 1)
                    if g + 1 in ROTATE:
                        swap(t, ROTATE.index(g + 1))

        @block.scalar
        def _(act):
            def squares(t):
                act.wait_ge(lat_loaded[t % 2], 16 * (t // 2 + 1))
                if t:
                    act.wait_ge(newton, 3 * t)
                act.activation(sq[:], lat[:, t % 2], ACT.Square).then_inc(sq_done, 1)

            def roots(t):
                act.wait_ge(ssq_done, t + 1)
                if t:
                    act.wait_ge(nrm_done, (KQ + KC) * t)
                for c, width in enumerate((Q_LORA, KV_LORA)):
                    act.activation(var[:, c], ssq_ps[:, c], ACT.Identity, scale=1.0 / width, bias=eps[:, 0:1]).then_inc(var_done, 1)
                act.wait_ge(var_done, 2 * t + 2)
                act.preload_act_table_set("natural_log_exp_and_others")
                act.activation(rstd[:], var, ACT.Ln).then_inc(log_done, 1)
                act.wait_ge(log_done, t + 1)
                act.activation(rstd[:], rstd[:], ACT.Exp, scale=-0.5).then_inc(root_done, 1)

            def angles(t):
                act.wait_ge(table, STEPS * (t + 1))
                act.activation(sin[:, tok[t]], ang[:], ACT.Sin).then_inc(sin_done, 1)
                act.activation(cos[:, tok[t]], ang[:], ACT.Abs).then_inc(abs_done, 1)
                act.wait_ge(abs_done, t + 1)
                act.activation(cos[:, tok[t]], cos[:, tok[t]], ACT.Sin, scale=-1.0, bias=half_pi[:, 0:1]).then_inc(cos_done, 1)

            def high(t):
                if t >= 2:
                    act.wait_ge(group_done, NG * (t - 1))
                for k in range(KL):
                    act.wait_ge(nrm_done, KL * t + k + 1)
                    act.activation(nrm_hi[:, t % 2, k], lat[:, t % 2, k], ACT.Copy).then_inc(nrm_hi_done, 1)

            act.wait_ge(consts, 8)
            squares(0)
            uq_act()
            ukv_act()
            roots(0)
            high(0)
            angles(0)
            for t in range(BLOCKS):
                for g in range(NG):
                    n = NG * t + g
                    act.wait_ge(group_done, n + 1)
                    if t and g == 0:
                        act.wait_ge(rot_done, 3 * t)
                    if t and g in (G_QN, G_KN, G_V):
                        sem = {G_QN: q_stored, G_KN: k_stored, G_V: v_stored}[g]
                        act.wait_ge(sem, 16 * t)
                    to = raw_r[:, g] if g < G_QN else out[:, g - G_QN]
                    act.activation(to, ring[:, n % RING], ACT.Copy, scale=SCALE if g < G_KN else 1.0).then_inc(out_copied, 1)
                    if g == 1 and t + 1 < BLOCKS:
                        squares(t + 1)
                    if g == 4 and t + 1 < BLOCKS:
                        roots(t + 1)
                    if g == 9 and t + 1 < BLOCKS:
                        high(t + 1)
                    if g == 13 and t + 1 < BLOCKS:
                        angles(t + 1)

        @block.vector
        def _(dve):
            def norm(t):
                b = t % 2
                dve.wait_ge(root_done, t + 1)
                dve.tensor_tensor(step_rs, rstd[:], rstd[:], ALU.mult).then_inc(newton, 1)
                dve.wait_ge(newton, 3 * t + 1)
                dve.scalar_tensor_tensor(step_rs, step_rs, -0.5, var, ALU.mult, ALU.mult).then_inc(newton, 1)
                dve.wait_ge(newton, 3 * t + 2)
                dve.scalar_tensor_tensor(rstd[:], step_rs, 1.5, rstd[:], ALU.add, ALU.mult).then_inc(newton, 1)
                dve.wait_ge(newton, 3 * t + 3)
                for k in range(KQ + KC):
                    dve.scalar_tensor_tensor(lat[:, b, k], lat[:, b, k], gain[:, k:k + 1], rstd[:, int(k >= KQ)],
                                             ALU.mult, ALU.mult).then_inc(nrm_done, 1)

            def low(t):
                for k in range(KL):
                    dve.wait_ge(nrm_hi_done, KL * t + k + 1)
                    dve.tensor_tensor(nrm_lo[:, t % 2, k], lat[:, t % 2, k], nrm_hi[:, t % 2, k].bitcast(F32),
                                      ALU.subtract).then_inc(nrm_lo_done, 1)

            def rotate(t, g):
                rows = P if g < 2 else ROPE
                src = raw_r[:, g] if g < 2 else kr[:, t % 2]
                n = 3 * t + g
                if g < 2:
                    dve.wait_ge(out_copied, NG * t + g + 1)
                else:
                    dve.wait_ge(kr_loaded[t % 2], 16 * (t // 2 + 1))
                dve.wait_ge(cos_done, t + 1)
                if n:
                    dve.wait_ge(rot_done, n)
                if t and g == 0:
                    dve.wait_ge(r_stored, 48 * t)
                dve.tensor_tensor(rot[0:rows, g], src, cos[0:rows, tok[t]], ALU.mult).then_inc(cos_part, 1)
                dve.wait_ge(turned, n + 1)
                dve.tensor_tensor(swapped[0:rows], turn_ps[0:rows], sin[0:rows, tok[t]], ALU.mult).then_inc(sin_part, 1)
                dve.wait_ge(cos_part, n + 1)
                dve.wait_ge(sin_part, n + 1)
                dve.tensor_tensor(rot[0:rows, g], rot[0:rows, g], swapped[0:rows], ALU.add).then_inc(rot_done, 1)

            uq_dve()
            ukv_dve()
            dve.wait_ge(small_loaded, 32)
            norm(0)
            low(0)
            for t in range(BLOCKS):
                for g in range(G_QN, NG):
                    if g + 1 in ROTATE:
                        rotate(t, ROTATE.index(g + 1))
                    if g == 5 and t + 1 < BLOCKS:
                        norm(t + 1)
                    if g == 11 and t + 1 < BLOCKS:
                        low(t + 1)


def delta_rule(nc, hT, a_log, dt_bias, norm_g, mixT):
    LEVELS = (2, 4, 8, 16, 32)
    BETA, GCUM, BETA_G, K_DEC, GATE = range(5)
    with ExitStack() as ctx:
        s = Scope(nc, ctx, "dr")
        qkv = s.sb("qkv", [P, 2, 3 * HEADS, P])
        zT = s.sb("zT", [P, 2, HEADS, P])
        ba_raw = s.sb("ba_raw", [2 * HEADS, SEQ])
        ba = s.sb("ba", [P, TILES, 2 * HEADS])
        bias = s.sb("bias", [P, HEADS])
        rate = s.sb("rate", [P, HEADS])
        gnorm = s.sb("gnorm", [P, 1])
        soft = s.sb("soft", [P, 3, TILES, HEADS])
        scal = s.sb("scal", [P, TILES, 5 * HEADS])
        cur = s.sb("cur", [P, 2, 5, HEADS])
        ident = s.sb("ident", [P, P])
        ones = s.sb("ones", [P, P])
        upto = s.sb("upto", [P, P])
        below = s.sb("below", [P, P])
        chunk = s.sb("chunk", [P, P])
        corner = s.sb("corner", [P, 1 + len(LEVELS), P])
        eps_l2 = s.sb("eps_l2", [P, 1])
        cums = s.sb("cums", [P, HEADS, P])
        eg = s.sb("eg", [P, 2, HEADS, P])
        e_last = s.sb("e_last", [P, HEADS, 2])
        sq = s.sb("sq", [P, 2 * HEADS, P])
        ssq = s.sb("ssq", [P, 2 * HEADS])
        rn = s.sb("rn", [P, 4, 2 * HEADS])
        qk_n = s.sb("qk_n", [P, 2 * HEADS, P])
        vb = s.sb("vb", [P, 2, HEADS, P])
        kbg = s.sb("kbg", [P, 2, HEADS, P])
        kdec = s.sb("kdec", [P, 2, HEADS, P])
        qk_nT = s.sb("qk_nT", [P, 2 * HEADS, P])
        dif = s.sb("dif", [P, HEADS, P])
        dec = s.sb("dec", [P, 2, HEADS, P])
        L = s.sb("L", [P, 2, HEADS, P])
        Z = s.sb("Z", [P, HEADS, P])
        Z0 = s.sb("Z0", [P, HEADS, P])
        U = s.sb("U", [P, 2, HEADS, P])
        T = s.sb("T", [P, HEADS, P])
        attnT = s.sb("attnT", [P, 2, HEADS, P])
        wT = s.sb("wT", [P, 2, HEADS, P])
        u = s.sb("u", [P, 2, HEADS, P])
        qdT = s.sb("qdT", [P, 2, HEADS, P])
        S = s.sb("S", [P, HEADS, P])
        Sd = s.sb("Sd", [P, HEADS, P])
        vnew = s.sb("vnew", [P, HEADS, P])
        osq = s.sb("osq", [P, HEADS, P])
        ossq = s.sb("ossq", [P, HEADS])
        orn = s.sb("orn", [P, 4, HEADS])
        on = s.sb("on", [P, HEADS, P])
        mix = s.sb("mix", [P, HEADS, P])
        b0, b1, b2, b3, solve0, solve1, step_ps, o_ps = [s.ps(f"b{n}", [P, HEADS, P]) for n in range(8)]

        const_sem, mask_sem = s.sem("consts"), s.sem("masks")
        small_loaded, ba_loaded = s.sem("small_loaded"), s.sem("ba_loaded")
        pre = s.sem("pre")
        loaded = [s.sem(f"loaded{b}") for b in range(2)]
        z_loaded = [s.sem(f"z_loaded{b}") for b in range(2)]
        cur_done = s.sem("cur_done")
        cums_done = s.sem("cums_done")
        qk_turned = s.sem("qk_turned")
        turned_done = s.sem("turned_done")
        eg_done = s.sem("eg_done")
        ssq_done, log_done, root_done = s.sem("ssq_done"), s.sem("log_done"), s.sem("root_done")
        newton = s.sem("newton")
        scaled = s.sem("scaled")
        vb_done = s.sem("vb_done")
        dif_done, dec_done = s.sem("dif_done"), s.sem("dec_done")
        kbg_done, kdec_done = s.sem("kbg_done"), s.sem("kdec_done")
        masked = s.sem("masked")
        back_done, back_copied = s.sem("back_done"), s.sem("back_copied")
        gram_done = s.sem("gram_done")
        L_done, attn_done = s.sem("L_done"), s.sem("attn_done")
        LT_done, z0_done, u_done = s.sem("LT_done"), s.sem("z0_done"), s.sem("u_done")
        t_copied, zp_done, z_done, yp_done, u_step, wu_done, wu_copied = (
            [s.sem(f"{n}{g}") for g in range(2)] for n in
            ("t_copied", "zp_done", "z_done", "yp_done", "u_step", "wu_done", "wu_copied"))
        qd_done = s.sem("qd_done")
        last_done = s.sem("last_done")
        ws_done, v_done, sd_done, kv_done, s_done = (s.sem(n) for n in ("ws_done", "v_done", "sd_done", "kv_done", "s_done"))
        o_done = s.sem("o_done")
        ossq_done, olog_done, oroot_done, onewton = (s.sem(n) for n in ("ossq_done", "olog_done", "oroot_done", "onewton"))
        on_done, oT_done, mix_done, mix_free, stored = (s.sem(n) for n in ("on_done", "oT_done", "mix_done", "mix_free", "stored"))
        block = ctx.enter_context(nc.Block())
        NL = len(LEVELS)
        PAIR = [slice(0, 2), slice(2, 4)]
        solve_ps = [solve0, solve1]
        N_MASKS = 5 + 2 * (1 + NL) + 1
        PRE_GATE = 13

        def column(c):
            return scal[:].rearrange("p t (c h) -> p t c h", c=5)[:, :, c, :]

        def heads(ap):
            return ap.unsqueeze(2).broadcast_to([P, ap.shape[1], P])

        def each(ap):
            return ap.unsqueeze(1).broadcast_to([P, HEADS, P])

        def twice(ap):
            return ap.unsqueeze(1).broadcast_to([P, 2, P])

        def pipeline(first, advance, all_three):
            def run(loop):
                first(0, 0)
                all_three(-1, 1, has_advance=False)
                with loop(0, TILES // 2 - 1) as i:
                    all_three(2 * i, 0)
                    all_three(2 * i + 1, 1)
                all_three(TILES - 2, 0, has_first=False)
                advance(TILES - 1, 1)
            return run

        @block.sync
        def _(sp):
            def load(t, b):
                src = hT[T_Q:T_Z, :, bass.ds(P * t, P)].rearrange("a p t -> p a t")
                sp.dma_start(qkv[:, b], src).then_inc(loaded[b], 16)

            def load_z(t, b):
                src = hT[T_Z:T_CQ, :, bass.ds(P * t, P)].rearrange("a p t -> p a t")
                sp.dma_start(zT[:, b], src).then_inc(z_loaded[b], 16)

            def step(t, b, more=True, more_z=True):
                if more:
                    sp.wait_ge(turned_done, t + 4)
                    load(t + 4, b)
                sp.wait_ge(mix_done, t + 1)
                sp.dma_start(mixT[0:HEADS, :, bass.ds(P * t, P)].rearrange("a p t -> p a t"), mix[:]).then_inc(stored, 16)
                if more_z:
                    load_z(t + 2, b)
                sp.wait_ge(stored, 16 * t + 16)
                sp.sem_inc(mix_free, 1)

            sp.dma_start(ba_raw[:], hT[T_KR, ROPE:ROPE + 2 * HEADS, :]).then_inc(ba_loaded, 16)
            sp.dma_start(bias[:], dt_bias.partition_broadcast(P)).then_inc(small_loaded, 16)
            sp.dma_start(rate[:], a_log.partition_broadcast(P)).then_inc(small_loaded, 16)
            sp.dma_start(gnorm[:], norm_g).then_inc(small_loaded, 16)
            sp.sem_inc(mix_free, 1)
            for t in range(2):
                load(t, t)
            for t in range(2):
                load_z(t, t)
            for t in range(2):
                sp.wait_ge(turned_done, t + 2)
                load(t + 2, t)
            with sp.Fori(0, TILES // 2 - 2) as i:
                step(2 * i, 0)
                step(2 * i + 1, 1)
            step(TILES - 4, 0, more=False)
            step(TILES - 3, 1, more=False)
            step(TILES - 2, 0, more=False, more_z=False)
            step(TILES - 1, 1, more=False, more_z=False)

        @block.gpsimd
        def _(pool):
            n = [0]

            def put(out, in_, op, fill, base, pattern, mult):
                if n[0]:
                    pool.wait_ge(mask_sem, n[0])
                pool.affine_select(out=out, in_=in_, compare_op=op, fill=fill, base=base, pattern=pattern,
                                   channel_multiplier=mult).then_inc(mask_sem, 1)
                n[0] += 1

            pool.memset(ident[:], 0.0).then_inc(const_sem, 1)
            pool.memset(ones[:], 1.0).then_inc(const_sem, 1)
            pool.memset(eps_l2[:], RMS_EPS).then_inc(const_sem, 1)
            pool.memset(corner[:], 0.0).then_inc(const_sem, 1)
            pool.wait_ge(const_sem, 4)
            put(ident[:], ident[:], ALU.not_equal, 1.0, 0, [[-1, P]], 1)
            halves = lambda ap: ap.rearrange("p (c f) -> p c f", c=2)
            put(halves(chunk[:]), halves(ones[:]), ALU.is_ge, 0.0, 0, [[-CHUNK, 2], [0, CHUNK]], 1)
            put(halves(chunk[:]), halves(chunk[:]), ALU.is_ge, 0.0, CHUNK - 1, [[CHUNK, 2], [0, CHUNK]], -1)
            put(upto[:], chunk[:], ALU.is_ge, 0.0, 0, [[1, P]], -1)
            put(below[:], chunk[:], ALU.is_gt, 0.0, 0, [[-1, P]], 1)
            for l, size in enumerate((1,) + LEVELS):
                blocks = P // (2 * size)
                right = lambda ap: ap.rearrange("p (n h r) -> p n h r", h=2, r=size)[:, :, 1, :]
                put(right(corner[:, l]), right(ones[:]), ALU.is_ge, 0.0, 0, [[-2 * size, blocks], [0, size]], 1)
                put(right(corner[:, l]), right(corner[:, l]), ALU.is_ge, 0.0, size - 1, [[2 * size, blocks], [0, size]], -1)
            pool.wait_ge(mask_sem, n[0])
            pool.sem_inc(mask_sem, 1)

            def sums(t, b):
                pool.wait_ge(cur_done, t + 1)
                pool.wait_ge(turned_done, t + 1)
                pool.tensor_tensor(cums[:], each(upto[:]), heads(cur[:, b, GATE]), ALU.mult).then_inc(cums_done, 1)

            def masks(t, b):
                pool.wait_ge(dec_done, t + 1)
                pool.tensor_tensor(dec[:, 0], dif[:], each(below[:]), ALU.mult).then_inc(masked, 1)
                pool.wait_ge(masked, 3 * t + 1)
                pool.tensor_tensor(dec[:, 0], dec[:, 0], heads(cur[:, b, BETA]), ALU.mult).then_inc(masked, 1)
                pool.tensor_tensor(dec[:, 1], dif[:], each(upto[:]), ALU.mult).then_inc(masked, 1)

            def products(t, b):
                pool.wait_ge(scaled, 2 * t + 1)
                for g in range(2):
                    reached(pool, wu_done[g], t - 1)
                pool.tensor_tensor(kbg[:, b], qk_n[:, HEADS:], heads(cur[:, b, BETA_G]), ALU.mult).then_inc(kbg_done, 1)
                reached(pool, o_done, 2 * t - 2)
                pool.tensor_tensor(kdec[:, b], qk_n[:, HEADS:], heads(cur[:, b, K_DEC]), ALU.mult).then_inc(kdec_done, 1)
                pool.wait_ge(back_copied, 2 * t + 2)
                pool.wait_ge(eg_done, t + 1)
                pool.tensor_tensor(qdT[:, b], qk_nT[:, 0:HEADS], eg[:, b], ALU.mult).then_inc(qd_done, 1)

            pool.sem_inc(kdec_done, 1)
            pool.sem_inc(qd_done, 1)
            def decay(t, b, c):
                pool.wait_ge(last_done, t + 1)
                pool.wait_ge(s_done, 2 * t + c + 1)
                pool.tensor_tensor(Sd[:], S[:], e_last[:, :, c:c + 1].broadcast_to([P, HEADS, P]), ALU.mult).then_inc(sd_done, 1)

            def first(t, b):
                sums(t, b)
                masks(t, b)
                products(t, b)

            def advance(t, b):
                decay(t, b, 0)
                decay(t, b, 1)

            def all_three(t, b, has_first=True, has_advance=True):
                if has_first:
                    sums(t + 2, b)
                if has_advance:
                    advance(t, b)
                if has_first:
                    masks(t + 2, b)
                    products(t + 2, b)

            pipeline(first, advance, all_three)(pool.Fori)

        @block.tensor
        def _(pe):
            def transposes(out, src, n0, count):
                for h in range(count):
                    last = pe.transpose(out[:, h], src[:, n0 + h], ident[:])
                return last

            def pre_scalars():
                pe.wait_ge(mask_sem, N_MASKS)
                pe.wait_ge(ba_loaded, 16)
                for t in range(TILES):
                    last = pe.transpose(b0[:].rearrange("p h f -> p (h f)")[:, 8 * t:8 * t + 8],
                                        ba_raw[:, t * P:(t + 1) * P], ident[0:8, 0:8])
                last.then_inc(pre, 1)
                pe.wait_ge(pre, PRE_GATE)
                pe.matmul(b1[:, 0, 0:64], upto[:], soft[:, 2].rearrange("p t h -> p (t h)"), start=True, stop=True)
                pe.matmul(b2[:, 0, 0:64], chunk[:], soft[:, 2].rearrange("p t h -> p (t h)"), start=True, stop=True).then_inc(pre, 1)
                pe.wait_ge(pre, PRE_GATE + 6)

            def p_turn(t, b):
                pe.wait_ge(loaded[b], 8 * (t - b) + 16)
                reached(pe, attn_done, t)
                transposes(b0, qkv[:, b], 0, HEADS)
                transposes(b1, qkv[:, b], HEADS, HEADS).then_inc(qk_turned, 1)

            def p_turn_v(t, b):
                reached(pe, z0_done, t)
                reached(pe, dif_done, t)
                transposes(b2, qkv[:, b], 2 * HEADS, HEADS)
                pe.wait_ge(cums_done, t + 1)
                pe.matmul(b3[:].rearrange("p h f -> p (h f)"), ones[:], cums[:].rearrange("p h f -> p (h f)"),
                          start=True, stop=True).then_inc(turned_done, 1)

            def p_back(t, b):
                pe.wait_ge(scaled, 2 * t + 2)
                transposes(b0, qk_n, 0, HEADS)
                transposes(b1, qk_n, HEADS, HEADS).then_inc(back_done, 1)

            def p_gram(t, b):
                pe.wait_ge(back_copied, 2 * t + 2)
                for h in range(HEADS):
                    pe.matmul(b0[:, h], qk_nT[:, HEADS + h], qk_nT[:, HEADS + h], start=True, stop=True)
                for h in range(HEADS):
                    last = pe.matmul(b1[:, h], qk_nT[:, HEADS + h], qk_nT[:, h], start=True, stop=True)
                last.then_inc(gram_done, 1)

            def p_turn_l(t, b):
                pe.wait_ge(L_done, t + 1)
                pe.wait_ge(vb_done, t + 1)
                for h in range(HEADS):
                    last = pe.transpose(b2[:, h], L[:, b, h], ident[:])
                last.then_inc(LT_done, 1)

            def s_z(t, b, l):
                if l == 0:
                    pe.wait_ge(u_done, t + 1)
                for g in range(2):
                    if l == 0:
                        reached(pe, wu_copied[g], 2 * t)
                    else:
                        pe.wait_ge(u_step[g], NL * t + l)
                    for h in range(2):
                        pe.transpose(solve_ps[g][:, h], U[:, b, 2 * g + h], ident[:])
                    for h in range(2):
                        last = pe.matmul(solve_ps[g][:, 2 + h], L[:, b, 2 * g + h], U[:, b, 2 * g + h], start=True, stop=True)
                    last.then_inc(zp_done[g], 1)

            def s_y(t, b, l):
                for g in range(2):
                    pe.wait_ge(z_done[g], NL * t + l + 1)
                    for h in range(2):
                        last = pe.matmul(solve_ps[g][:, h], T[:, 2 * g + h], Z[:, 2 * g + h], start=True, stop=True)
                    last.then_inc(yp_done[g], 1)

            def s_wu(t, b):
                pe.wait_ge(kbg_done, t + 1)
                pe.wait_ge(vb_done, t + 1)
                for g in range(2):
                    pe.wait_ge(u_step[g], NL * (t + 1))
                    for h in range(2):
                        pe.matmul(solve_ps[g][:, h], kbg[:, b, 2 * g + h], U[:, b, 2 * g + h], start=True, stop=True)
                    for h in range(2):
                        last = pe.matmul(solve_ps[g][:, 2 + h], U[:, b, 2 * g + h], vb[:, b, 2 * g + h], start=True, stop=True)
                    last.then_inc(wu_done[g], 1)

            def a_state(t, b, c):
                lo, hi = CHUNK * c, CHUNK * (c + 1)
                if c == 0:
                    for g in range(2):
                        pe.wait_ge(wu_copied[g], 2 * t + 2)
                    pe.wait_ge(qd_done, t + 2)
                    pe.wait_ge(on_done, t + 1)
                    reached(pe, mix_done, t)
                pe.wait_ge(s_done, 2 * t + c + 1)
                for h in range(HEADS):
                    last = pe.matmul(step_ps[lo:hi, h], wT[:, b, h, lo:hi], S[:, h], start=True, stop=True)
                last.then_inc(ws_done, 1)
                for h in range(HEADS):
                    pe.matmul(o_ps[lo:hi, h], qdT[:, b, h, lo:hi], S[:, h], start=(h == 0), stop=False, skip_group_check=True)

            def a_update(t, b, c):
                lo, hi = CHUNK * c, CHUNK * (c + 1)
                pe.wait_ge(v_done, 2 * t + c + 1)
                if c == 0:
                    pe.wait_ge(kdec_done, t + 2)
                for h in range(HEADS):
                    last = pe.matmul(step_ps[:, h], kdec[lo:hi, b, h], vnew[lo:hi, h], start=True, stop=True)
                last.then_inc(kv_done, 1)
                for h in range(HEADS):
                    last = pe.matmul(o_ps[lo:hi, h], attnT[lo:hi, b, h, lo:hi], vnew[lo:hi, h], start=False, stop=True,
                                     skip_group_check=True)
                last.then_inc(o_done, 1)

            def a_out(t, b):
                pe.wait_ge(on_done, t + 2)
                pe.wait_ge(s_done, 2 * t + 3)
                transposes(step_ps, on, 0, HEADS).then_inc(oT_done, 1)

            def first(t, b):
                p_turn(t, b)
                p_turn_v(t, b)
                p_back(t, b)
                p_gram(t, b)
                p_turn_l(t, b)

            def advance(t, b):
                for c in range(2):
                    a_state(t, b, c)
                    a_update(t, b, c)
                a_out(t, b)

            def all_three(t, b, has_first=True, has_advance=True):
                m, n, c = t + 2, t + 1, 1 - b
                if has_first:
                    p_turn(m, b)
                if has_advance:
                    a_state(t, b, 0)
                s_z(n, c, 0)
                if has_first:
                    p_turn_v(m, b)
                s_y(n, c, 0)
                if has_advance:
                    a_update(t, b, 0)
                s_z(n, c, 1)
                if has_advance:
                    a_state(t, b, 1)
                s_y(n, c, 1)
                s_z(n, c, 2)
                if has_advance:
                    a_update(t, b, 1)
                if has_first:
                    p_back(m, b)
                s_y(n, c, 2)
                s_z(n, c, 3)
                if has_first:
                    p_gram(m, b)
                s_y(n, c, 3)
                s_z(n, c, 4)
                if has_advance:
                    a_out(t, b)
                s_y(n, c, 4)
                if has_first:
                    p_turn_l(m, b)
                s_wu(n, c)

            pe.sem_inc(turned_done, 1)
            pre_scalars()
            pipeline(first, advance, all_three)(pe.Fori)

        @block.scalar
        def _(act):
            def pre_scalars():
                act.preload_act_table_set("natural_log_exp_and_others")
                act.wait_ge(small_loaded, 48)
                act.wait_ge(pre, 1)
                act.activation(ba[:].rearrange("p t c -> p (t c)"), b0[:, 0, :], ACT.Copy).then_inc(pre, 1)
                act.activation(rate[:], rate[:], ACT.Exp).then_inc(pre, 1)
                act.wait_ge(pre, 4)
                act.activation(soft[:, 1], soft[:, 0], ACT.Abs).then_inc(pre, 1)
                act.wait_ge(pre, 5)
                act.activation(soft[:, 1], soft[:, 1], ACT.Exp, scale=-1.0).then_inc(pre, 1)
                act.wait_ge(pre, 6)
                act.activation(soft[:, 1], soft[:, 1], ACT.Ln, bias=1.0).then_inc(pre, 1)
                act.activation(ba[:, :, 0:HEADS], ba[:, :, 0:HEADS], ACT.Exp, scale=-1.0).then_inc(pre, 1)
                act.wait_ge(pre, PRE_GATE + 1)
                act.activation(soft[:, 0].rearrange("p t h -> p (t h)"), b1[:, 0, 0:64], ACT.Exp).then_inc(pre, 1)
                act.wait_ge(pre, PRE_GATE + 4)
                act.activation(column(K_DEC), soft[:, 1], ACT.Exp).then_inc(pre, 1)

            def p_squares(t, b):
                act.wait_ge(qk_turned, t + 1)
                for n in range(2 * HEADS):
                    bank = b0 if n < HEADS else b1
                    last = act.activation(sq[:, n], bank[:, n % HEADS], ACT.Square, accum_out=ssq[:, n:n + 1])
                last.then_inc(ssq_done, 1)

            def p_eg(t, b):
                act.wait_ge(turned_done, t + 2)
                reached(act, last_done, t - 1)
                reached(act, qd_done, t)
                act.activation(eg[:, b], b3[:], ACT.Exp).then_inc(eg_done, 1)

            def p_roots(t, b):
                act.wait_ge(ssq_done, t + 1)
                act.activation(rn[:, 0], ssq[:], ACT.Ln, bias=eps_l2[:, 0:1]).then_inc(log_done, 1)
                act.wait_ge(log_done, t + 1)
                act.activation(rn[:, 1], rn[:, 0], ACT.Exp, scale=-0.5).then_inc(root_done, 1)

            def p_differences(t, b):
                act.wait_ge(cur_done, t + 1)
                for h in range(HEADS):
                    last = act.activation(dif[:, h], b3[:, h], ACT.Abs, scale=-1.0, bias=cur[:, b, GCUM, h:h + 1])
                last.then_inc(dif_done, 1)

            def p_decays(t, b):
                act.wait_ge(dif_done, t + 1)
                act.activation(dif[:], dif[:], ACT.Exp, scale=-1.0).then_inc(dec_done, 1)

            def p_scale_v(t, b):
                for g in range(2):
                    reached(act, wu_done[g], t - 1)
                for h in range(HEADS):
                    last = act.activation(vb[:, b, h], b2[:, h], ACT.Copy, scale=cur[:, b, BETA, h:h + 1])
                last.then_inc(vb_done, 1)

            def p_copy_back(t, b):
                act.wait_ge(back_done, t + 1)
                act.wait_ge(qd_done, t + 1)
                act.activation(qk_nT[:, 0:HEADS], b0[:], ACT.Copy, scale=float(P) ** -0.5).then_inc(back_copied, 1)
                act.activation(qk_nT[:, HEADS:], b1[:], ACT.Copy).then_inc(back_copied, 1)

            def s_copy_t(t, l):
                for g in range(2):
                    act.wait_ge(zp_done[g], NL * t + l + 1)
                    act.activation(T[:, PAIR[g]], solve_ps[g][:, 0:2], ACT.Copy).then_inc(t_copied[g], 1)

            def s_copy_wu(t, b):
                reached(act, v_done, 2 * t - 2)
                for g in range(2):
                    act.wait_ge(wu_done[g], t + 1)
                    act.activation(wT[:, b, PAIR[g]], solve_ps[g][:, 0:2], ACT.Copy).then_inc(wu_copied[g], 1)
                    act.activation(u[:, b, PAIR[g]], solve_ps[g][:, 2:4], ACT.Copy).then_inc(wu_copied[g], 1)

            def a_squares(t, b):
                act.wait_ge(o_done, 2 * t + 2)
                for h in range(HEADS):
                    last = act.activation(osq[:, h], o_ps[:, h], ACT.Square, accum_out=ossq[:, h:h + 1])
                last.then_inc(ossq_done, 1)

            def a_roots(t, b):
                act.wait_ge(ossq_done, t + 1)
                act.activation(orn[:, 0], ossq[:], ACT.Ln, bias=eps_l2[:, 0:1], scale=1.0 / P).then_inc(olog_done, 1)
                act.wait_ge(olog_done, t + 1)
                act.activation(orn[:, 1], orn[:, 0], ACT.Exp, scale=-0.5).then_inc(oroot_done, 1)

            def first(t, b):
                p_squares(t, b)
                p_eg(t, b)
                p_differences(t, b)
                p_roots(t, b)
                p_decays(t, b)
                p_scale_v(t, b)
                p_copy_back(t, b)

            def advance(t, b):
                a_squares(t, b)
                a_roots(t, b)

            def all_three(t, b, has_first=True, has_advance=True):
                m, n, c = t + 2, t + 1, 1 - b
                if has_first:
                    p_squares(m, b)
                s_copy_t(n, 0)
                if has_first:
                    p_eg(m, b)
                    p_differences(m, b)
                s_copy_t(n, 1)
                if has_first:
                    p_roots(m, b)
                    p_decays(m, b)
                    p_scale_v(m, b)
                s_copy_t(n, 2)
                if has_advance:
                    a_squares(t, b)
                if has_first:
                    p_copy_back(m, b)
                if has_advance:
                    a_roots(t, b)
                s_copy_t(n, 3)
                s_copy_t(n, 4)
                s_copy_wu(n, c)

            act.wait_ge(const_sem, 4)
            pre_scalars()
            pipeline(first, advance, all_three)(act.Fori)

        @block.vector
        def _(dve):
            def pre_scalars():
                dve.memset(S[:], 0.0).then_inc(s_done, 1)
                dve.sem_inc(on_done, 1)
                dve.wait_ge(pre, 3)
                dve.tensor_tensor(soft[:, 0], ba[:, :, HEADS:], bias[:].unsqueeze(1).broadcast_to([P, TILES, HEADS]),
                                  ALU.add).then_inc(pre, 1)
                dve.wait_ge(pre, 8)
                dve.scalar_tensor_tensor(soft[:, 1], soft[:, 0], 0.0, soft[:, 1], ALU.max, ALU.add).then_inc(pre, 1)
                dve.wait_ge(pre, 9)
                dve.scalar_tensor_tensor(soft[:, 2], soft[:, 1], -1.0, rate[:].unsqueeze(1).broadcast_to([P, TILES, HEADS]),
                                         ALU.mult, ALU.mult).then_inc(pre, 1)
                dve.tensor_scalar(ba[:, :, 0:HEADS], ba[:, :, 0:HEADS], 1.0, None, ALU.add).then_inc(pre, 1)
                dve.wait_ge(pre, 11)
                dve.reciprocal(column(BETA), ba[:, :, 0:HEADS]).then_inc(pre, 1)
                dve.tensor_copy(column(GATE), soft[:, 2]).then_inc(pre, 1)
                dve.wait_ge(pre, PRE_GATE + 2)
                view = lambda bank: bank[:, 0, 0:64].rearrange("p (t h) -> p t h", h=HEADS)
                dve.tensor_copy(column(GCUM), view(b1)).then_inc(pre, 1)
                dve.wait_ge(pre, PRE_GATE + 3)
                dve.tensor_tensor(soft[:, 1], view(b2), column(GCUM), ALU.subtract).then_inc(pre, 1)
                dve.tensor_tensor(column(BETA_G), column(BETA), soft[:, 0], ALU.mult).then_inc(pre, 1)
                dve.wait_ge(pre, PRE_GATE + 6)

            def p_scalars(t, b):
                reached(dve, kdec_done, t)
                dve.tensor_scalar(cur[:, b].rearrange("p c h -> p (c h)"), scal[:, bass.ds(t, 1)].rearrange("p a c -> p (a c)"),
                                  1.0, None, ALU.mult).then_inc(cur_done, 1)

            def p_newton(t, b):
                dve.wait_ge(root_done, t + 1)
                dve.tensor_tensor(rn[:, 2], rn[:, 1], rn[:, 1], ALU.mult).then_inc(newton, 1)
                dve.tensor_scalar(ssq[:], ssq[:], RMS_EPS, -0.5, ALU.add, ALU.mult).then_inc(newton, 1)
                dve.wait_ge(newton, 4 * t + 2)
                dve.tensor_tensor(rn[:, 2], rn[:, 2], ssq[:], ALU.mult).then_inc(newton, 1)
                dve.wait_ge(newton, 4 * t + 3)
                dve.scalar_tensor_tensor(rn[:, 3], rn[:, 2], 1.5, rn[:, 1], ALU.add, ALU.mult).then_inc(newton, 1)
                dve.wait_ge(newton, 4 * t + 4)

            def p_scale(t, b):
                dve.wait_ge(kdec_done, t + 1)
                dve.tensor_tensor(qk_n[:, HEADS:], b1[:], heads(rn[:, 3, HEADS:]), ALU.mult).then_inc(scaled, 1)
                dve.tensor_tensor(qk_n[:, 0:HEADS], b0[:], heads(rn[:, 3, 0:HEADS]), ALU.mult).then_inc(scaled, 1)

            def p_grams(t, b):
                dve.wait_ge(gram_done, t + 1)
                dve.wait_ge(masked, 3 * t + 3)
                for g in range(2):
                    reached(dve, wu_done[g], t - 1)
                reached(dve, o_done, 2 * t - 2)
                dve.tensor_tensor(L[:, b], b0[:], dec[:, 0], ALU.mult).then_inc(L_done, 1)

            def p_attention(t, b):
                dve.tensor_tensor(attnT[:, b], b1[:], dec[:, 1], ALU.mult).then_inc(attn_done, 1)

            def p_inverse(t, b):
                dve.wait_ge(LT_done, t + 1)
                dve.tensor_tensor(Z0[:], b2[:], each(corner[:, 0]), ALU.mult).then_inc(z0_done, 1)
                dve.wait_ge(z0_done, t + 1)
                dve.tensor_tensor(U[:, b], each(ident[:]), Z0[:], ALU.subtract).then_inc(u_done, 1)

            def s_z(t, l):
                for g in range(2):
                    dve.wait_ge(t_copied[g], NL * t + l + 1)
                    dve.tensor_tensor(Z[:, PAIR[g]], solve_ps[g][:, 2:4], twice(corner[:, l + 1]), ALU.mult).then_inc(z_done[g], 1)

            def s_u(t, b, l):
                for g in range(2):
                    dve.wait_ge(yp_done[g], NL * t + l + 1)
                    dve.tensor_tensor(U[:, b, PAIR[g]], U[:, b, PAIR[g]], solve_ps[g][:, 0:2], ALU.subtract).then_inc(u_step[g], 1)

            def a_v(t, b, c):
                lo, hi = CHUNK * c, CHUNK * (c + 1)
                dve.wait_ge(ws_done, 2 * t + c + 1)
                dve.tensor_tensor(vnew[lo:hi], u[lo:hi, b], step_ps[lo:hi], ALU.subtract).then_inc(v_done, 1)

            def a_last(t, b):
                reached(dve, sd_done, 2 * t)
                dve.wait_ge(eg_done, t + 1)
                ends = eg[:, b].rearrange("p h (c f) -> p h c f", c=2)[:, :, :, CHUNK - 1]
                dve.tensor_copy(e_last[:], ends).then_inc(last_done, 1)

            def a_s(t, b, c):
                dve.wait_ge(sd_done, 2 * t + c + 1)
                dve.wait_ge(kv_done, 2 * t + c + 1)
                dve.tensor_tensor(S[:], Sd[:], step_ps[:], ALU.add).then_inc(s_done, 1)

            def a_norm(t, b):
                dve.wait_ge(oroot_done, t + 1)
                dve.tensor_tensor(orn[:, 2], orn[:, 1], orn[:, 1], ALU.mult).then_inc(onewton, 1)
                dve.tensor_scalar(ossq[:], ossq[:], RMS_EPS * P, -0.5 / P, ALU.add, ALU.mult).then_inc(onewton, 1)
                dve.wait_ge(onewton, 4 * t + 2)
                dve.tensor_tensor(orn[:, 2], orn[:, 2], ossq[:], ALU.mult).then_inc(onewton, 1)
                dve.wait_ge(onewton, 4 * t + 3)
                dve.scalar_tensor_tensor(orn[:, 3], orn[:, 2], 1.5, orn[:, 1], ALU.add, ALU.mult).then_inc(onewton, 1)
                dve.wait_ge(onewton, 4 * t + 4)
                dve.tensor_tensor(on[:], o_ps[:], heads(orn[:, 3]), ALU.mult).then_inc(on_done, 1)

            def a_gate(t, b):
                dve.wait_ge(oT_done, t + 1)
                dve.wait_ge(z_loaded[b], 8 * (t - b) + 16)
                dve.wait_ge(mix_free, t + 1)
                dve.scalar_tensor_tensor(mix[:], step_ps[:], gnorm[:, 0:1], zT[:, b], ALU.mult, ALU.mult).then_inc(mix_done, 1)

            def first(t, b):
                p_scalars(t, b)
                p_newton(t, b)
                p_scale(t, b)
                p_grams(t, b)
                p_attention(t, b)
                p_inverse(t, b)

            def advance(t, b):
                a_last(t, b)
                for c in range(2):
                    a_v(t, b, c)
                    a_s(t, b, c)
                a_norm(t, b)
                a_gate(t, b)

            def all_three(t, b, has_first=True, has_advance=True):
                m, n, c = t + 2, t + 1, 1 - b
                if has_first:
                    p_scalars(m, b)
                if has_advance:
                    a_last(t, b)
                    a_v(t, b, 0)
                s_z(n, 0)
                s_u(n, c, 0)
                if has_advance:
                    a_s(t, b, 0)
                s_z(n, 1)
                if has_advance:
                    a_v(t, b, 1)
                s_u(n, c, 1)
                if has_first:
                    p_newton(m, b)
                    p_scale(m, b)
                s_z(n, 2)
                if has_advance:
                    a_s(t, b, 1)
                s_u(n, c, 2)
                s_z(n, 3)
                if has_advance:
                    a_norm(t, b)
                s_u(n, c, 3)
                if has_first:
                    p_grams(m, b)
                s_z(n, 4)
                if has_first:
                    p_attention(m, b)
                s_u(n, c, 4)
                if has_first:
                    p_inverse(m, b)
                if has_advance:
                    a_gate(t, b)

            pre_scalars()
            pipeline(first, advance, all_three)(dve.Fori)


def attention(nc, made, mixT):
    QB = 2 * P
    NB = SEQ // QB
    blocks = [(0, j) for j in range(NB)] + [(1, j) for j in reversed(range(NB))]
    N = len(blocks)
    pairs = [j + 1 for _, j in blocks]
    groups = [j // 2 + 1 for _, j in blocks]
    pair0 = [sum(pairs[:n]) for n in range(N + 1)]
    group0 = [sum(2 * g for g in groups[:n]) for n in range(N + 1)]
    PAIRS, GROUPS = pair0[-1], group0[-1]
    ROUNDS = HEADS // 2
    S_RING, T_RING = 4, 3
    RAW = 4
    PIECES = 4 * BLOCKS
    SHARE = (0, 1, 2, 2, 3, 4, 4, 0, 0, 4, 4, 3, 3, 2, 0, 0)
    assert sum(SHARE[:NB]) == sum(SHARE[NB:]) == PIECES
    MASK = -1e30
    with ExitStack() as ctx:
        s = Scope(nc, ctx, "at")
        q_hi, q_lo, k_hi, k_lo, v_hi, v_lo, qr = (s.sb(n, [P, 2, SEQ], F32R) for n in
                                                  ("q_hi", "q_lo", "k_hi", "k_lo", "v_hi", "v_lo", "qr"))
        kr = s.sb("kr", [P, SEQ], F32R)
        kr_hi = s.sb("kr_hi", [P, SEQ], F32R)
        ident = s.sb("ident", [P, P])
        raw = s.sb("raw", [P, RAW, NTOK])
        qr_hi = s.sb("qr_hi", [P, NTOK], F32R)
        zero = s.sb("zero", [P, 1])
        prob = s.sb("prob", [P, 2, 2, SEQ])
        negm = s.sb("negm", [P, 2, 2, 4])
        sums = s.sb("sums", [P, 2, 2, 4])
        top = s.sb("top", [P, 2, 2])
        fac = s.sb("fac", [P, 2, 2, 4])
        part = s.sb("part", [P, 2, 2, 4])
        total = s.sb("total", [P, 2, 2])
        scale = s.sb("scale", [P, 2, 2, 4])
        pT_hi = s.sb("pT_hi", [P, T_RING, 2 * QB], F32R)
        pT_lo = s.sb("pT_lo", [P, T_RING, 2 * QB], F32R)
        out = s.sb("out", [P, 2, QB])
        score_ps = s.ps("score_ps", [P, S_RING, NTOK])
        pT_ps = s.ps("pT_ps", [P, T_RING, 2 * QB])
        acc_ps = s.ps("acc_ps", [P, NTOK])

        C_EXP, C_TURN, C_LO, C_PV, C_OUT, C_FREE = S_RING, 2, T_RING, T_RING, 1, 2
        raw0 = prob[:].rearrange("p a b (c n) -> p (a b c) n", n=NTOK)
        raw_kr = raw[:].rearrange("p a n -> p (a n)")
        const_sem = s.sem("consts")
        kr_loaded = s.sem("kr_loaded")
        kr_done = s.sem("kr_done")
        head0_loaded = [s.sem(f"head0_loaded{c}") for c in range(BLOCKS)]
        raw_loaded = [s.sem(f"raw_loaded{n}") for n in range(RAW)]
        hi_split = s.sem("hi_split")
        qr_hi_done = s.sem("qr_hi_done")
        pool_hi = s.sem("pool_hi")
        taken = s.sem("taken")
        split_done = [s.sem(f"split_done{b}") for b in range(2)]
        score_done = s.sem("score_done")
        diag_done = s.sem("diag_done")
        max_done = s.sem("max_done")
        exp_done = s.sem("exp_done")
        top_done, gap_done, fac_done, part_done, total_done, inv_done = (
            s.sem(n) for n in ("top_done", "gap_done", "fac_done", "part_done", "total_done", "inv_done"))
        scale_done = s.sem("scale_done")
        scaled = s.sem("scaled")
        turned = s.sem("turned")
        hi_done = s.sem("hi_done")
        lo_done = s.sem("lo_done")
        pv_done = s.sem("pv_done")
        out_done = s.sem("out_done")
        out_free = s.sem("out_free")
        stored = s.sem("stored")
        block = ctx.enter_context(nc.Block())
        many = [n for n in range(N) if groups[n] > 1]
        MANY = len(many)

        def pieces(h, n):
            first = sum(SHARE[NB * (n // NB):n])
            return range(first, first + SHARE[n]) if h + 1 < HEADS else ()

        def per_slot(kind, h, m):
            each = 32 if kind == 2 else 16
            return each * ((PIECES * (h - 1) + m) // RAW + 1)

        def widths(j, tile):
            keys = P * (2 * j + tile + 1)
            return [min(NTOK, keys - NTOK * g) for g in range(j // 2 + 1)]

        def score_groups(n, which):
            every = [(tile, g, w) for tile in range(2) for g, w in enumerate(widths(blocks[n][1], tile))]
            every = [(tile, g, w, group0[n] + k, g + 1 == groups[n]) for k, (tile, g, w) in enumerate(every)]
            return every[:-1] if which == "first" else every[-1:]

        @block.gpsimd
        def _(pool):
            pool.memset(ident[:], 0.0).then_inc(const_sem, 1)
            pool.memset(zero[:], 0.0).then_inc(const_sem, 1)
            pool.wait_ge(const_sem, 2)
            pool.affine_select(out=ident[:], in_=ident[:], compare_op=ALU.not_equal, fill=1.0, base=0, pattern=[[-1, P]],
                               channel_multiplier=1).then_inc(const_sem, 1)

            def split(h, m):
                count, b = PIECES * h + m, h % 2
                slot, kind, ts = count % RAW, m % 4, slice(NTOK * (m // 4), NTOK * (m // 4 + 1))
                pool.wait_ge(raw_loaded[slot], per_slot(kind, h, m))
                src = raw[:, slot]
                if kind == 2:
                    pool.tensor_tensor(qr_hi[:], src, zero[:, 0:1].broadcast_to([P, NTOK]), ALU.add).then_inc(pool_hi, 1)
                    pool.wait_ge(pool_hi, count + 1 - PIECES)
                    pool.tensor_tensor(qr[ROPE:, b, ts], src[ROPE:], zero[ROPE:, 0:1].broadcast_to([ROPE, NTOK]),
                                       ALU.add).then_inc(qr_hi_done, 1)
                    pool.wait_ge(qr_hi_done, (count - PIECES) // 4 + 1)
                    low, high, src = qr[0:ROPE, b, ts], qr_hi[0:ROPE], src[0:ROPE]
                else:
                    high, low = ((q_hi, q_lo), (k_hi, k_lo), None, (v_hi, v_lo))[kind]
                    high, low = high[:, b, ts], low[:, b, ts]
                    pool.tensor_tensor(high, src, zero[:, 0:1].broadcast_to([P, NTOK]), ALU.add).then_inc(pool_hi, 1)
                pool.wait_ge(pool_hi, count + 1 - PIECES)
                pool.tensor_tensor(low, src, high.bitcast(F32), ALU.subtract).then_inc(taken, 1)
                pool.wait_ge(taken, count + 1)
                pool.sem_inc(split_done[b], 1)

            for i in range(ROUNDS):
                for n, (b, j) in enumerate(blocks):
                    pool.wait_ge(scale_done, N * i + n + 1)
                    pb, g = n % 2, groups[n]
                    ops = []
                    for tile in range(2):
                        if g > 1:
                            view = prob[:, pb, tile, 0:NTOK * (g - 1)].rearrange("p (g n) -> p g n", n=NTOK)
                            ops.append((view, scale[:, pb, tile, 0:g - 1].unsqueeze(2).broadcast_to([P, g - 1, NTOK])))
                        w = widths(j, tile)[-1]
                        view = prob[:, pb, tile, NTOK * (g - 1):NTOK * (g - 1) + w]
                        ops.append((view, scale[:, pb, tile, g - 1:g].broadcast_to([P, w])))
                    for view, by in ops:
                        op = pool.tensor_tensor(view, view, by, ALU.mult)
                    op.then_inc(scaled, 1)
                    if pieces(2 * i + b, n):
                        pool.wait_ge(scaled, N * i + n + 1)
                    h = 2 * i + b
                    for m in pieces(h, n):
                        if h and m == 0:
                            pool.wait_ge(pv_done, PAIRS * i + pair0[NB * b] + C_PV)
                        split(h + 1, m)

        @block.tensor
        def _(pe):
            def scores(i, n, which):
                b, j = blocks[n]
                if which == "first":
                    needed = 4 * (j // 2 + 1) if b == 0 else PIECES
                    pe.wait_ge(split_done[b], PIECES * i + needed)
                for tile, g, w, G, _ in score_groups(n, which):
                    qs = slice(QB * j + P * tile, QB * j + P * tile + P)
                    pe.wait_ge(exp_done, GROUPS * i + (G + 1 - S_RING + C_EXP))
                    ks, acc = slice(NTOK * g, NTOK * g + w), score_ps[:, G % S_RING, 0:w]
                    pe.matmul(acc, q_lo[:, b, qs], k_hi[:, b, ks], start=True, stop=False)
                    pe.matmul(acc, qr[:, b, qs], kr[:, ks], start=False, stop=False)
                    pe.matmul(acc, qr[ROPE:, b, qs], kr_hi[ROPE:, ks], start=False, stop=False)
                    pe.matmul(acc, q_hi[:, b, qs], k_lo[:, b, ks], start=False, stop=False)
                    pe.matmul(acc, q_hi[:, b, qs], k_hi[:, b, ks], start=False, stop=True).then_inc(score_done, 1)

            def turn(i, n, p):
                j, k = blocks[n][1], pair0[n] + p
                if p == 0:
                    pe.wait_ge(scaled, N * i + n + 1)
                pe.wait_ge(lo_done, PAIRS * i + (k + 1 - T_RING + C_LO))
                for kt in range(2):
                    for tile in range(2):
                        if p == j and kt > tile:
                            continue
                        at = QB * kt + P * (tile if p < j or kt == 0 else 0)
                        src = prob[:, n % 2, tile, P * (2 * p + kt):P * (2 * p + kt) + P]
                        last = pe.transpose(pT_ps[:, k % T_RING, at:at + P], src, ident[:])
                last.then_inc(turned, 1)

            def values(i, n, p):
                (b, j), k = blocks[n], pair0[n] + p
                if p == 0:
                    pe.wait_ge(out_done, N * i + (n + C_OUT))
                pe.wait_ge(lo_done, PAIRS * i + (k + 1 + C_LO))
                for kt in range(2):
                    diag = p == j and kt == 1
                    acc = acc_ps[:, P:QB] if diag else acc_ps[:, 0:QB]
                    ps = slice(QB * kt, QB * kt + (P if diag else QB))
                    vs = slice(P * (2 * p + kt), P * (2 * p + kt) + P)
                    r = k % T_RING
                    pe.matmul(acc, v_lo[:, b, vs], pT_hi[:, r, ps], start=(p == 0 and kt == 0), stop=False)
                    pe.matmul(acc, v_hi[:, b, vs], pT_lo[:, r, ps], start=False, stop=False)
                    last = pe.matmul(acc, v_hi[:, b, vs], pT_hi[:, r, ps], start=False, stop=diag)
                last.then_inc(pv_done, 1)

            pe.wait_ge(kr_done, 3)
            pe.wait_ge(const_sem, 3)
            pe.sem_inc(turned, C_TURN)
            pe.sem_inc(pv_done, C_PV)
            with pe.Fori(0, ROUNDS) as i:
                scores(i, 0, "first")
                scores(i, 0, "last")
                for n in range(N):
                    if n + 1 < N:
                        scores(i, n + 1, "first")
                    for p in range(min(2, pairs[n])):
                        turn(i, n, p)
                    if n + 1 < N:
                        scores(i, n + 1, "last")
                    for p in range(pairs[n]):
                        if p + 2 < pairs[n]:
                            turn(i, n, p + 2)
                        values(i, n, p)

        @block.scalar
        def _(act):
            def exps(i, n, which):
                pb = n % 2
                if which == "first":
                    act.wait_ge(turned, PAIRS * i + (pair0[n] - pairs[n - 1] + C_TURN))
                for tile, g, w, G, _ in score_groups(n, which):
                    act.wait_ge(max_done, GROUPS * i + (G + 1))
                    act.activation(prob[:, pb, tile, NTOK * g:NTOK * g + w], score_ps[:, G % S_RING, 0:w], ACT.Exp,
                                   bias=negm[:, pb, tile, g:g + 1], accum_out=sums[:, pb, tile, g:g + 1]).then_inc(exp_done, 1)

            def factors(i, n):
                if groups[n] > 1:
                    m, pb, gs = many.index(n), n % 2, slice(0, groups[n])
                    act.wait_ge(gap_done, MANY * i + (m + 1))
                    act.activation(fac[:, pb, :, gs], part[:, pb, :, gs], ACT.Exp).then_inc(fac_done, 1)

            def highs(i, n, p0, p1):
                for p in range(p0, p1):
                    k = pair0[n] + p
                    w = 2 * QB if p + 1 < pairs[n] else QB + P
                    act.wait_ge(turned, PAIRS * i + (k + 1 + C_TURN))
                    act.wait_ge(pv_done, PAIRS * i + (k + 1 - T_RING + C_PV))
                    act.activation(pT_hi[:, k % T_RING, 0:w], pT_ps[:, k % T_RING, 0:w], ACT.Copy).then_inc(hi_done, 1)

            def out_copy(i, n):
                act.wait_ge(pv_done, PAIRS * i + (pair0[n + 1] + C_PV))
                act.wait_ge(out_free, N * i + (n - 1 + C_FREE))
                act.activation(out[:, n % 2], acc_ps[:, 0:QB], ACT.Copy).then_inc(out_done, 1)

            act.preload_act_table(ACT.Exp)
            act.sem_inc(exp_done, C_EXP)
            act.sem_inc(out_done, C_OUT)
            act.wait_ge(kr_loaded, 32)
            act.activation(kr_hi[:], raw_kr, ACT.Copy).then_inc(kr_done, 1)
            act.activation(kr[0:ROPE], raw_kr[0:ROPE], ACT.Copy).then_inc(kr_done, 1)
            for m in range(PIECES):
                kind, ts = m % 4, slice(NTOK * (m // 4), NTOK * (m // 4 + 1))
                act.wait_ge(head0_loaded[m // 4], 80)
                if kind == 2:
                    if m > 4:
                        act.wait_ge(taken, m - 3)
                    act.activation(qr_hi[:], raw0[:, m], ACT.Copy)
                    act.activation(qr[ROPE:, 0, ts], raw0[ROPE:, m], ACT.Copy).then_inc(hi_split, 1)
                else:
                    high = (q_hi, k_hi, None, v_hi)[kind]
                    act.activation(high[:, 0, ts], raw0[:, m], ACT.Copy).then_inc(hi_split, 1)
            act.wait_ge(taken, PIECES)
            with act.Fori(0, ROUNDS) as i:
                exps(i, 0, "first")
                exps(i, 0, "last")
                factors(i, 0)
                for n in range(N):
                    early, soon = min(2, pairs[n]), min(4, pairs[n])
                    if n + 1 < N:
                        exps(i, n + 1, "first")
                    highs(i, n, 0, early)
                    if n + 1 < N:
                        exps(i, n + 1, "last")
                    highs(i, n, early, soon)
                    if n + 1 < N:
                        factors(i, n + 1)
                    highs(i, n, soon, pairs[n])
                    out_copy(i, n)

        @block.vector
        def _(dve):
            def maxima(i, n, which):
                pb = n % 2
                for tile, g, w, G, last in score_groups(n, which):
                    acc = score_ps[:, G % S_RING, 0:w]
                    dve.wait_ge(score_done, GROUPS * i + (G + 1))
                    if last:
                        dve.memset(acc[0:CHUNK, w - CHUNK:w], MASK).then_inc(diag_done, 1)
                        dve.wait_ge(diag_done, 2 * N * i + (2 * n + tile + 1))
                    dve.tensor_reduce(negm[:, pb, tile, g:g + 1], acc, AX.X, ALU.max, negate=True).then_inc(max_done, 1)

            def scales(i, n, step):
                G, pb, gs, g = group0[n + 1], n % 2, slice(0, groups[n]), groups[n]
                if g == 1:
                    if step == 0:
                        dve.wait_ge(exp_done, GROUPS * i + (G + C_EXP))
                        dve.reciprocal(scale[:, pb, :, gs], sums[:, pb, :, gs]).then_inc(scale_done, 1)
                    return
                m = many.index(n)
                if step == 0:
                    dve.wait_ge(max_done, GROUPS * i + G)
                    dve.tensor_reduce(top[:, pb], negm[:, pb, :, gs], AX.X, ALU.min).then_inc(top_done, 1)
                elif step == 1:
                    dve.wait_ge(top_done, MANY * i + (m + 1))
                    wide = top[:, pb].unsqueeze(2).broadcast_to([P, 2, g])
                    dve.tensor_tensor(part[:, pb, :, gs], wide, negm[:, pb, :, gs], ALU.subtract).then_inc(gap_done, 1)
                elif step == 2:
                    dve.wait_ge(fac_done, MANY * i + (m + 1))
                    dve.tensor_tensor(part[:, pb, :, gs], fac[:, pb, :, gs], sums[:, pb, :, gs], ALU.mult).then_inc(part_done, 1)
                    dve.wait_ge(part_done, MANY * i + (m + 1))
                    dve.tensor_reduce(total[:, pb], part[:, pb, :, gs], AX.X, ALU.add).then_inc(total_done, 1)
                else:
                    dve.wait_ge(total_done, MANY * i + (m + 1))
                    dve.reciprocal(total[:, pb], total[:, pb]).then_inc(inv_done, 1)
                    dve.wait_ge(inv_done, MANY * i + (m + 1))
                    wide = total[:, pb].unsqueeze(2).broadcast_to([P, 2, g])
                    dve.tensor_tensor(scale[:, pb, :, gs], fac[:, pb, :, gs], wide, ALU.mult).then_inc(scale_done, 1)

            def lows(i, n, p0, p1):
                for p in range(p0, p1):
                    k = pair0[n] + p
                    w = 2 * QB if p + 1 < pairs[n] else QB + P
                    r = k % T_RING
                    dve.wait_ge(hi_done, PAIRS * i + (k + 1))
                    dve.tensor_tensor(pT_lo[:, r, 0:w], pT_ps[:, r, 0:w], pT_hi[:, r, 0:w].bitcast(F32),
                                      ALU.subtract).then_inc(lo_done, 1)

            dve.sem_inc(lo_done, C_LO)
            dve.wait_ge(kr_done, 2)
            dve.tensor_tensor(kr[ROPE:], raw_kr[ROPE:], kr_hi[ROPE:].bitcast(F32), ALU.subtract).then_inc(kr_done, 1)
            for m in range(PIECES):
                kind, ts = m % 4, slice(NTOK * (m // 4), NTOK * (m // 4 + 1))
                dve.wait_ge(hi_split, m + 1)
                if kind == 2:
                    dve.tensor_tensor(qr[0:ROPE, 0, ts], raw0[0:ROPE, m], qr_hi[0:ROPE].bitcast(F32), ALU.subtract).then_inc(taken, 1)
                else:
                    high, low = ((q_hi, q_lo), (k_hi, k_lo), None, (v_hi, v_lo))[kind]
                    dve.tensor_tensor(low[:, 0, ts], raw0[:, m], high[:, 0, ts].bitcast(F32), ALU.subtract).then_inc(taken, 1)
                dve.wait_ge(taken, m + 1)
                dve.sem_inc(split_done[0], 1)
            with dve.Fori(0, ROUNDS) as i:
                maxima(i, 0, "first")
                maxima(i, 0, "last")
                for step in range(4):
                    scales(i, 0, step)
                for n in range(N):
                    early = min(2, pairs[n])
                    if n + 1 < N:
                        maxima(i, n + 1, "first")
                    lows(i, n, 0, early)
                    if n + 1 < N:
                        maxima(i, n + 1, "last")
                    for step in range(max(4, pairs[n] - early)):
                        if n + 1 < N and step < 4:
                            scales(i, n + 1, step)
                        if early + step < pairs[n]:
                            lows(i, n, early + step, early + step + 1)

        @block.sync
        def _(sp):
            def load(h, m):
                count = PIECES * h + m
                slot, kind, ts = count % RAW, m % 4, slice(NTOK * (m // 4), NTOK * (m // 4 + 1))
                if h == 0:
                    to, sem = raw0[:, m], head0_loaded[m // 4]
                else:
                    to, sem = raw[:, slot], raw_loaded[slot]
                    if h == 1 and m < RAW:
                        sp.wait_ge(kr_done, 3)
                    else:
                        sp.wait_ge(taken, count + 1 - RAW)
                if kind == 2:
                    for rows in (slice(0, ROPE), slice(ROPE, P)):
                        sp.dma_start(to[rows], made["qrT"][h, :, ts]).then_inc(sem, 16)
                elif kind == 3:
                    src = made["v"][4 * (m // 4):4 * (m // 4) + 4, :, P * h:P * h + P].rearrange("a p n -> p a n")
                    sp.dma_start(to.rearrange("p (a n) -> p a n", n=P), src).then_inc(sem, 16)
                else:
                    sp.dma_start(to, made["qnT" if kind == 0 else "knT"][h, :, ts]).then_inc(sem, 16)

            for rows in (slice(0, ROPE), slice(ROPE, P)):
                sp.dma_start(raw_kr[rows], made["krT"]).then_inc(kr_loaded, 16)
            for m in range(PIECES):
                load(0, m)
            sp.sem_inc(out_free, C_FREE)
            for m in range(RAW):
                load(1, m)
            for i in range(ROUNDS):
                for n, (b, j) in enumerate(blocks):
                    h = 2 * i + b
                    for m in pieces(h, n):
                        if m + RAW < PIECES:
                            load(h + 1, m + RAW)
                        elif h + 2 < HEADS:
                            load(h + 2, m + RAW - PIECES)
                    sp.wait_ge(out_done, N * i + n + 1 + C_OUT)
                    sp.dma_start(mixT[HEADS + h, :, QB * j:QB * (j + 1)], out[:, n % 2]).then_inc(stored, 16)
                    sp.wait_ge(stored, 16 * (N * i + n + 1))
                    sp.sem_inc(out_free, 1)


def feed_in(nc, xT, w_gate_up, hid):
    with ExitStack() as ctx:
        s = Scope(nc, ctx, "ff")
        x_raw = s.sb("x_raw", [P, 2, SEQ])
        x_hi = s.sb("x_hi", [P, KD, SEQ], F32R)
        x_lo = s.sb("x_lo", [P, KD, SEQ], F32R)
        w_raw = s.sb("w_raw", [P, 2, KD * P])
        w_hi = s.sb("w_hi", [P, 2, KD * P], F32R)
        w_lo = s.sb("w_lo", [P, 2, KD * P], F32R)
        zero = s.sb("zero", [P, 1])
        out = s.sb("out", [P, 2, SEQ])
        h_ps = s.ps("h_ps", [P, 2, BLOCKS, NTOK])

        x_loaded = [s.sem(f"x_loaded{b}") for b in range(2)]
        x_hi_done, x_lo_done = s.sem("x_hi_done"), s.sem("x_lo_done")
        w_loaded = [s.sem(f"w_loaded{b}") for b in range(2)]
        w_hi_done, w_lo_done = s.sem("w_hi_done"), s.sem("w_lo_done")
        made = s.sem("made")
        gate_free, up_free = s.sem("gate_free"), s.sem("up_free")
        zeroed = s.sem("zeroed")
        silu_done = s.sem("silu_done")
        out_made = s.sem("out_made")
        out_free = s.sem("out_free")
        stored = [s.sem(f"stored{b}") for b in range(2)]
        block = ctx.enter_context(nc.Block())

        @block.sync
        def _(sp):
            for k in range(KD):
                if k >= 2:
                    sp.wait_ge(x_lo_done, k - 1)
                sp.dma_start(x_raw[:, k % 2, :], xT[k]).then_inc(x_loaded[k % 2], 16)
            sp.sem_inc(out_free, 2)
            with sp.Fori(0, FT // 2) as i:
                for b in range(2):
                    dst = hid[:, :, bass.ds(2 * i + b, 1), :].rearrange("t p a c -> p t (a c)")
                    sp.wait_ge(out_made, 2 * i + b + 1)
                    sp.dma_start(dst, out[:, b].rearrange("p (t c) -> p t c", c=P)).then_inc(stored[b], 16)
                    sp.wait_ge(stored[b], 16 * i + 16)
                    sp.sem_inc(out_free, 1)

        @block.gpsimd
        def _(pool):
            def load(m, b):
                pool.dma_start(w_raw[:, b, :], w_gate_up[bass.ds(m, 1)].rearrange("a p f -> p (a f)")).then_inc(w_loaded[b], 16)

            def split(i, b):
                m = 2 * i + b
                pool.wait_ge(w_loaded[b], 16 * i + 16)
                if b:
                    pool.wait_ge(up_free, i + 1)
                else:
                    pool.wait_ge(gate_free, i + 1)
                pool.tensor_tensor(w_hi[:, b, :], w_raw[:, b, :], zero[:, 0:1].broadcast_to([P, KD * P]),
                                   ALU.add).then_inc(w_hi_done, 1)
                pool.wait_ge(w_hi_done, m + 1)
                pool.tensor_tensor(w_lo[:, b, :], w_raw[:, b, :], w_hi[:, b, :].bitcast(F32),
                                   ALU.subtract).then_inc(w_lo_done, 1)

            pool.memset(zero[:, :], 0.0).then_inc(zeroed, 1)
            pool.wait_ge(zeroed, 1)
            load(0, 0)
            load(1, 1)
            with pool.Fori(0, FT - 1) as i:
                for b in range(2):
                    split(i, b)
                    pool.wait_ge(w_lo_done, 2 * i + b + 1)
                    load(2 * i + b + 2, b)
            for b in range(2):
                split(FT - 1, b)

        @block.tensor
        def _(pe):
            def products(b, k):
                ws = slice(k * P, (k + 1) * P)
                for t in range(BLOCKS):
                    ts = slice(t * NTOK, (t + 1) * NTOK)
                    acc = h_ps[:, b, t, :]
                    pe.matmul(acc, w_lo[:, b, ws], x_hi[:, k, ts], start=(k == 0), stop=False)
                    pe.matmul(acc, w_hi[:, b, ws], x_lo[:, k, ts], start=False, stop=False)
                    last = pe.matmul(acc, w_hi[:, b, ws], x_hi[:, k, ts], start=False, stop=(k == KD - 1))
                return last

            for k in range(KD):
                pe.wait_ge(x_lo_done, k + 1)
                for b in range(2):
                    if k == 0:
                        pe.wait_ge(w_lo_done, b + 1)
                    last = products(b, k)
                    if k == KD - 1:
                        last.then_inc(made, 1)
            with pe.Fori(1, FT) as i:
                for b in range(2):
                    pe.wait_ge(w_lo_done, 2 * i + b + 1)
                    pe.wait_ge(up_free if b else gate_free, i + 1)
                    for k in range(KD):
                        last = products(b, k)
                    last.then_inc(made, 1)

        @block.scalar
        def _(act):
            act.sem_inc(gate_free, 1)
            for k in range(KD):
                act.wait_ge(x_loaded[k % 2], 16 * (k // 2 + 1))
                act.activation(x_hi[:, k, :], x_raw[:, k % 2, :], ACT.Copy).then_inc(x_hi_done, 1)
            act.preload_act_table(ACT.Silu)
            with act.Fori(0, FT // 2) as i:
                for b in range(2):
                    act.wait_ge(made, 4 * i + 2 * b + 1)
                    act.wait_ge(out_free, 2 * i + b + 1)
                    act.activation(out[:, b], h_ps[:, 0].rearrange("p a t -> p (a t)"), ACT.Silu).then_inc(silu_done, 1)
                    act.wait_ge(silu_done, 2 * i + b + 1)
                    act.sem_inc(gate_free, 1)

        @block.vector
        def _(dve):
            dve.sem_inc(up_free, 1)
            for k in range(KD):
                dve.wait_ge(x_hi_done, k + 1)
                dve.tensor_tensor(x_lo[:, k, :], x_raw[:, k % 2, :], x_hi[:, k, :].bitcast(F32),
                                  ALU.subtract).then_inc(x_lo_done, 1)
            with dve.Fori(0, FT // 2) as i:
                for b in range(2):
                    dve.wait_ge(made, 4 * i + 2 * b + 2)
                    dve.wait_ge(silu_done, 2 * i + b + 1)
                    dve.tensor_tensor(out[:, b], out[:, b], h_ps[:, 1].rearrange("p a t -> p (a t)"), ALU.mult).then_inc(out_made, 1)
                    dve.wait_ge(out_made, 2 * i + b + 1)
                    dve.sem_inc(up_free, 1)


def hold(eng, begun):
    eng.sem_inc(begun, 1)


def over_tiles(loop, first, tile, last):
    first(0, 0)
    tile(0, 1)
    tile(0, 2)
    with loop(1, TILES // 2 - 1) as i:
        tile(i, 1)
        tile(i, 2)
    tile(TILES // 2 - 1, 1)
    last(TILES // 2 - 1, 2)


class TokenProduct:

    def __init__(self, nc, s, K, lhs, weights, w_raw, accs):
        self.nc, self.K, self.lhs, self.weights, self.w_raw = nc, K, lhs, weights, w_raw
        self.CH = K // 2
        self.accs = accs
        self.w_hi = s.sb("w_hi", [P, K, D_MODEL], F32R)
        self.w_lo = s.sb("w_lo", [P, K, D_MODEL], F32R)
        self.a_raw = s.sb("a_raw", [P, 2, 2 * P])
        self.a_hi = s.sb("a_hi", [P, 2, 2 * P], F32R)
        self.a_lo = s.sb("a_lo", [P, 2, 2 * P], F32R)
        self.w_loaded = [s.sem(f"w_loaded{b}") for b in range(len(w_raw))]
        self.w_hi_done, self.w_lo_done = s.sem("w_hi_done"), s.sem("w_lo_done")
        self.a_loaded = [s.sem(f"a_loaded{b}") for b in range(2)]
        self.a_hi_done, self.a_lo_done = s.sem("a_hi_done"), s.sem("a_lo_done")
        self.a_used = s.sem("a_used")

    def chunk(self, i, b, c):
        n = self.CH * b + c
        return 2 * self.CH * i + n, n % 2, self.CH * i + n // 2 + 1

    def product_done(self, eng, i, b):
        eng.wait_ge(self.a_used, 2 * self.CH * i + self.CH * (b + 1))

    def load_weights(self, eng):
        for k in range(self.K):
            ring = len(self.w_raw)
            reached(eng, self.w_lo_done, k + 1 - ring)
            eng.dma_start(self.w_raw[k % ring], self.weights[k]).then_inc(self.w_loaded[k % ring], 16)

    def load(self, eng, i, b):
        for c in range(self.CH):
            n, slot, _ = self.chunk(i, b, c)
            src = self.lhs(2 * i + b, 2 * c)
            reached(eng, self.a_lo_done, n - 1)
            eng.dma_start(self.a_raw[:, slot].rearrange("p (k t) -> p k t", k=2), src).then_inc(self.a_loaded[slot], 16)

    def high(self, act, i, b, c, with_weights=False):
        n, slot, loads = self.chunk(i, b, c)
        if with_weights:
            for k in (2 * c, 2 * c + 1):
                ring = len(self.w_raw)
                act.wait_ge(self.w_loaded[k % ring], 16 * (k // ring + 1))
                act.activation(self.w_hi[:, k], self.w_raw[k % ring], ACT.Copy).then_inc(self.w_hi_done, 1)
        act.wait_ge(self.a_loaded[slot], 16 * loads)
        reached(act, self.a_used, n - 1)
        act.activation(self.a_hi[:, slot], self.a_raw[:, slot], ACT.Copy).then_inc(self.a_hi_done, 1)

    def low(self, dve, i, b, c, with_weights=False):
        n, slot, _ = self.chunk(i, b, c)
        if with_weights:
            for k in (2 * c, 2 * c + 1):
                dve.wait_ge(self.w_hi_done, k + 1)
                dve.tensor_tensor(self.w_lo[:, k], self.w_raw[k % len(self.w_raw)], self.w_hi[:, k].bitcast(F32),
                                  ALU.subtract).then_inc(self.w_lo_done, 1)
        dve.wait_ge(self.a_hi_done, n + 1)
        dve.tensor_tensor(self.a_lo[:, slot], self.a_raw[:, slot], self.a_hi[:, slot].bitcast(F32),
                          ALU.subtract).then_inc(self.a_lo_done, 1)

    def product(self, pe, i, b, acc_free):
        reached(pe, acc_free, 2 * i + b - 1)
        for c in range(self.CH):
            n, slot, _ = self.chunk(i, b, c)
            if isinstance(i, int) and i == 0 and b == 0:
                pe.wait_ge(self.w_lo_done, 2 * c + 2)
            pe.wait_ge(self.a_lo_done, n + 1)
            for k in (2 * c, 2 * c + 1):
                k0, k1, acc = next(a for a in self.accs if a[0] <= k <= a[1])
                rows = slice(P * (k % 2), P * (k % 2) + P)
                for half in range(2):
                    cols = slice(NTOK * half, NTOK * (half + 1))
                    to = acc[:, b % 2, cols]
                    pe.matmul(to, self.a_lo[:, slot, rows], self.w_hi[:, k, cols], start=(k == k0), stop=False)
                    pe.matmul(to, self.a_hi[:, slot, rows], self.w_lo[:, k, cols], start=False, stop=False)
                    last = pe.matmul(to, self.a_hi[:, slot, rows], self.w_hi[:, k, cols], start=False, stop=(k == k1))
            last.then_inc(self.a_used, 1)


def project_norm(nc, stage, K, lhs, weights, res, gain, bias, x_out, xT_out):
    with ExitStack() as ctx:
        s = Scope(nc, ctx, stage)
        y = s.sb("y", [P, 2, D_MODEL])
        old = s.sb("old", [P, D_MODEL])
        g_all = s.sb("g_all", [P, D_MODEL])
        b_all = s.sb("b_all", [P, D_MODEL])
        ident = s.sb("ident", [P, P])
        stats = s.sb("stats", [P, 2, 6])
        mean = s.sb("mean", [P, 2])
        eps = s.sb("eps", [P, 1])
        root = s.sb("root", [P, 4])
        rstd = root[:, 3:4]
        xT = s.sb("xT", [P, KD, P])
        acc = s.ps("acc", [P, 2, D_MODEL])
        xT_ps = s.ps("xT_ps", [P, KD, P])
        w_raw = [y[:, 0], y[:, 1], old[:], xT[:].rearrange("p k t -> p (k t)")]
        tp = TokenProduct(nc, s, K, lhs, weights, w_raw, [(0, K - 1, acc)])

        const_sem = s.sem("consts")
        small_loaded = s.sem("small_loaded")
        res_loaded = s.sem("res_loaded")
        added = s.sem("added")
        stats_done, mean_done, root_done, newton = (s.sem(n) for n in ("stats_done", "mean_done", "root_done", "newton"))
        centered, y_done = s.sem("centered"), s.sem("y_done")
        x_stored, xT_stored = [s.sem(f"x_stored{b}") for b in range(2)], s.sem("xT_stored")
        turned, xT_copied = s.sem("turned"), s.sem("xT_copied")
        dve_holds, pool_holds, sp_holds = s.sem("dve_holds"), s.sem("pool_holds"), s.sem("sp_holds")
        block = ctx.enter_context(nc.Block())
        LAST = TILES // 2 - 1

        @block.sync
        def _(sp):
            sp.dma_start(g_all[:], gain.partition_broadcast(P)).then_inc(small_loaded, 16)
            sp.dma_start(b_all[:], bias.partition_broadcast(P)).then_inc(small_loaded, 16)
            def tile(i, b):
                t = 2 * i + b
                tp.load(sp, i, b)
                if isinstance(i, int) and t == 0:
                    sp.wait_ge(tp.w_lo_done, K)
                reached(sp, added, t)
                hold(sp, sp_holds)
                sp.dma_start(old[:], res[bass.ds(P * t, P)]).then_inc(res_loaded, 16)

            tile(0, 0)
            tile(0, 1)
            with sp.Fori(1, TILES // 2) as i:
                tile(i, 0)
                tile(i, 1)

        @block.gpsimd
        def _(pool):
            def finish(i, b):
                t, at = 2 * i + b, b % 2
                dst = x_out[bass.ds(P * t, P)]
                pool.wait_ge(y_done, t + 1)
                hold(pool, pool_holds)
                pool.dma_start(dst, y[:, at]).then_inc(x_stored[at], 16)

            pool.memset(ident[:], 0.0).then_inc(const_sem, 1)
            pool.wait_ge(const_sem, 1)
            pool.affine_select(out=ident[:], in_=ident[:], compare_op=ALU.not_equal, fill=1.0, base=0, pattern=[[-1, P]],
                               channel_multiplier=1).then_inc(const_sem, 1)
            pool.memset(eps[:], LN_EPS).then_inc(const_sem, 1)
            tp.load_weights(pool)
            finish(0, 0)
            with pool.Fori(0, LAST) as i:
                finish(i, 1)
                finish(i, 2)
            finish(LAST, 1)
            for b in range(2):
                pool.wait_ge(x_stored[b], 16 * (TILES // 2))

        @block.tensor
        def _(pe):
            def turn(i, b):
                t = 2 * i + b
                pe.wait_ge(y_done, t + 1)
                reached(pe, xT_copied, t)
                for k in range(KD):
                    last = pe.transpose(xT_ps[:, k], y[:, b % 2, P * k:P * (k + 1)], ident[:])
                last.then_inc(turned, 1)

            def tile(i, b):
                tp.product(pe, i, b, added)
                turn(i, b - 1)

            over_tiles(pe.Fori, lambda i, b: tp.product(pe, i, b, added), tile, lambda i, b: turn(i, b - 1))

        @block.scalar
        def _(act):
            def out(i, b):
                t = 2 * i + b
                act.wait_ge(turned, t + 1)
                reached(act, xT_stored, 16 * t)
                act.activation(xT[:], xT_ps[:], ACT.Copy).then_inc(xT_copied, 1)
                dst = xT_out[:, :, bass.ds(P * t, P)].rearrange("a p t -> p a t")
                act.wait_ge(xT_copied, t + 1)
                act.dma_start(dst, xT[:]).then_inc(xT_stored, 16)

            def deviation(i, b):
                act.wait_ge(mean_done, 2 * i + b + 1)
                act.activation(root[:, 0:1], mean[:, 1:2], ACT.Sqrt, bias=eps[:, 0:1]).then_inc(root_done, 1)

            def tile(i, b):
                for c in range(tp.CH):
                    tp.high(act, i, b, c)
                    if c == 1:
                        if b == 2:
                            out(i, 0)
                        elif not (isinstance(i, int) and i == 0):
                            out(i - 1, 1)
                        deviation(i, b - 1)

            act.preload_act_table(ACT.Sqrt)
            act.wait_ge(const_sem, 3)

            over_tiles(act.Fori, lambda i, b: [tp.high(act, i, b, c, True) for c in range(tp.CH)], tile,
                       lambda i, b: [out(i, b - 2), deviation(i, b - 1), out(i, b - 1)])
            act.wait_ge(xT_stored, 16 * TILES)

        @block.vector
        def _(dve):
            def add(i, b):
                at = b % 2
                tp.product_done(dve, i, b)
                dve.wait_ge(res_loaded, 32 * i + 16 * b + 16)
                reached(dve, x_stored[at], 16 * i + 16 * (b // 2))
                reached(dve, turned, 2 * i + b - 1)
                dve.scalar_tensor_tensor(y[:, at], old[:], ALPHA, acc[:, at], ALU.mult, ALU.add).then_inc(added, 1)

            def moments(i, b):
                t, at = 2 * i + b, b % 2
                dve.wait_ge(added, t + 1)
                for half in range(2):
                    dve.bn_stats(stats[:, half], y[:, at, NTOK * half:NTOK * (half + 1)]).then_inc(stats_done, 1)
                dve.wait_ge(stats_done, 2 * t + 2)
                hold(dve, dve_holds)
                dve.bn_aggr(mean[:], stats[:].rearrange("p a c -> p (a c)")).then_inc(mean_done, 1)

            def norm(i, b):
                t, at = 2 * i + b, b % 2
                dve.wait_ge(mean_done, t + 1)
                dve.scalar_tensor_tensor(y[:, at], y[:, at], mean[:, 0:1], g_all[:], ALU.subtract, ALU.mult).then_inc(centered, 1)
                dve.wait_ge(root_done, t + 1)
                dve.tensor_scalar(mean[:, 1:2], mean[:, 1:2], LN_EPS, -0.5, ALU.add, ALU.mult).then_inc(newton, 1)
                dve.reciprocal(root[:, 1:2], root[:, 0:1]).then_inc(newton, 1)
                dve.wait_ge(newton, 4 * t + 2)
                dve.scalar_tensor_tensor(root[:, 2:3], root[:, 1:2], mean[:, 1:2], root[:, 1:2], ALU.mult, ALU.mult).then_inc(newton, 1)
                dve.wait_ge(newton, 4 * t + 3)
                dve.scalar_tensor_tensor(rstd, root[:, 2:3], 1.5, root[:, 1:2], ALU.add, ALU.mult).then_inc(newton, 1)
                dve.wait_ge(newton, 4 * t + 4)
                dve.wait_ge(centered, t + 1)
                dve.scalar_tensor_tensor(y[:, at], y[:, at], rstd, b_all[:], ALU.mult, ALU.add).then_inc(y_done, 1)

            def tile(i, b):
                for c in range(tp.CH):
                    tp.low(dve, i, b, c)
                    if c == 0:
                        add(i, b - 1)
                    if c == 1:
                        moments(i, b - 1)
                    if c == 2:
                        norm(i, b - 1)

            dve.wait_ge(small_loaded, 32)
            over_tiles(dve.Fori, lambda i, b: [tp.low(dve, i, b, c, True) for c in range(tp.CH)], tile,
                       lambda i, b: [add(i, b - 1), moments(i, b - 1), norm(i, b - 1)])


def embed(nc, lhs, weights, x, out):
    K = KD + PLE_DIM // P
    with ExitStack() as ctx:
        s = Scope(nc, ctx, "em")
        w_raw = s.sb("w_raw", [P, 4, D_MODEL])
        xt = s.sb("xt", [P, 2, D_MODEL])
        y = s.sb("y", [P, 2, D_MODEL])
        gate_ps = s.ps("gate_ps", [P, 2, D_MODEL])
        ple_ps = s.ps("ple_ps", [P, 2, D_MODEL])
        tp = TokenProduct(nc, s, K, lhs, weights, [w_raw[:, n] for n in range(4)], [(0, KD - 1, gate_ps), (KD, K - 1, ple_ps)])
        x_loaded = [s.sem(f"x_loaded{b}") for b in range(2)]
        gate_done = s.sem("gate_done")
        gated = s.sem("gated")
        summed = s.sem("summed")
        pool_holds = s.sem("pool_holds")
        stored = [s.sem(f"stored{b}") for b in range(2)]
        block = ctx.enter_context(nc.Block())

        @block.sync
        def _(sp):
            tp.load(sp, 0, 0)
            tp.load(sp, 0, 1)
            with sp.Fori(1, TILES // 2) as i:
                tp.load(sp, i, 0)
                tp.load(sp, i, 1)

        @block.gpsimd
        def _(pool):
            def load_x(t, b):
                pool.dma_start(xt[:, b], x[bass.ds(P * t, P)]).then_inc(x_loaded[b], 16)

            def finish(i, b, more):
                t = 2 * i + b
                pool.wait_ge(x_loaded[b], 16 * i + 16)
                pool.wait_ge(gated, t + 1)
                pool.tensor_tensor(y[:, b], y[:, b], xt[:, b], ALU.add).then_inc(summed, 1)
                dst = out[bass.ds(P * t, P)]
                pool.wait_ge(summed, t + 1)
                hold(pool, pool_holds)
                pool.dma_start(dst, y[:, b]).then_inc(stored[b], 16)
                if more:
                    load_x(t + 2, b)

            tp.load_weights(pool)
            load_x(0, 0)
            load_x(1, 1)
            with pool.Fori(0, TILES // 2 - 1) as i:
                finish(i, 0, True)
                finish(i, 1, True)
            for b in range(2):
                finish(TILES // 2 - 1, b, False)
            for b in range(2):
                pool.wait_ge(stored[b], 16 * (TILES // 2))

        @block.tensor
        def _(pe):
            product = lambda i, b: tp.product(pe, i, b, gated)
            over_tiles(pe.Fori, product, product, lambda i, b: None)

        @block.scalar
        def _(act):
            def gate(i, b):
                at = b % 2
                tp.product_done(act, i, b)
                reached(act, stored[at], 16 * i + 16 * (b // 2))
                act.activation(y[:, at], gate_ps[:, at], ACT.Sigmoid).then_inc(gate_done, 1)

            def tile(i, b):
                for c in range(tp.CH):
                    tp.high(act, i, b, c)
                    if c == 1:
                        gate(i, b - 1)

            act.preload_act_table(ACT.Sigmoid)
            over_tiles(act.Fori, lambda i, b: [tp.high(act, i, b, c, True) for c in range(tp.CH)], tile,
                       lambda i, b: gate(i, b - 1))

        @block.vector
        def _(dve):
            def multiply(i, b):
                at = b % 2
                dve.wait_ge(gate_done, 2 * i + b + 1)
                dve.tensor_tensor(y[:, at], y[:, at], ple_ps[:, at], ALU.mult).then_inc(gated, 1)

            def tile(i, b):
                for c in range(tp.CH):
                    tp.low(dve, i, b, c)
                    if c == 1:
                        multiply(i, b - 1)

            over_tiles(dve.Fori, lambda i, b: [tp.low(dve, i, b, c, True) for c in range(tp.CH)], tile,
                       lambda i, b: multiply(i, b - 1))


def lay_in(x, w_in, conv_w):
    xT = np.ascontiguousarray(x[0].T.reshape(KD, P, SEQ).transpose(1, 0, 2))
    w = w_in[0]
    cuts = np.cumsum([4 * HEADS * P, HEADS, HEADS, Q_LORA, KV_LORA, ROPE])
    qkvz, b, a, cq, ckv, kr = np.split(w, cuts[:-1], axis=1)
    pad = np.zeros((D_MODEL, N_IN * P - w.shape[1]), w.dtype)
    w = np.concatenate([qkvz, cq, ckv, kr, b, a, pad], axis=1)
    w = w.reshape(KD, P, N_IN, P).transpose(2, 1, 0, 3).reshape(N_IN, P, KD * P)
    taps = conv_w[0].T.reshape(T_Z, P, CONV_WIDTH).transpose(1, 0, 2).reshape(P, T_Z * CONV_WIDTH)
    return xT, np.ascontiguousarray(w), np.ascontiguousarray(taps)


def lay_latents(w_uq, w_ukv, q_norm_g, kv_norm_g):
    uq = w_uq[0].reshape(KQ, P, HEADS, P + ROPE)
    uq = np.concatenate([uq[..., P:].reshape(KQ, P, -1), uq[..., :P].reshape(KQ, P, -1)], axis=2)
    ukv = w_ukv[0].reshape(KC, P, HEADS, 2, P).transpose(0, 1, 3, 2, 4).reshape(KC, P, -1)
    gains = np.concatenate([q_norm_g[0].reshape(KQ, P), kv_norm_g[0].reshape(KC, P)]).T
    return (np.ascontiguousarray(uq.transpose(1, 0, 2)), np.ascontiguousarray(ukv.transpose(1, 0, 2)),
            np.ascontiguousarray(gains))


def rotary_frequencies():
    f = ROPE_THETA ** (-np.arange(0, ROPE, 2) / ROPE)
    return np.tile(f.astype(np.float32), P // (ROPE // 2)).reshape(P, 1)


def lay_tail(w_gate_up, w_ple_gate, w_ple, p):
    gu = w_gate_up[0].reshape(KD, P, 2, FT, P).transpose(3, 2, 1, 0, 4).reshape(2 * FT, P, KD * P)
    ple = np.concatenate([w_ple_gate[0], w_ple[0]]).reshape(-1, P, D_MODEL)
    pT = p[0, 0].T.reshape(PLE_DIM // P, P, SEQ)
    return np.ascontiguousarray(gu), np.ascontiguousarray(ple), np.ascontiguousarray(pT)


def tokens_of(xT):
    return lambda t, k: xT[k:k + 2, :, bass.ds(P * t, P)].rearrange("a p t -> p a t")


def build(nc, a, out):
    def scratch(name, shape, dt=F32):
        return nc.dram_tensor(f"scratch_{name}", shape, dt, kind="Internal").ap()

    hT = scratch("hT", [N_IN, P, SEQ])
    shapes = {"qnT": [HEADS, P, SEQ], "qrT": [HEADS, ROPE, SEQ], "knT": [HEADS, P, SEQ], "krT": [ROPE, SEQ],
              "v": [TILES, P, HEADS * P]}
    made = {n: scratch(n, shape) for n, shape in shapes.items()}
    mixT = scratch("mixT", [2 * HEADS, P, SEQ])
    x1, x1T = scratch("x1", [SEQ, D_MODEL]), scratch("x1T", [KD, P, SEQ])
    hid = scratch("hid", [TILES, P, FT, P])
    x2, x2T = scratch("x2", [SEQ, D_MODEL]), scratch("x2T", [KD, P, SEQ])

    project_in(nc, a["xT"], a["w_in"], a["taps"], hT)
    latents(nc, hT, a["positions"][0], a["inv_freq"], a["w_uq"], a["w_ukv"], a["gains"], made)
    delta_rule(nc, hT, a["a_log"][0], a["dt_bias"][0], a["gdn_norm_g"], mixT)
    attention(nc, made, mixT)
    project_norm(nc, "op", KD, tokens_of(mixT), a["w_out"], a["x"], a["ln1_g"][0], a["ln1_b"][0], x1, x1T)
    feed_in(nc, x1T, a["w_gate_up"], hid)
    hidden = lambda t, k: hid[bass.ds(t, 1), :, k:k + 2, :].rearrange("x p a c -> p (x a) c")
    project_norm(nc, "fd", FT, hidden, a["w_down"], x1, a["ln2_g"][0], a["ln2_b"][0], x2, x2T)
    from_x, from_p = tokens_of(x2T), tokens_of(a["pT"])
    embed(nc, lambda t, k: from_x(t, k) if k < KD else from_p(t, k - KD), a["w_ple"], x2, out)


def lay_all(i):
    xT, w_in, taps = lay_in(i["x"], i["w_in"], i["conv_w"])
    uq, ukv, gains = lay_latents(i["w_uq"], i["w_ukv"], i["q_norm_g"], i["kv_norm_g"])
    gate_up, ple, pT = lay_tail(i["w_gate_up"], i["w_ple_gate"], i["w_ple"], i["p"])
    return {
        "x": i["x"][0], "xT": xT, "w_in": w_in, "taps": taps,
        "positions": i["positions"], "inv_freq": rotary_frequencies(), "w_uq": uq, "w_ukv": ukv, "gains": gains,
        "a_log": i["a_log"], "dt_bias": i["dt_bias"], "gdn_norm_g": i["gdn_norm_g"].reshape(P, 1),
        "w_out": i["w_out"][0].reshape(KD, P, D_MODEL), "ln1_g": i["ln1_g"], "ln1_b": i["ln1_b"],
        "w_gate_up": gate_up, "w_down": i["w_down"][0].reshape(FT, P, D_MODEL), "ln2_g": i["ln2_g"], "ln2_b": i["ln2_b"],
        "w_ple": ple, "pT": pT,
    }


def kernel(**inputs):
    import concourse.bacc as bacc
    from concourse.bass_utils import run_bass_kernel_spmd

    nc = bacc.Bacc("TRN2", target_bir_lowering=False, num_devices=1)
    arrays = {n: np.ascontiguousarray(v) for n, v in lay_all({n: np.asarray(v) for n, v in inputs.items()}).items()}
    a = {n: nc.dram_tensor(n, v.shape, mybir.dt.from_np(v.dtype), kind="ExternalInput").ap() for n, v in arrays.items()}
    out = nc.dram_tensor("out", [SEQ, D_MODEL], F32, kind="ExternalOutput").ap()
    build(nc, a, out)
    r = run_bass_kernel_spmd(nc, [arrays], core_ids=[0])
    return r.results[0]["out"].reshape(1, SEQ, D_MODEL)
```
